# Optimizing a Trainium2 kernel written in Bass

```python
import jax
import jax.numpy as jnp
from jax import lax
import numpy as np

D_MODEL = 1024
BATCH = 1
SEQ = 256
DEPTH = 2
DEC_BATCH = 8
DEC_SEQ = 4
PAST_LEN = 1024
PAGE_SIZE = 128

N_A_LAYERS = DEPTH // 2
N_B_LAYERS = DEPTH - N_A_LAYERS
D_RNN = D_MODEL
LRU_HEADS = 8
LRU_BW = D_RNN // LRU_HEADS
CONV_W = 4
LRU_C = 8.0
N_HEADS = 16
QK_NOPE = 64
QK_ROPE = 32
V_HEAD = 64
KV_LORA = 256
Q_LORA = 512
ROPE_THETA = 10000.0
SOFTMAX_SCALE = (QK_NOPE + QK_ROPE) ** -0.5
Q_BLOCK = 128
PEER_HEADS = 8
PEER_KEYS = 128
PEER_EXPERTS = PEER_KEYS * PEER_KEYS
PEER_DK = 256
PEER_TOPK = 16
PEER_BLOCK = 256

RMS_EPS = 1e-6
NEG_INF = -1e30

kernel_name = 'yoco_rglru_mla_peer_step'

def rmsnorm(x, g):
    xf = x.astype(jnp.float32)
    y = xf * lax.rsqrt(jnp.mean(xf * xf, axis=-1, keepdims=True) + RMS_EPS)
    return (y * g.astype(jnp.float32)).astype(x.dtype)

def rope(x, pos):
    half = x.shape[-1] // 2
    inv = ROPE_THETA ** (-jnp.arange(half, dtype=jnp.float32) / half)
    ang = pos.astype(jnp.float32)[:, None] * inv[None, :]
    shape = (1, pos.shape[0]) + (1,) * (x.ndim - 3) + (half,)
    cos = jnp.cos(ang).reshape(shape)
    sin = jnp.sin(ang).reshape(shape)
    xf = x.astype(jnp.float32)
    x1, x2 = xf[..., :half], xf[..., half:]
    return jnp.concatenate([x1 * cos - x2 * sin, x2 * cos + x1 * sin], axis=-1).astype(x.dtype)

def lru_scan(a, b, h0):
    b = b.at[:, 0].add(a[:, 0] * h0)

    def combine(left, right):
        a_l, b_l = left
        a_r, b_r = right
        return a_l * a_r, a_r * b_l + b_r

    _, h = lax.associative_scan(combine, (a, b), axis=1)
    return h

def rglru_mixer(x_n, conv_buf, h0, w_in, conv_w, conv_b, gate_a_w, gate_a_b, gate_x_w, gate_x_b, lam, w_out):
    b, t, _ = x_n.shape
    proj = x_n @ w_in
    gate = jax.nn.gelu(proj[..., :D_RNN])
    xb = proj[..., D_RNN:]
    xcat = jnp.concatenate([conv_buf.astype(xb.dtype), xb], axis=1)
    xc = conv_b + sum(xcat[:, k:k + t] * conv_w[k] for k in range(CONV_W))
    new_buf = xcat[:, -(CONV_W - 1):]
    xh = xc.reshape(b, t, LRU_HEADS, LRU_BW)
    r = jax.nn.sigmoid(jnp.einsum('bthi,hij->bthj', xh, gate_a_w, preferred_element_type=jnp.float32).reshape(b, t, D_RNN) + gate_a_b.astype(jnp.float32))
    i = jax.nn.sigmoid(jnp.einsum('bthi,hij->bthj', xh, gate_x_w, preferred_element_type=jnp.float32).reshape(b, t, D_RNN) + gate_x_b.astype(jnp.float32))
    log_a = -LRU_C * r * jax.nn.softplus(-lam.astype(jnp.float32))
    a = jnp.exp(log_a)
    bx = jnp.sqrt(-jnp.expm1(2.0 * log_a)) * i * xc.astype(jnp.float32)
    h = lru_scan(a, bx, h0.astype(jnp.float32))
    y = (h.astype(x_n.dtype) * gate) @ w_out
    return y, new_buf, h[:, -1].astype(x_n.dtype)

def peer_ffn(x_n, w_q, subkeys, u_tab, v_tab):
    shp = x_n.shape
    xf = x_n.reshape(-1, shp[-1])
    n = xf.shape[0]
    nb = -(-n // PEER_BLOCK)
    xb = jnp.pad(xf, ((0, nb * PEER_BLOCK - n), (0, 0))).reshape(nb, PEER_BLOCK, shp[-1])

    def per_block(xt):
        m = xt.shape[0]
        q = (xt @ w_q).reshape(m, PEER_HEADS, 2, PEER_DK // 2)
        s = jnp.einsum('nhpd,hpkd->nhpk', q, subkeys, preferred_element_type=jnp.float32)
        sv, si = lax.top_k(s, PEER_TOPK)
        cand = (sv[:, :, 0, :, None] + sv[:, :, 1, None, :]).reshape(m, PEER_HEADS, PEER_TOPK * PEER_TOPK)
        cidx = (si[:, :, 0, :, None] * PEER_KEYS + si[:, :, 1, None, :]).reshape(m, PEER_HEADS, PEER_TOPK * PEER_TOPK)
        cs, cp = lax.top_k(cand, PEER_TOPK)
        e = jnp.take_along_axis(cidx, cp, axis=-1)
        g = jax.nn.softmax(cs, axis=-1)
        act = jax.nn.gelu(jnp.einsum('nd,nhkd->nhk', xt, u_tab[e], preferred_element_type=jnp.float32))
        return jnp.einsum('nhk,nhkd->nd', (g * act).astype(xt.dtype), v_tab[e])

    out = lax.map(per_block, xb).reshape(nb * PEER_BLOCK, shp[-1])[:n]
    return out.reshape(shp)

def shared_kv(h, pos, kv_norm, w_dkv, ckv_norm, w_kr):
    hn = rmsnorm(h, kv_norm)
    c = rmsnorm(hn @ w_dkv, ckv_norm)
    kr = rope(hn @ w_kr, pos)
    return c, kr

def mla_queries(x_n, pos, w_dq, q_norm, w_uq, w_uk):
    b, t, _ = x_n.shape
    q = (rmsnorm(x_n @ w_dq, q_norm) @ w_uq).reshape(b, t, N_HEADS, QK_NOPE + QK_ROPE)
    q_lat = jnp.einsum('bthn,chn->bthc', q[..., :QK_NOPE], w_uk)
    q_rope = rope(q[..., QK_NOPE:], pos)
    return q_lat, q_rope

def mla_attend(q_lat, q_rope, segments, w_uv):
    scores = []
    for c, kr, mask in segments:
        s = (jnp.einsum('bqhc,bkc->bhqk', q_lat, c, preferred_element_type=jnp.float32)
             + jnp.einsum('bqhr,bkr->bhqk', q_rope, kr, preferred_element_type=jnp.float32)) * SOFTMAX_SCALE
        if mask is not None:
            s = jnp.where(mask, s, NEG_INF)
        scores.append(s)
    p = jax.nn.softmax(jnp.concatenate(scores, axis=-1), axis=-1)
    o_lat, off = [], 0
    for c, _, _ in segments:
        tk = c.shape[1]
        o_lat.append(jnp.einsum('bhqk,bkc->bqhc', p[..., off:off + tk].astype(c.dtype), c))
        off += tk
    return jnp.einsum('bqhc,chv->bqhv', sum(o_lat), w_uv)

def mla_prompt_attention(q_lat, q_rope, pos, c, kr, w_uv):
    b, t = q_lat.shape[:2]
    nb = t // Q_BLOCK

    def per_block(args):
        ql, qr, qp = args
        mask = pos[None, :] <= qp[:, None]
        return mla_attend(ql, qr, [(c, kr, mask)], w_uv)

    def to_blocks(a):
        return jnp.swapaxes(a.reshape((b, nb, Q_BLOCK) + a.shape[2:]), 0, 1)

    o = lax.map(per_block, (to_blocks(q_lat), to_blocks(q_rope), pos.reshape(nb, Q_BLOCK)))
    return jnp.swapaxes(o, 0, 1).reshape(b, t, N_HEADS, V_HEAD)

def setup_inputs(seed: int = 0) -> dict:
    key = jax.random.key(seed)
    ks = iter(jax.random.split(key, 48))
    f32 = jnp.float32

    def nrm(shape, scale):
        return jax.random.normal(next(ks), shape, f32) * scale

    def gain(shape):
        return 1.0 + 0.02 * jax.random.normal(next(ks), shape, f32)

    n_pages = PAST_LEN // PAGE_SIZE
    n_used = DEC_BATCH * n_pages
    n_pool = n_used + n_used // 4
    x_prompt = nrm((BATCH, SEQ, D_MODEL), 1.0)
    x_sample = nrm((DEC_BATCH, DEC_SEQ, D_MODEL), 1.0)
    cache_ckv = nrm((n_pool, PAGE_SIZE, KV_LORA), 1.0)
    cache_krope = nrm((n_pool, PAGE_SIZE, QK_ROPE), 1.0)
    page_table = jax.random.permutation(next(ks), n_pool)[:n_used].reshape(DEC_BATCH, n_pages).astype(jnp.int32)
    state_h = nrm((DEC_BATCH, N_A_LAYERS, D_RNN), 0.5)
    state_conv = nrm((DEC_BATCH, N_A_LAYERS, CONV_W - 1, D_RNN), 1.0)
    ln_mix = gain((DEPTH, D_MODEL))
    ln_ffn = gain((DEPTH, D_MODEL))
    ln_final = gain((D_MODEL,))
    lru_w_in = nrm((N_A_LAYERS, D_MODEL, 2 * D_RNN), D_MODEL ** -0.5)
    lru_conv_w = nrm((N_A_LAYERS, CONV_W, D_RNN), CONV_W ** -0.5)
    lru_conv_b = nrm((N_A_LAYERS, D_RNN), 0.02)
    lru_gate_a_w = nrm((N_A_LAYERS, LRU_HEADS, LRU_BW, LRU_BW), LRU_BW ** -0.5)
    lru_gate_a_b = nrm((N_A_LAYERS, D_RNN), 0.02)
    lru_gate_x_w = nrm((N_A_LAYERS, LRU_HEADS, LRU_BW, LRU_BW), LRU_BW ** -0.5)
    lru_gate_x_b = nrm((N_A_LAYERS, D_RNN), 0.02)
    a_c = jax.random.uniform(next(ks), (N_A_LAYERS, D_RNN), f32, 0.9, 0.999)
    a0 = a_c ** (1.0 / LRU_C)
    lru_lambda = jnp.log(a0) - jnp.log1p(-a0)
    lru_w_out = nrm((N_A_LAYERS, D_RNN, D_MODEL), D_RNN ** -0.5)
    kv_norm = gain((D_MODEL,))
    w_dkv = nrm((D_MODEL, KV_LORA), D_MODEL ** -0.5)
    ckv_norm = gain((KV_LORA,))
    w_kr = nrm((D_MODEL, QK_ROPE), D_MODEL ** -0.5)
    w_uk = nrm((KV_LORA, N_HEADS, QK_NOPE), KV_LORA ** -0.5)
    w_uv = nrm((KV_LORA, N_HEADS, V_HEAD), KV_LORA ** -0.5)
    mla_w_dq = nrm((N_B_LAYERS, D_MODEL, Q_LORA), D_MODEL ** -0.5)
    mla_q_norm = gain((N_B_LAYERS, Q_LORA))
    mla_w_uq = nrm((N_B_LAYERS, Q_LORA, N_HEADS * (QK_NOPE + QK_ROPE)), Q_LORA ** -0.5)
    mla_w_o = nrm((N_B_LAYERS, N_HEADS * V_HEAD, D_MODEL), (N_HEADS * V_HEAD) ** -0.5)
    peer_w_q = nrm((DEPTH, D_MODEL, PEER_HEADS * PEER_DK), D_MODEL ** -0.5)
    peer_subkeys = nrm((DEPTH, PEER_HEADS, 2, PEER_KEYS, PEER_DK // 2), (PEER_DK // 2) ** -0.5)
    peer_u = nrm((DEPTH, PEER_EXPERTS, D_MODEL), D_MODEL ** -0.5)
    peer_v = nrm((DEPTH, PEER_EXPERTS, D_MODEL), 0.5 * PEER_HEADS ** -0.5)
    return {'x_prompt': x_prompt, 'x_sample': x_sample, 'cache_ckv': cache_ckv, 'cache_krope': cache_krope,
            'page_table': page_table, 'state_h': state_h, 'state_conv': state_conv,
            'ln_mix': ln_mix, 'ln_ffn': ln_ffn, 'ln_final': ln_final,
            'lru_w_in': lru_w_in, 'lru_conv_w': lru_conv_w, 'lru_conv_b': lru_conv_b,
            'lru_gate_a_w': lru_gate_a_w, 'lru_gate_a_b': lru_gate_a_b,
            'lru_gate_x_w': lru_gate_x_w, 'lru_gate_x_b': lru_gate_x_b,
            'lru_lambda': lru_lambda, 'lru_w_out': lru_w_out,
            'kv_norm': kv_norm, 'w_dkv': w_dkv, 'ckv_norm': ckv_norm, 'w_kr': w_kr, 'w_uk': w_uk, 'w_uv': w_uv,
            'mla_w_dq': mla_w_dq, 'mla_q_norm': mla_q_norm, 'mla_w_uq': mla_w_uq, 'mla_w_o': mla_w_o,
            'peer_w_q': peer_w_q, 'peer_subkeys': peer_subkeys, 'peer_u': peer_u, 'peer_v': peer_v}

def reference(x_prompt, x_sample, cache_ckv, cache_krope, page_table, state_h, state_conv,
              ln_mix, ln_ffn, ln_final,
              lru_w_in, lru_conv_w, lru_conv_b, lru_gate_a_w, lru_gate_a_b, lru_gate_x_w, lru_gate_x_b,
              lru_lambda, lru_w_out,
              kv_norm, w_dkv, ckv_norm, w_kr, w_uk, w_uv,
              mla_w_dq, mla_q_norm, mla_w_uq, mla_w_o,
              peer_w_q, peer_subkeys, peer_u, peer_v):
    bp, sp, _ = x_prompt.shape
    bd, sd, _ = x_sample.shape
    pos_p = jnp.arange(sp, dtype=jnp.int32)
    pos_d = PAST_LEN + jnp.arange(sd, dtype=jnp.int32)
    past_len = page_table.shape[1] * cache_ckv.shape[1]
    c_past = cache_ckv[page_table].reshape(bd, past_len, KV_LORA)
    kr_past = cache_krope[page_table].reshape(bd, past_len, QK_ROPE)
    mask_new = pos_d[None, :] <= pos_d[:, None]

    conv_p0 = jnp.zeros((bp, CONV_W - 1, D_RNN), x_prompt.dtype)
    h_p0 = jnp.zeros((bp, D_RNN), x_prompt.dtype)
    hl_p, cb_p, hl_d, cb_d = [], [], [], []
    hp, hd = x_prompt, x_sample
    c_p = kr_p = c_d = kr_d = None
    for l in range(DEPTH):
        if l < N_A_LAYERS:
            la = l
            wts = (lru_w_in[la], lru_conv_w[la], lru_conv_b[la], lru_gate_a_w[la], lru_gate_a_b[la],
                   lru_gate_x_w[la], lru_gate_x_b[la], lru_lambda[la], lru_w_out[la])
            yp, bufp, hlp = rglru_mixer(rmsnorm(hp, ln_mix[l]), conv_p0, h_p0, *wts)
            yd, bufd, hld = rglru_mixer(rmsnorm(hd, ln_mix[l]), state_conv[:, la], state_h[:, la], *wts)
            hl_p.append(hlp)
            cb_p.append(bufp)
            hl_d.append(hld)
            cb_d.append(bufd)
        else:
            lb = l - N_A_LAYERS
            qw = (mla_w_dq[lb], mla_q_norm[lb], mla_w_uq[lb], w_uk)
            ql_p, qr_p = mla_queries(rmsnorm(hp, ln_mix[l]), pos_p, *qw)
            op = mla_prompt_attention(ql_p, qr_p, pos_p, c_p, kr_p, w_uv)
            ql_d, qr_d = mla_queries(rmsnorm(hd, ln_mix[l]), pos_d, *qw)
            od = mla_attend(ql_d, qr_d, [(c_past, kr_past, None), (c_d, kr_d, mask_new)], w_uv)
            yp = op.reshape(bp, sp, N_HEADS * V_HEAD) @ mla_w_o[lb]
            yd = od.reshape(bd, sd, N_HEADS * V_HEAD) @ mla_w_o[lb]
        hp = hp + yp
        hd = hd + yd
        pw = (peer_w_q[l], peer_subkeys[l], peer_u[l], peer_v[l])
        hp = hp + peer_ffn(rmsnorm(hp, ln_ffn[l]), *pw)
        hd = hd + peer_ffn(rmsnorm(hd, ln_ffn[l]), *pw)
        if l == N_A_LAYERS - 1:
            c_p, kr_p = shared_kv(hp, pos_p, kv_norm, w_dkv, ckv_norm, w_kr)
            c_d, kr_d = shared_kv(hd, pos_d, kv_norm, w_dkv, ckv_norm, w_kr)

    y_prompt = rmsnorm(hp, ln_final)
    y_sample = rmsnorm(hd, ln_final)
    state_h_prompt = jnp.stack(hl_p, axis=1)
    state_conv_prompt = jnp.stack(cb_p, axis=1)
    state_h_sample = jnp.stack(hl_d, axis=1)
    state_conv_sample = jnp.stack(cb_d, axis=1)
    return (y_prompt, y_sample, state_h_prompt, state_conv_prompt, c_p, kr_p,
            state_h_sample, state_conv_sample, c_d, kr_d)


_drawn_inputs = setup_inputs


def setup_inputs(seed=0):
    import zlib

    import numpy as np

    out = dict(_drawn_inputs(seed))
    spreads = {}
    factors = {'ln_mix': 2.799,
     'ln_ffn': 2.941,
     'ln_final': 2.851,
     'lru_gate_a_b': 8.0,
     'lru_gate_x_b': 6.806,
     'kv_norm': 2.804,
     'ckv_norm': 2.9,
     'mla_q_norm': 8.0}
    for name, (base, spread) in spreads.items():
        noise = np.random.default_rng([zlib.crc32(name.encode()), seed]).standard_normal(out[name].shape)
        drawn = base * np.exp(spread * noise) if base else spread * noise
        out[name] = jnp.asarray(drawn.astype(out[name].dtype))
    for name, factor in factors.items():
        out[name] = (out[name] * factor).astype(out[name].dtype)
    return out
```

```python
from contextlib import ExitStack

import numpy as np

import concourse.bass as bass
from concourse import mybir

F32 = mybir.dt.float32
F32R = mybir.dt.float32r
U32 = mybir.dt.uint32
I32 = mybir.dt.int32
ALU = mybir.AluOpType
ACT = mybir.ActivationFunctionType
AX_X = mybir.AxisListType.X

P = 128
D = 1024
DC = D // P
SEQ, DB, DS = 256, 8, 4
NSAMP = DB * DS
TOK = SEQ + NSAMP
PAST, PAGE = 1024, 128
NPAGES = PAST // PAGE
NPOOL = 80
CONV = 4
HIST = CONV - 1
HEADS, NOPE, ROPE, VH = 16, 64, 32, 64
LAT, QLORA = 256, 512
LC, QC = LAT // P, QLORA // P
SCALE = float(NOPE + ROPE) ** -0.5
PH, KEYS, TOPK = 8, 128, 16
EPS = 1e-6
NEG = -1e30
LOWEST = -3.0e38
BLOCKS = [(0, 128), (128, 128), (256, NSAMP)]

SLOTS = 4
TILE = 1024
HALF = TILE // 2
PHASES = [("w_x", 8), ("w_gate", 8), ("w_out", 8), ("wq0", 16), ("u0", 128), ("v0", 128),
          ("kv", 4), ("w_dq", 4), ("w_uq", 8), ("w_o", 8), ("wq1", 16), ("u1", 128), ("v1", 128)]
FIRST = {}
NTILES = 0
for _name, _n in PHASES:
    FIRST[_name] = NTILES
    NTILES += _n
COUNT = dict(PHASES)

XBW = HIST + SEQ + DB * (HIST + DS)
SCW = SEQ + DB * (1 + DS)

G_MIX0, G_FFN0, G_MIX1, G_FFN1, G_FIN, G_KV, G_CKV, G_Q = 0, 8, 16, 24, 32, 40, 48, 50
NGAIN = 54
C_W, C_B, C_GA, C_GX, C_LAM = 0, 32, 40, 48, 56
NLRU = 64


class Steps:

    def __init__(self, eng, sem):
        self.eng, self.sem, self.n = eng, sem, 0

    def __call__(self, ins):
        self.n += 1
        ins.then_inc(self.sem, 1)
        self.eng.wait_ge(self.sem, self.n)


def build(nc, a, o):
    with ExitStack() as ctx:
        BASE = (nc.sbuf_base + 63) // 64 * 64
        HBW = P * TOK
        R0, RAW, HL = HBW, HBW + 4608, HBW + 4608 + SLOTS * TILE
        KON = HL + 4 * TILE

        def at(name, word, shape, dt=F32):
            return nc.alloc_sbuf_tensor_at(name, shape, dt, offset=BASE + 4 * word)

        def sem(name):
            return ctx.enter_context(nc.semaphore(name))

        raw = [at(f"raw{s}", RAW + s * TILE, [P, TILE]) for s in range(SLOTS)]
        hi = [at(f"hi{s}", HL + s * TILE, [P, HALF], F32R) for s in range(4)]
        lo = [at(f"lo{s}", HL + s * TILE + HALF, [P, HALF], F32R) for s in range(4)]
        X = at("X", KON, [P, DC, TOK])
        E = at("E", KON + 2304, [P, 3, P])
        CM = at("CM", KON + 2688, [P, 3, P])
        ident = at("ident", KON + 3072, [P, P])
        blk = at("blk", KON + 3200, [P, P])
        iota = at("iota", KON + 3328, [P, P])
        gains = at("gains", KON + 3456, [P, NGAIN])
        assert BASE + 4 * (KON + 3456 + NGAIN) <= nc.sbuf_usable_end

        SQ = at("SQ", HL, [P, DC, TOK])
        ones = at("ones", HL + 2304, [P, P])
        RT = at("RT", HL + 2432, [P, TOK])
        RV = at("RV", HL + 2720, [P, TOK])
        XN = at("XN", 25600, [P, DC, TOK])

        XB = at("XB", 0, [P, DC, XBW])
        XC = at("XC", 2560, [P, DC, TOK])
        GATE = at("GATE", 4864, [P, DC, TOK])
        RG = at("RG", 7168, [P, DC, TOK])
        IG = at("IG", 9536, [P, DC, TOK])
        LA = at("LA", 11840, [P, DC, SCW])
        LB = at("LB", 14208, [P, DC, SCW])
        LH = at("LH", 16576, [P, DC, SCW])
        Y = at("Y", 18944, [P, DC, TOK])
        T1 = at("T1", 21248, [P, DC, TOK])
        T2 = at("T2", 16576, [P, DC, TOK])
        wg = at("wg", 23552, [P, 2 * DC, P])
        hist = at("hist", 27904, [P, DC, DB, HIST])
        h0 = at("h0", 28096, [P, DC, DB])
        lru = at("lru", 28160, [P, NLRU])
        SP = at("SP", 28224, [P, 10, DC])
        HS = at("HS", 28352, [P, DC, 1 + DB])
        CV = at("CV", 28480, [P, DC, (1 + DB) * HIST])

        HB = at("HB", 0, [P, P, TOK])
        XH = at("XH", R0, [P, DC, TOK], F32R)
        XL = at("XL", R0 + 2304, [P, DC, TOK], F32R)
        XP = at("XP", 15840, [P, DC, TOK])
        QT = at("QT", 18144, [P, 2 * PH, TOK])
        SK = at("SK", 22752, [P, 2 * PH, KEYS])
        FREE_Q = 15840 // TOK
        S = at("S", 24800, [P, 3, 2 * PH, KEYS])
        FREE_S = 24800 // TOK
        W0 = 24800 + 6144
        V16 = at("V16", W0, [P, 2 * PH, TOPK])
        I16 = at("I16", W0 + 256, [P, 2 * PH, TOPK], U32)
        IF = at("IF", W0 + 512, [P, 2 * PH, TOPK])
        CAND = at("CAND", W0 + 768, [P, PH, TOPK, TOPK])
        CS = at("CS", W0 + 2816, [P, PH, TOPK])
        CP = at("CP", W0 + 2944, [P, PH, TOPK], U32)
        CA = at("CA", W0 + 3072, [P, 2, PH * TOPK], U32)
        CF = at("CF", W0 + 3328, [P, 2, PH * TOPK])
        EE = at("EE", W0 + 3584, [P, 2, PH * TOPK])
        IT = at("IT", R0, [P, TOK])
        JT = at("JT", R0 + 288, [P, TOK])
        GT = at("GT", R0 + 576, [P, TOK])
        EU = at("EU", R0 + 864, [P, TOK], U32)
        IU = at("IU", R0 + 1152, [P, TOK], U32)
        JU = at("JU", R0 + 1440, [P, TOK], U32)
        EX = at("EX", R0 + 1728, [P, TOK])
        ohi = [at(f"ohi{b}", R0 + 2048 + 1024 * b, [P, 4, P]) for b in range(2)]
        ohj = [at(f"ohj{b}", R0 + 2560 + 1024 * b, [P, 4, P]) for b in range(2)]
        WH = [at(f"WH{b}", R0 + 288 * b, [P, TOK], F32R) for b in range(2)]
        WL = [at(f"WL{b}", R0 + 576 + 288 * b, [P, TOK], F32R) for b in range(2)]

        QL = at("QL", 0, [P, LC, HEADS, TOK])
        QR = at("QR", 9216, [ROPE, HEADS, TOK])
        CT = at("CT", 13824, [P, LC, TOK])
        KR = at("KR", 14400, [ROPE, TOK])
        KT = at("KT", 14688, [ROPE, TOK])
        CN = at("CN", 14976, [P, 3, LAT])
        QN = at("QN", 15744, [P, HEADS // 2, TOK])
        QRC = at("QRC", 18048, [P, 4, TOK])
        QRS = at("QRS", 19200, [P, 4, TOK])
        CQ = at("CQ", 20352, [P, QC, TOK])
        CQN = at("CQN", 21504, [P, QC, TOK])
        wuk = at("wuk", 22656, [P, HEADS // 2, LAT])
        OL = at("OL", 15744, [P, LC, HEADS, TOK])
        stat = at("stat", 24960, [P, 2, 8])
        smask = at("smask", 25024, [HEADS * DS, DB, NSAMP])
        CR = at("CR", 30000, [P, LC, TOK])
        QLS = at("QLS", 25600, [P, LC, DB, HEADS * DS])
        QRP = at("QRP", 26624, [ROPE, DB, HEADS * DS])
        AO = at("AO", 25600, [P, DC, TOK])
        wuv = at("wuv", 27904, [P, LC, HEADS * VH])
        PP = [at(f"PP{b}", 29952 + 256 * b, [P, SEQ]) for b in range(2)]
        PT = [at(f"PT{b}", 30464 + 256 * b, [P, 2, P]) for b in range(2)]
        PTS = at("PTS", 29952, [P, NPAGES + 1, HEADS * DS])
        PS = [at(f"PS{b}", HL + 1024 + 1088 * b, [HEADS * DS, PAST + NSAMP]) for b in range(2)]
        PGW = 2 * LAT + PAGE
        page = [at("page0", 30976, [P, NPAGES, PGW]), at("page1", 30976 + NPAGES * PGW, [P, NPAGES, PGW])]
        COS = at("COS", KON + 2304, [P, TOK])
        SIN = at("SIN", KON + 2592, [P, TOK])
        causal = at("causal", KON + 2880, [P, P])
        pages = at("pages", 25280, [1, DB * NPAGES], I32)

        ps = [ctx.enter_context(nc.psum_tensor(f"ps{b}", [P, 512], F32)) for b in range(8)]

        raw_full = [sem(f"raw_full{s}") for s in range(SLOTS)]
        x_in, const_in, lru_in, sk_in, mla_in, out_dma = map(sem, (
            "x_in", "const_in", "lru_in", "sk_in", "mla_in", "out_dma"))
        pg_in = [sem("pg_in0"), sem("pg_in1")]
        proj_done, proj_evac = sem("proj_done"), sem("proj_evac")
        sq_ready, ones_ready, ss_done, ms_ready, sqrt_ready, xn_ready, x_ready = map(sem, (
            "sq_ready", "ones_ready", "ss_done", "ms_ready", "sqrt_ready", "xn_ready", "x_ready"))
        act_step, dve_step, pool_step = sem("act_step"), sem("dve_step"), sem("pool_step")
        sp_act, sp_dve = sem("sp_act"), sem("sp_dve")
        hist_ready, xc_ready, z_ready, at_ready, m2_ready, m_ready, y_ready, st_ready = map(sem, (
            "hist_ready", "xc_ready", "z_ready", "at_ready", "m2_ready", "m_ready", "y_ready", "st_ready"))
        s_done, s_evac, xh_ready, xl_ready = map(sem, ("s_done", "s_evac", "xh_ready", "xl_ready"))
        hi_ready, lo_ready, mm_done, h_evac = map(sem, ("hi_ready", "lo_ready", "mm_done", "h_evac"))
        topk_done, tr_done, ex_ready, bs_done, ij_ready, gt_ready = map(sem, (
            "topk_done", "tr_done", "ex_ready", "bs_done", "ij_ready", "gt_ready"))
        dif_ready, dif_sq, ohi_ready, ohj_ready, g_done, g_used = map(sem, (
            "dif_ready", "dif_sq", "ohi_ready", "ohj_ready", "g_done", "g_used"))
        kr_ready, ct_ready, cnt_done, cn_ready, qr_ready, qr_in = map(sem, (
            "kr_ready", "ct_ready", "cnt_done", "cn_ready", "qr_ready", "qr_in"))
        sc_done, nm_ready, p_exp, p_ready, pt_done, pt_ready, pv_done, ol_ready = map(sem, (
            "sc_done", "nm_ready", "p_exp", "p_ready", "pt_done", "pt_ready", "pv_done", "ol_ready"))
        gate_ready = sem("gate_ready")
        y_fin, qs_ready, kv_free = sem("y_fin"), sem("qs_ready"), sem("kv_free")

        PLAIN, EVAC = {}, {}
        n = 0
        for name, k in [("w_x", 8), ("gates", 16), ("w_gate", 8), ("w_out", 8), ("wq0", 16), ("kv", 4), ("w_dq", 4),
                        ("w_uq", 8), ("q_lat", 32), ("v_up", 8), ("w_o", 8), ("wq1", 16)]:
            PLAIN[name] = n
            EVAC[name] = n if n <= PLAIN["kv" if "kv" in PLAIN else name] else n - 4
            n += k

        def last_use(phase, k):
            if phase[0] in "uv":
                return lo_ready, 512 * int(phase[1]) + (0 if phase[0] == "u" else 256) + 2 * k + 2
            return proj_done, PLAIN[phase] + k + 1

        block = ctx.enter_context(nc.Block())

        @block.sync
        def _(sp):
            sp.dma_start(X[:], a["x"]).then_inc(x_in, 16)

            def load(t, s):
                src = a["stream"][t] if isinstance(t, int) else \
                    a["stream"][bass.ds(t, 1)].rearrange("a p f -> (a p) f")
                sp.dma_start(raw[s][:], src).then_inc(raw_full[s], 16)

            before = None
            for phase, count in PHASES:
                t0 = FIRST[phase]
                if phase == "w_o":
                    sp.wait_ge(mla_in, 16 * MLA_LOADS)
                    sp.wait_ge(x_ready, 2)
                    for b in range(DB):
                        if b >= 2:
                            sp.wait_ge(pv_done, 32 + b - 1)
                        else:
                            sp.wait_ge(ol_ready, 1 + 0 * b)
                        for j in range(NPAGES):
                            n = b * NPAGES + j
                            pg = sp.value_load(pages[0:1, n:n + 1], min_val=0, max_val=NPOOL - 1)
                            sp.dma_start(page[b % 2][:, j, :], a["pool"][bass.ds(pg, 1)].rearrange("a p f -> (a p) f"))\
                                .then_inc(pg_in[b % 2], 16)
                for s in range(SLOTS):
                    if before:
                        sp.wait_ge(*last_use(before, COUNT[before] - SLOTS + s))
                    load(t0 + s, s)
                if count > SLOTS:
                    with sp.Fori(1, count // SLOTS) as i:
                        for s in range(SLOTS):
                            used, value = last_use(phase, s - SLOTS)
                            rate = 2 if phase[0] in "uv" else 1
                            sp.wait_ge(used, i * (SLOTS * rate) + value)
                            load(i * SLOTS + t0 + s, s)
                before = phase
            sp.wait_ge(y_fin, 1)
            sp.dma_start(o["y"], X[:]).then_inc(out_dma, 16)
            sp.wait_ge(out_dma, 16 * 5)

        @block.tensor
        def _(pe):
            def full(phase, i, s):
                pe.wait_ge(raw_full[s], i * 16 + 16 * (FIRST[phase] // SLOTS + 1))

            def norm(k, chunks):
                pe.wait_ge(sq_ready, k + 1)
                pe.wait_ge(ones_ready, k + 1)
                for c in range(chunks):
                    mm = pe.matmul(ps[7][:, 0:TOK], ones[:], SQ[:, c, :], start=c == 0, stop=c == chunks - 1)
                mm.then_inc(ss_done, 1)

            def project(phase, xin, chunks=DC, m=P):
                def tile(i, s):
                    full(phase, i, s)
                    p = EVAC[phase] + s
                    if not isinstance(i, int) or i * SLOTS + p - 3 > 0:
                        pe.wait_ge(proj_evac, i * SLOTS + p - 3)
                    for c in range(chunks):
                        mm = pe.matmul(ps[s][:, 0:TOK], raw[s][:, c * P:(c + 1) * P], xin[:, c, :],
                                       start=c == 0, stop=c == chunks - 1)
                    mm.then_inc(proj_done, 1)

                for s in range(SLOTS):
                    tile(0, s)
                if COUNT[phase] > SLOTS:
                    with pe.Fori(1, COUNT[phase] // SLOTS) as i:
                        for s in range(SLOTS):
                            tile(i, s)

            def experts(l):
                kn = (1, 5)[l]
                norm(kn, DC)
                pe.wait_ge(xn_ready, (2, 7)[l])
                project(f"wq{l}", XP)
                pe.wait_ge(proj_evac, EVAC[f"wq{l}"] + 16)
                pe.wait_ge(sk_in, 16 * (l + 1))
                for nb, (n0, rows) in enumerate(BLOCKS):
                    for g in range(4):
                        k = 12 * l + 4 * nb + g
                        if k >= 4:
                            pe.wait_ge(s_evac, k - 3)
                        for q in range(4):
                            hp = 4 * g + q
                            mm = pe.matmul(ps[4 + g][0:rows, q * KEYS:(q + 1) * KEYS], QT[:, hp, n0:n0 + rows],
                                           SK[:, hp, :], start=True, stop=True)
                        mm.then_inc(s_done, 1)
                pe.wait_ge(xl_ready, l + 1)

                def h_tile(i, s):
                    if not isinstance(i, int) or 128 * l + s - 3 > 0:
                        pe.wait_ge(h_evac, i * SLOTS + 128 * l + s - 3)
                    for half in range(2):
                        k = 2 * s + half
                        pe.wait_ge(lo_ready, i * (2 * SLOTS) + 512 * l + k + 1)
                        for c in range(4 * half, 4 * half + 4):
                            w = slice((c % 4) * P, (c % 4 + 1) * P)
                            h, r = hi[k % 4][:, w], lo[k % 4][:, w]
                            pe.matmul(ps[s][:, 0:TOK], h, XH[:, c, :], start=c == 0, stop=False)
                            pe.matmul(ps[s][:, 0:TOK], h, XL[:, c, :], start=False, stop=False)
                            mm = pe.matmul(ps[s][:, 0:TOK], r, XH[:, c, :], start=False, stop=c == DC - 1)
                        mm.then_inc(mm_done, 1)

                for s in range(SLOTS):
                    h_tile(0, s)
                with pe.Fori(1, P // SLOTS) as i:
                    for s in range(SLOTS):
                        h_tile(i, s)
                pe.wait_ge(topk_done, 3 * (l + 1))
                for bank, src in ((4, E), (5, CM)):
                    for nb, (n0, rows) in enumerate(BLOCKS):
                        mm = pe.transpose(ps[bank][:, n0:n0 + rows], src[0:rows, nb, :], ident[0:rows, 0:rows])
                    mm.then_inc(tr_done, 1)
                pe.wait_ge(ex_ready, l + 1)
                pe.matmul(ps[6][:, 0:TOK], blk[:], EX[:], start=True, stop=True).then_inc(bs_done, 1)
                pe.wait_ge(gt_ready, l + 1)

                def g_batch(i, u):
                    pe.wait_ge(ohi_ready, i * 4 + 72 * l + u + 1)
                    pe.wait_ge(ohj_ready, i * 4 + 72 * l + u + 1)
                    if not isinstance(i, int) or 72 * l + u - 3 > 0:
                        pe.wait_ge(g_used, i * 4 + 72 * l + u - 3)
                    for t in range(4):
                        mm = pe.matmul(ps[u][:, t * P:(t + 1) * P], ohi[u % 2][:, t, :], ohj[u % 2][:, t, :],
                                       start=True, stop=True)
                    mm.then_inc(g_done, 1)

                for u in range(4):
                    g_batch(0, u)
                with pe.Fori(1, TOK // 16) as i:
                    for u in range(4):
                        g_batch(i, u)

                def v_tile(i, s, first, last):
                    for half in range(2):
                        k = 2 * s + half
                        pe.wait_ge(lo_ready, i * (2 * SLOTS) + 512 * l + 256 + k + 1)
                        for c in range(4 * half, 4 * half + 4):
                            w = slice((c % 4) * P, (c % 4 + 1) * P)
                            for bank, d0, n0, n1, opens in V_OUT[c]:
                                for n, (x, y) in enumerate(((hi, WH), (hi, WL), (lo, WH))):
                                    mm = pe.matmul(ps[bank][:, d0:d0 + n1 - n0], x[k % 4][:, w], y[s % 2][:, n0:n1],
                                                   start=first and opens and n == 0, stop=last and n == 2,
                                                   skip_group_check=True)
                        mm.then_inc(mm_done, 1)

                for s in range(SLOTS):
                    v_tile(0, s, s == 0, False)
                with pe.Fori(1, P // SLOTS - 1) as i:
                    for s in range(SLOTS):
                        v_tile(i, s, False, False)
                for s in range(SLOTS):
                    v_tile(P // SLOTS - 1, s, False, s == SLOTS - 1)

            pe.wait_ge(const_in, 16 * 4)
            norm(0, DC)
            pe.wait_ge(xn_ready, 1)
            project("w_x", XN)
            pe.wait_ge(lru_in, 16 * 4)
            for k in range(16):
                p = PLAIN["gates"] + k
                pe.wait_ge(proj_evac, p - 3)
                pe.wait_ge(xc_ready, min(k, DC - 1) + 1)
                pe.matmul(ps[p % 4][:, 0:TOK], wg[:, k, :], XC[:, k % DC, :], start=True, stop=True)\
                    .then_inc(proj_done, 1)
            project("w_gate", XN)
            pe.wait_ge(y_ready, 1)
            project("w_out", Y)
            experts(0)

            norm(2, DC)
            pe.wait_ge(xn_ready, 3)
            for s in range(4):
                full("kv", 0, s)
                m = P if s < LC else ROPE
                for c in range(DC):
                    mm = pe.matmul(ps[s][0:m, 0:TOK], raw[s][:, c * m:(c + 1) * m], XN[:, c, :],
                                   start=c == 0, stop=c == DC - 1)
                mm.then_inc(proj_done, 1)
            norm(3, LC)
            pe.wait_ge(xn_ready, 4)
            pe.wait_ge(kv_free, 1)
            project("w_dq", XN)
            pe.wait_ge(ct_ready, 1)
            for nb, (n0, rows) in enumerate(BLOCKS):
                for c in range(LC):
                    mm = pe.transpose(ps[4 + nb][0:rows, c * P:(c + 1) * P], CT[:, c, n0:n0 + rows], ident[:])
            mm.then_inc(cnt_done, 1)
            norm(4, QC)
            pe.wait_ge(xn_ready, 6)
            pe.wait_ge(cn_ready, 1)
            for t in range(8):
                i, s = divmod(t, SLOTS)
                full("w_uq", i, s)
                pe.wait_ge(proj_evac, EVAC["w_uq"] + (t - 3 if t < 4 else 4))
                for half in range(2):
                    for c in range(QC):
                        mm = pe.matmul(ps[s + 4 * half][:, 0:TOK], raw[s][:, (half * QC + c) * P:(half * QC + c + 1) * P],
                                       CQN[:, c, :], start=c == 0, stop=c == QC - 1)
                mm.then_inc(proj_done, 1)
            pe.wait_ge(mla_in, 16 * MLA_LOADS)
            for h in range(HEADS):
                for c in range(LC):
                    p = PLAIN["q_lat"] + LC * h + c
                    k = EVAC["q_lat"] + LC * h + c
                    pe.wait_ge(proj_evac, k if k == EVAC["q_lat"] else k - 3)
                    r = slice(NOPE * (h % 2), NOPE * (h % 2) + NOPE)
                    pe.matmul(ps[p % 4][:, 0:TOK], wuk[r, h // 2, c * P:(c + 1) * P], QN[r, h // 2, :],
                              start=True, stop=True).then_inc(proj_done, 1)
            pe.wait_ge(proj_evac, EVAC["q_lat"] + 32)
            pe.wait_ge(qr_in, 16 * 4)

            def p_scores(m):
                qb, h = divmod(m, HEADS)
                q = slice(qb * P, qb * P + P)
                kk = P * (qb + 1)
                out = ps[m % 2][:, 0:kk]
                if m >= 2:
                    pe.wait_ge(nm_ready, m - 1)
                for c in range(LC):
                    pe.matmul(out, QL[:, c, h, q], CT[:, c, 0:kk], start=c == 0, stop=False)
                pe.matmul(out, QR[:, h, q], KR[:, 0:kk], start=False, stop=True).then_inc(sc_done, 1)

            def p_turn(m):
                qb = m // HEADS
                pe.wait_ge(p_ready, m + 1)
                if m >= 2:
                    pe.wait_ge(pt_ready, m - 1)
                for kb in range(qb + 1):
                    mm = pe.transpose(ps[2 + m % 2][:, kb * P:(kb + 1) * P], PP[m % 2][:, kb * P:(kb + 1) * P], ident[:])
                mm.then_inc(pt_done, 1)

            def p_values(m):
                qb = m // HEADS
                pe.wait_ge(pt_ready, m + 1)
                if m >= 2:
                    pe.wait_ge(ol_ready, m)
                for c in range(LC):
                    for kb in range(qb + 1):
                        mm = pe.matmul(ps[4 + m % 2][:, c * P:(c + 1) * P], CN[:, kb, c * P:(c + 1) * P],
                                       PT[m % 2][:, kb, :], start=kb == 0, stop=kb == qb)
                mm.then_inc(pv_done, 1)

            for m in range(32 + 2):
                if m < 32:
                    p_scores(m)
                if 1 <= m <= 32:
                    p_turn(m - 1)
                if m >= 2:
                    p_values(m - 2)

            pe.wait_ge(qs_ready, 1)

            def s_scores(b):
                bk = 3 * (b % 2)
                pe.wait_ge(pg_in[b % 2], 16 * NPAGES * (b // 2 + 1))
                if b >= 2:
                    pe.wait_ge(p_exp, 32 + b - 1)
                else:
                    pe.wait_ge(ol_ready, 33)
                q = [QLS[:, c, b, :] for c in range(LC)] + [QRP[:, b, :]]
                for half in range(2):
                    pg = slice(4 * half, 4 * half + 4)
                    keys = [page[b % 2][:, pg, LAT + c * PAGE:LAT + (c + 1) * PAGE] for c in range(LC)]
                    keys.append(page[b % 2][0:ROPE, pg, 2 * LAT:])
                    for k in range(3):
                        pe.matmul(ps[bk + half][0:64, :], q[k], keys[k], start=k == 0, stop=k == 2)
                keys = [CT[:, c, SEQ:TOK] for c in range(LC)] + [KR[:, SEQ:TOK]]
                for k in range(3):
                    mm = pe.matmul(ps[bk + 2][0:64, 0:NSAMP], q[k], keys[k], start=k == 0, stop=k == 2)
                mm.then_inc(sc_done, 1)

            def s_turn(b):
                pe.wait_ge(p_ready, 32 + b + 1)
                if b >= 1:
                    pe.wait_ge(ol_ready, 32 + b + 1)
                for j in range(NPAGES):
                    pe.transpose(ps[6][:, 64 * j:64 * j + 64], PS[b % 2][:, j * P:(j + 1) * P], ident[0:64, 0:64])
                pe.transpose(ps[7][0:NSAMP, 128:192], PS[b % 2][:, PAST:PAST + NSAMP], ident[0:64, 0:64])\
                    .then_inc(pt_done, 1)

            def s_values(b):
                pe.wait_ge(pt_ready, 32 + b + 1)
                for c in range(LC):
                    w = slice(c * P, (c + 1) * P)
                    for j in range(NPAGES):
                        pe.matmul(ps[7][:, 64 * c:64 * c + 64], page[b % 2][:, j, w], PTS[:, j, :],
                                  start=j == 0, stop=False)
                    mm = pe.matmul(ps[7][:, 64 * c:64 * c + 64], CN[0:NSAMP, 2, w], PTS[0:NSAMP, NPAGES, :],
                                   start=False, stop=True)
                mm.then_inc(pv_done, 1)

            for b in range(DB + 1):
                if b < DB:
                    s_scores(b)
                if b >= 1:
                    s_turn(b - 1)
                    s_values(b - 1)
            pe.wait_ge(ol_ready, 32 + DB + 1)
            for k in range(HEADS // 2):
                p = PLAIN["v_up"] + k
                pe.wait_ge(proj_evac, EVAC["v_up"] + k - 3)
                for h in (2 * k, 2 * k + 1):
                    r = VH * (h % 2)
                    for c in range(LC):
                        mm = pe.matmul(ps[p % 4][r:r + VH, 0:TOK], wuv[:, c, h * VH:(h + 1) * VH], OL[:, c, h, :],
                                       start=c == 0, stop=c == LC - 1)
                mm.then_inc(proj_done, 1)
            pe.wait_ge(proj_evac, EVAC["w_o"])
            project("w_o", AO)
            experts(1)
            norm(6, DC)

        @block.scalar
        def _(act):
            link = Steps(act, act_step)

            def square(k, src, chunks):
                act.activation(SQ[:, 0:chunks, :], src, ACT.Square).then_inc(sq_ready, 1)
                act.wait_ge(ms_ready, k + 1)
                act.activation(RV[:], RV[:], ACT.Sqrt).then_inc(sqrt_ready, 1)

            def evacuate(phase, write):
                def tile(i, s):
                    act.wait_ge(proj_done, i * SLOTS + PLAIN[phase] + s + 1)
                    write(i * SLOTS + s, s).then_inc(proj_evac, 1)
                with act.Fori(0, COUNT[phase] // SLOTS) as i:
                    for s in range(SLOTS):
                        tile(i, s)

            def at_chunk(t, k):
                return t[:, bass.ds(k, 1), :].rearrange("p a n -> p (a n)")

            def experts(l):
                kn = (1, 5)[l]
                act.wait_ge(x_ready, 2 * l + 1)
                act.dma_start(SK[:], a["sk"][l]).then_inc(sk_in, 16)
                square(kn, X[:], DC)
                act.wait_ge(xn_ready, (2, 7)[l])
                act.activation(XH[:], XP[:], ACT.Copy).then_inc(xh_ready, 1)
                evacuate(f"wq{l}", lambda k, s: act.activation(at_chunk(QT, k), ps[s][:, 0:TOK], ACT.Copy))
                for nb, (n0, rows) in enumerate(BLOCKS):
                    for g in range(4):
                        act.wait_ge(s_done, 12 * l + 4 * nb + g + 1)
                        act.activation(S[0:rows, nb, 4 * g:4 * g + 4, :],
                                       ps[4 + g][0:rows, :].rearrange("p (q k) -> p q k", q=4), ACT.Copy)\
                            .then_inc(s_evac, 1)

                def split(i, s, phase, base):
                    act.wait_ge(raw_full[s], i * 16 + 16 * (FIRST[phase] // SLOTS + 1))
                    for half in range(2):
                        k = 2 * s + half
                        if not (isinstance(i, int) and base + 2 * SLOTS * i + k - 3 <= 0):
                            act.wait_ge(mm_done, i * (2 * SLOTS) + base + k - 3)
                        act.activation(hi[k % 4][:], raw[s][:, half * HALF:(half + 1) * HALF], ACT.Copy)\
                            .then_inc(hi_ready, 1)

                def gelu(i, s):
                    act.activation(at_chunk(HB, i * SLOTS + s), ps[s % SLOTS][:, 0:TOK], ACT.Gelu_apprx_tanh)\
                        .then_inc(h_evac, 1)

                def h_tile(i, s):
                    split(i, s, f"u{l}", 512 * l)
                    if not (isinstance(i, int) and SLOTS * i + s < 2):
                        gelu(i, s - 2)

                for s in range(SLOTS):
                    h_tile(0, s)
                for r0, r1 in ((1, FREE_Q // 4 + 1), (FREE_Q // 4 + 1, FREE_S // 4 + 1), (FREE_S // 4 + 1, 32)):
                    if r0 == FREE_Q // 4 + 1:
                        act.wait_ge(s_done, 12 * (l + 1))
                        act.wait_ge(xl_ready, l + 1)
                    if r0 == FREE_S // 4 + 1:
                        act.wait_ge(topk_done, 3 * (l + 1))
                    with act.Fori(r0, r1) as i:
                        for s in range(SLOTS):
                            h_tile(i, s)
                for s in (2, 3):
                    act.wait_ge(mm_done, 512 * l + 2 * (124 + s + 1))
                    gelu(31, s)
                act.wait_ge(tr_done, 2 * (l + 1))
                act.activation(EX[:], ps[5][:, 0:TOK], ACT.Exp).then_inc(ex_ready, 1)
                def g_onehot(i, u):
                    n = 72 * l + u + 1
                    act.wait_ge(dif_ready, i * 4 + n)
                    act.activation(ohi[u % 2][:], ohi[u % 2][:], ACT.Square).then_inc(dif_sq, 1)
                    act.wait_ge(dif_sq, i * 4 + n)
                    act.activation(ohi[u % 2][:], ohi[u % 2][:], ACT.Relu, scale=-1.0, bias=1.0).then_inc(ohi_ready, 1)

                with act.Fori(0, TOK // 16) as i:
                    for u in range(4):
                        g_onehot(i, u)
                act.wait_ge(g_used, 72 * (l + 1))

                def v_tile(i, s):
                    if not (isinstance(i, int)):
                        act.wait_ge(mm_done, i * (2 * SLOTS) + 512 * l + 256 + 2 * s - 2)
                    act.activation(WH[s % 2][:], at_chunk(HB, i * SLOTS + s), ACT.Copy)
                    split(i, s, f"v{l}", 512 * l + 256)

                with act.Fori(0, P // SLOTS) as i:
                    for s in range(SLOTS):
                        v_tile(i, s)

            for t, name in ((gains, "gains"), (ident, "ident"), (blk, "blk"), (iota, "iota")):
                act.dma_start(t[:], a[name]).then_inc(const_in, 16)
            for t, name in ((lru, "lru"), (hist, "hist"), (h0, "h0"), (wg, "wg")):
                act.dma_start(t[:], a[name]).then_inc(lru_in, 16)
            act.wait_ge(x_in, 16)
            square(0, X[:], DC)
            act.wait_ge(lru_in, 16 * 4)
            link(act.activation(SP[:, 0, :], lru[:, C_LAM:C_LAM + DC], ACT.Abs))
            act.activation(SP[:, 1, :], SP[:, 0, :], ACT.Exp, scale=-1.0).then_inc(sp_act, 1)
            act.wait_ge(sp_dve, 1)
            act.activation(SP[:, 3, :], SP[:, 2, :], ACT.Ln).then_inc(sp_act, 1)
            act.wait_ge(hist_ready, 1)
            for c in range(DC):
                s = c % SLOTS
                act.wait_ge(proj_done, c + 1)
                act.activation(XB[:, c, HIST:HIST + SEQ], ps[s][:, 0:SEQ], ACT.Copy)
                act.activation(XB[:, c, HIST + SEQ:XBW].rearrange("p (b t) -> p b t", b=DB)[:, :, HIST:],
                               ps[s][:, SEQ:TOK].rearrange("p (b t) -> p b t", b=DB), ACT.Copy)\
                    .then_inc(proj_evac, 1)
            for k in range(16):
                p = PLAIN["gates"] + k
                act.wait_ge(proj_done, p + 1)
                dst, bias = (RG, C_GA) if k < DC else (IG, C_GX)
                c = k % DC
                act.activation(dst[:, c, :], ps[p % 4][:, 0:TOK], ACT.Sigmoid, bias=lru[:, bias + c:bias + c + 1])\
                    .then_inc(proj_evac, 1)

            def gate_inputs(*chunks):
                for c in chunks:
                    act.wait_ge(proj_done, PLAIN["w_gate"] + c + 1)
                    act.activation(GATE[:, c, :], ps[c % SLOTS][:, 0:TOK], ACT.Copy).then_inc(proj_evac, 1)

            act.wait_ge(z_ready, 1)
            act.activation(LA[:, :, 0:SEQ], RG[:, :, 0:SEQ], ACT.Exp)
            act.activation(LA[:, :, SEQ:SCW].rearrange("p c (b t) -> p c b t", b=DB)[:, :, :, 1:],
                           RG[:, :, SEQ:TOK].rearrange("p c (b t) -> p c b t", b=DB), ACT.Exp)
            link(act.activation(T1[:], RG[:], ACT.Tanh, scale=-1.0))
            gate_inputs(0, 1)
            link(act.activation(T2[:], T1[:], ACT.Ln, bias=1.0))
            act.activation(T2[:], T2[:], ACT.Exp, scale=-1.0).then_inc(at_ready, 1)
            gate_inputs(2, 3, 4)
            act.wait_ge(m2_ready, 1)
            act.activation(T1[:], T1[:], ACT.Sqrt, scale=2.0).then_inc(m_ready, 1)
            gate_inputs(5, 6, 7)
            act.wait_ge(proj_evac, PLAIN["w_gate"] + DC)
            act.activation(GATE[:], GATE[:], ACT.Gelu_apprx_tanh).then_inc(gate_ready, 1)
            act.wait_ge(st_ready, 1)
            act.dma_start(o["h"], HS[:]).then_inc(out_dma, 16)
            act.dma_start(o["conv"], CV[:]).then_inc(out_dma, 16)
            act.wait_ge(out_dma, 32)
            experts(0)

            act.wait_ge(x_ready, 2)
            for t, name in ((COS, "cos"), (SIN, "sin"), (causal, "causal"), (smask, "smask"), (wuk, "wuk"),
                            (wuv, "wuv"), (pages, "pages")):
                act.dma_start(t[:], a[name]).then_inc(mla_in, 16)
            square(2, X[:], DC)
            for s in range(LC):
                act.wait_ge(proj_done, PLAIN["kv"] + s + 1)
                ins = act.activation(CR[:, s, :], ps[s][:, 0:TOK], ACT.Copy)
                if s == LC - 1:
                    link(ins)
            act.wait_ge(xn_ready, 4)
            square(3, CR[:], LC)
            evacuate("w_dq", lambda k, s: act.activation(at_chunk(CQ, k), ps[s][:, 0:TOK], ACT.Copy))
            act.wait_ge(cnt_done, 1)
            for nb, (n0, rows) in enumerate(BLOCKS):
                ins = act.activation(CN[0:rows, nb, :], ps[4 + nb][0:rows, 0:LAT], ACT.Copy)
            ins.then_inc(cn_ready, 1)
            act.wait_ge(proj_evac, EVAC["w_dq"] + 4)
            square(4, CQ[:], QC)
            act.wait_ge(ct_ready, 1)
            act.wait_ge(kr_ready, 1)
            act.dma_start(o["ckv"], CT[:]).then_inc(out_dma, 16)
            act.dma_start(o["kr"], KR[:]).then_inc(out_dma, 16)
            for t in range(4):
                act.wait_ge(proj_done, PLAIN["w_uq"] + t + 1)
                act.activation(QN[:, 2 * t, :], ps[t][:, 0:TOK], ACT.Copy)
                act.activation(QN[:, 2 * t + 1, :], ps[4 + t][:, 0:TOK], ACT.Copy).then_inc(proj_evac, 1)
            act.wait_ge(qr_ready, 1)
            for q in range(4):
                act.dma_start(QR[:].rearrange("r (g q) n -> r g q n", q=4)[:, :, q, :],
                              QRC[ROPE * q:ROPE * (q + 1), :, :]).then_inc(qr_in, 16)
            for h in range(HEADS):
                for c in range(LC):
                    p = PLAIN["q_lat"] + LC * h + c
                    act.wait_ge(proj_done, p + 1)
                    act.activation(QL[:, c, h, :], ps[p % 4][:, 0:TOK], ACT.Copy).then_inc(proj_evac, 1)
            act.wait_ge(qr_in, 16 * 4)
            act.wait_ge(proj_done, PLAIN["q_lat"] + 32)
            act.activation(stat[:, 0, 7:8], ident[:, 0:1], ACT.Copy).then_inc(ol_ready, 1)

            def p_exp_item(m):
                kk = P * (m // HEADS + 1)
                act.wait_ge(nm_ready, m + 1)
                act.activation(PP[m % 2][:, 0:kk], PP[m % 2][:, 0:kk], ACT.Exp, bias=stat[:, m % 2, 1:2],
                               scale=SCALE, accum_out=stat[:, m % 2, 2:3]).then_inc(p_exp, 1)

            def p_turn(m):
                qb = m // HEADS
                act.wait_ge(pt_done, m + 1)
                if m >= 2:
                    act.wait_ge(pv_done, m - 1)
                act.activation(PT[m % 2][:, 0:qb + 1, :], ps[2 + m % 2][:, 0:P * (qb + 1)].rearrange(
                    "p (k q) -> p k q", q=P), ACT.Copy).then_inc(pt_ready, 1)

            def p_out(m):
                qb, h = divmod(m, HEADS)
                act.wait_ge(pv_done, m + 1)
                act.activation(OL[:, :, h, qb * P:(qb + 1) * P],
                               ps[4 + m % 2][:, 0:LC * P].rearrange("p (c q) -> p c q", c=LC), ACT.Copy)\
                    .then_inc(ol_ready, 1)

            for m in range(32 + 2):
                if m < 32:
                    p_exp_item(m)
                if 1 <= m <= 32:
                    p_turn(m - 1)
                if m >= 2:
                    p_out(m - 2)

            def s_exp(b):
                bk = 3 * (b % 2)
                act.wait_ge(nm_ready, 32 + b + 1)
                st = stat[0:64, b % 2, :]
                for k in range(2):
                    act.activation(PS[b % 2][:, 512 * k:512 * k + 512], ps[bk + k][0:64, :], ACT.Exp,
                                   bias=st[:, 1:2], scale=SCALE, accum_out=st[:, 2 + k:3 + k])
                act.activation(PS[b % 2][:, PAST:], PS[b % 2][:, PAST:], ACT.Exp, bias=st[:, 1:2], scale=SCALE,
                               accum_out=st[:, 4:5]).then_inc(p_exp, 1)

            def s_turn(b):
                act.wait_ge(pt_done, 32 + b + 1)
                act.activation(PTS[:, 0:NPAGES, :], ps[6][:].rearrange("p (j q) -> p j q", q=64), ACT.Copy)
                act.activation(PTS[0:NSAMP, NPAGES, :], ps[7][0:NSAMP, 128:192], ACT.Copy).then_inc(pt_ready, 1)

            def s_out(b):
                act.wait_ge(pv_done, 32 + b + 1)
                n0 = SEQ + DS * b
                for c in range(LC):
                    ins = act.activation(OL[:, c, :, n0:n0 + DS],
                                         ps[7][:, 64 * c:64 * c + 64].rearrange("p (h t) -> p h t", t=DS), ACT.Copy)
                ins.then_inc(ol_ready, 1)

            for b in range(DB + 1):
                if b < DB:
                    s_exp(b)
                if b >= 1:
                    s_turn(b - 1)
                    s_out(b - 1)
            for k in range(HEADS // 2):
                p = PLAIN["v_up"] + k
                act.wait_ge(proj_done, p + 1)
                act.activation(AO[:, k, :], ps[p % 4][:, 0:TOK], ACT.Copy).then_inc(proj_evac, 1)
            experts(1)
            act.wait_ge(x_ready, 4)
            square(6, X[:], DC)

        @block.vector
        def _(dve):
            link = Steps(dve, dve_step)

            def ones_for(k):
                dve.memset(ones[:], 1.0).then_inc(ones_ready, 1)

            def inv_rms(k, width):
                dve.wait_ge(ss_done, k + 1)
                dve.tensor_scalar(RV[:], ps[7][:, 0:TOK], 1.0 / width, EPS, ALU.mult, ALU.add).then_inc(ms_ready, 1)
                dve.wait_ge(sqrt_ready, k + 1)
                link(dve.reciprocal(RT[:], RV[:]))

            def scaled(dst, src, gain, chunks):
                for c in range(chunks):
                    ins = dve.scalar_tensor_tensor(dst[:, c, :], src[:, c, :], gains[:, gain + c:gain + c + 1], RT[:],
                                                   ALU.mult, ALU.mult)
                return ins

            def add_to_x(phase):
                with dve.Fori(0, COUNT[phase] // SLOTS) as i:
                    for s in range(SLOTS):
                        dve.wait_ge(proj_done, i * SLOTS + PLAIN[phase] + s + 1)
                        xc = X[:, bass.ds(i * SLOTS + s, 1), :].rearrange("p a n -> p (a n)")
                        dve.tensor_tensor(xc, xc, ps[s][:, 0:TOK], ALU.add).then_inc(proj_evac, 1)
                dve.wait_ge(proj_evac, EVAC[phase] + COUNT[phase])

            def per_head(fn, count):
                for k in range(count):
                    ins = fn(k)
                link(ins)

            def topk(nb, rows):
                r = slice(0, rows)
                s = [S[r, nb, hp, :] for hp in range(2 * PH)]
                per_head(lambda k: dve.max(V16[r, k, 0:8], s[k]), 16)
                per_head(lambda k: dve.max_index(I16[r, k, 0:8], V16[r, k, 0:8], s[k]), 16)
                per_head(lambda k: dve.match_replace(s[k], V16[r, k, 0:8], s[k], LOWEST), 16)
                per_head(lambda k: dve.max(V16[r, k, 8:16], s[k]), 16)
                per_head(lambda k: dve.max_index(I16[r, k, 8:16], V16[r, k, 8:16], s[k]), 16)
                v = V16[r].rearrange("p (h t) k -> p h t k", t=2)
                c4 = CAND[r]
                link(dve.tensor_tensor(
                    c4, v[:, :, 0, :].unsqueeze(3).broadcast_to([rows, PH, TOPK, TOPK]),
                    v[:, :, 1, :].unsqueeze(2).broadcast_to([rows, PH, TOPK, TOPK]), ALU.add))
                c = [CAND[r, h].rearrange("p a b -> p (a b)") for h in range(PH)]
                per_head(lambda k: dve.max(CS[r, k, 0:8], c[k]), 8)
                per_head(lambda k: dve.max_index(CP[r, k, 0:8], CS[r, k, 0:8], c[k]), 8)
                per_head(lambda k: dve.match_replace(c[k], CS[r, k, 0:8], c[k], LOWEST), 8)
                per_head(lambda k: dve.max(CS[r, k, 8:16], c[k]), 8)
                per_head(lambda k: dve.max_index(CP[r, k, 8:16], CS[r, k, 8:16], c[k]), 8)
                cp = CP[r].rearrange("p h k -> p (h k)")
                dve.tensor_scalar(CA[r, 0, :], cp, 4, None, ALU.logical_shift_right)
                dve.tensor_scalar(CA[r, 1, :], cp, 15, None, ALU.bitwise_and)
                i2 = I16[r].rearrange("p (h t) k -> p h t k", t=2)
                f2 = IF[r].rearrange("p (h t) k -> p h t k", t=2)
                dve.tensor_scalar(f2[:, :, 0, :], i2[:, :, 0, :], float(KEYS), None, ALU.mult)
                dve.tensor_copy(f2[:, :, 1, :], i2[:, :, 1, :])
                link(dve.tensor_tensor(CM[r, nb].rearrange("p (h k) -> p h k", k=TOPK), CS[r],
                                       CS[r, :, 0:1].broadcast_to([rows, PH, TOPK]), ALU.subtract))
                link(dve.tensor_copy(CF[r], CA[r]))
                for t in range(2):
                    eq = CAND[r].rearrange("p h k a -> p (h k) a")
                    link(dve.tensor_tensor(eq, CF[r, t, :].unsqueeze(2).broadcast_to([rows, PH * TOPK, TOPK]),
                                           iota[r, 0:TOPK].unsqueeze(1).broadcast_to([rows, PH * TOPK, TOPK]),
                                           ALU.is_equal))
                    link(dve.tensor_tensor(c4, c4, f2[:, :, t, :].unsqueeze(2).broadcast_to([rows, PH, TOPK, TOPK]),
                                           ALU.mult))
                    link(dve.tensor_reduce(EE[r, t, :], eq, AX_X, ALU.add))
                dve.tensor_tensor(E[r, nb], EE[r, 0, :], EE[r, 1, :], ALU.add).then_inc(topk_done, 1)

            def experts(l):
                kn = (1, 5)[l]
                ones_for(kn)
                inv_rms(kn, D)
                scaled(XP, X, (G_FFN0, G_FFN1)[l], DC).then_inc(xn_ready, 1)
                dve.wait_ge(xh_ready, l + 1)
                dve.wait_ge(xn_ready, (2, 7)[l])
                dve.tensor_tensor(XL[:], XP[:], XH[:].bitcast(F32), ALU.subtract).then_inc(xl_ready, 1)
                for nb, (_, rows) in enumerate(BLOCKS):
                    dve.wait_ge(s_evac, 12 * l + 4 * nb + 4)
                    if 3 * l + nb:
                        dve.wait_ge(topk_done, 3 * l + nb)
                    topk(nb, rows)
                dve.wait_ge(tr_done, 2 * (l + 1))
                link(dve.tensor_copy(EU[:], ps[4][:, 0:TOK]))
                dve.tensor_scalar(IU[:], EU[:], 7, None, ALU.logical_shift_right)
                link(dve.tensor_scalar(JU[:], EU[:], KEYS - 1, None, ALU.bitwise_and))
                dve.tensor_copy(IT[:], IU[:])
                link(dve.tensor_copy(JT[:], JU[:]))
                dve.wait_ge(bs_done, l + 1)
                link(dve.reciprocal(GT[:], ps[6][:, 0:TOK]))
                dve.tensor_tensor(GT[:], GT[:], EX[:], ALU.mult).then_inc(gt_ready, 1)
                dve.wait_ge(gt_ready, l + 1)
                dve.wait_ge(h_evac, 128 * (l + 1))
                hb = HB[:].rearrange("p j n -> p n j")

                def g_onehot(i, u):
                    if not (isinstance(i, int) and 72 * l + u - 1 <= 0):
                        dve.wait_ge(g_done, i * 4 + 72 * l + u - 1)
                    for t in range(4):
                        n = i * 16 + 4 * u + t
                        ins = dve.tensor_scalar(ohj[u % 2][:, t, :], iota[:], JT[:, bass.ds(n, 1)],
                                                GT[:, bass.ds(n, 1)], ALU.is_equal, ALU.mult)
                    ins.then_inc(ohj_ready, 1)

                def g_apply(i, u):
                    dve.wait_ge(g_done, i * 4 + 72 * l + u + 1)
                    w = hb[:, bass.ds(i * 16 + 4 * u, 4), :]
                    dve.tensor_tensor(w, w, ps[u % 4][:].rearrange("p (n j) -> p n j", n=4), ALU.mult)\
                        .then_inc(g_used, 1)

                g_onehot(0, 0)
                with dve.Fori(0, TOK // 16 - 1) as i:
                    for u in range(4):
                        if u < 3:
                            g_onehot(i, u + 1)
                        else:
                            g_onehot(i + 1, 0)
                        g_apply(i, u)
                for u in range(4):
                    if u < 3:
                        g_onehot(TOK // 16 - 1, u + 1)
                    g_apply(TOK // 16 - 1, u)
                dve.wait_ge(g_used, 72 * (l + 1))
                with dve.Fori(0, P // SLOTS) as i:
                    for s in range(SLOTS):
                        for half in range(2):
                            k = 2 * s + half
                            dve.wait_ge(hi_ready, i * (2 * SLOTS) + 512 * l + 256 + k + 1)
                            if half == 0:
                                hbr = HB[:, bass.ds(i * SLOTS + s, 1), :].rearrange("p a n -> p (a n)")
                                dve.tensor_tensor(WL[s % 2][:], hbr, WH[s % 2][:].bitcast(F32), ALU.subtract)
                            dve.tensor_tensor(lo[k % 4][:], raw[s][:, half * HALF:(half + 1) * HALF],
                                              hi[k % 4][:].bitcast(F32), ALU.subtract).then_inc(lo_ready, 1)
                dve.wait_ge(mm_done, 512 * (l + 1))
                for c in range(DC):
                    for bank, d0, n0, n1, _ in V_OUT[c]:
                        ins = dve.tensor_tensor(X[:, c, n0:n1], X[:, c, n0:n1], ps[bank][:, d0:d0 + n1 - n0], ALU.add)
                ins.then_inc(x_ready, 1)
                dve.wait_ge(x_ready, 2 * (l + 1))

            ones_for(0)
            dve.wait_ge(const_in, 16 * 4)
            dve.wait_ge(x_in, 16)
            inv_rms(0, D)
            scaled(XN, X, G_MIX0, DC).then_inc(xn_ready, 1)
            dve.wait_ge(lru_in, 16 * 4)
            dve.wait_ge(sp_act, 1)
            dve.tensor_scalar(SP[:, 2, :], SP[:, 1, :], 1.0, None, ALU.add).then_inc(sp_dve, 1)
            dve.wait_ge(sp_dve, 1)
            link(dve.tensor_scalar(SP[:, 4, :], SP[:, 2, :], -1.0, None, ALU.add))
            dve.tensor_scalar(SP[:, 5, :], SP[:, 4, :], 1e-30, None, ALU.max)
            link(dve.scalar_tensor_tensor(SP[:, 7, :], SP[:, 4, :], 0.0, SP[:, 1, :], ALU.is_equal, ALU.mult))
            link(dve.reciprocal(SP[:, 6, :], SP[:, 5, :]))
            dve.wait_ge(sp_act, 2)
            link(dve.tensor_tensor(SP[:, 6, :], SP[:, 6, :], SP[:, 3, :], ALU.mult))
            link(dve.tensor_tensor(SP[:, 6, :], SP[:, 6, :], SP[:, 1, :], ALU.mult))
            link(dve.tensor_tensor(SP[:, 6, :], SP[:, 6, :], SP[:, 7, :], ALU.add))
            link(dve.tensor_scalar(SP[:, 8, :], lru[:, C_LAM:C_LAM + DC], -1.0, 0.0, ALU.mult, ALU.max))
            link(dve.tensor_tensor(SP[:, 8, :], SP[:, 8, :], SP[:, 6, :], ALU.add))
            link(dve.tensor_scalar(SP[:, 9, :], SP[:, 8, :], -8.0, None, ALU.mult))
            def taps(k, c):
                return ((XC[:, c, 0:SEQ], XB[:, c, k:k + SEQ]),
                        (XC[:, c, SEQ:TOK].rearrange("p (b t) -> p b t", b=DB),
                         XB[:, c, HIST + SEQ:XBW].rearrange("p (b t) -> p b t", b=DB)[:, :, k:k + DS]))

            for c in range(DC):
                dve.wait_ge(proj_evac, c + 1)
                for k in range(CONV):
                    w = lru[:, C_W + k * DC + c:C_W + k * DC + c + 1]
                    for dst, src in taps(k, c):
                        if k == 0:
                            ins = dve.tensor_scalar(dst, src, w, lru[:, C_B + c:C_B + c + 1], ALU.mult, ALU.add)
                        else:
                            ins = dve.scalar_tensor_tensor(dst, src, w, dst, ALU.mult, ALU.add)
                    if k < CONV - 1:
                        link(ins)
                ins.then_inc(xc_ready, 1)
            dve.wait_ge(proj_evac, PLAIN["gates"] + DC)
            for c in range(DC):
                ins = dve.tensor_scalar(RG[:, c, :], RG[:, c, :], SP[:, 9, c:c + 1], None, ALU.mult)
            ins.then_inc(z_ready, 1)
            dve.wait_ge(proj_evac, PLAIN["gates"] + 2 * DC)
            dve.wait_ge(xc_ready, DC)
            link(dve.tensor_tensor(IG[:], IG[:], XC[:], ALU.mult))
            dve.wait_ge(at_ready, 1)
            dve.tensor_tensor(T1[:], T1[:], T2[:], ALU.mult).then_inc(m2_ready, 1)
            dve.wait_ge(m_ready, 1)

            def sample_cols(t, off):
                return t[:, :, SEQ:SCW].rearrange("p c (b t) -> p c b t", b=DB)[:, :, :, off:]

            def samples(t):
                return t[:, :, SEQ:TOK].rearrange("p c (b t) -> p c b t", b=DB)

            dve.wait_ge(hist_ready, 1)
            dve.tensor_tensor(LB[:, :, 0:SEQ], T1[:, :, 0:SEQ], IG[:, :, 0:SEQ], ALU.mult)
            link(dve.tensor_tensor(sample_cols(LB, 1), samples(T1), samples(IG), ALU.mult))
            for c in range(DC):
                ins = dve.tensor_tensor_scan(LH[:, c, :], LA[:, c, :], LB[:, c, :], 0.0, ALU.mult, ALU.add)
            link(ins)
            dve.wait_ge(gate_ready, 1)
            dve.tensor_tensor(Y[:, :, 0:SEQ], LH[:, :, 0:SEQ], GATE[:, :, 0:SEQ], ALU.mult)
            dve.tensor_tensor(samples(Y), sample_cols(LH, 1), samples(GATE), ALU.mult).then_inc(y_ready, 1)
            dve.tensor_copy(HS[:, :, 0:1], LH[:, :, SEQ - 1:SEQ])
            dve.tensor_copy(CV[:, :, 0:HIST], XB[:, :, SEQ:SEQ + HIST])
            for c in range(DC):
                dve.tensor_copy(HS[:, c, 1:].unsqueeze(2), sample_cols(LH, DS)[:, c])
                ins = dve.tensor_copy(CV[:, c, HIST:].rearrange("p (b t) -> p b t", b=DB),
                                      XB[:, c, HIST + SEQ:XBW].rearrange("p (b t) -> p b t", b=DB)[:, :, DS:])
            ins.then_inc(st_ready, 1)
            add_to_x("w_out")
            link(dve.memset(RT[:, 0:1], 0.0))
            dve.memset(RV[:, 0:1], 0.0).then_inc(x_ready, 1)
            experts(0)

            ones_for(2)
            inv_rms(2, D)
            scaled(XN, X, G_KV, DC).then_inc(xn_ready, 1)
            dve.wait_ge(mla_in, 16 * MLA_LOADS)
            dve.wait_ge(proj_done, PLAIN["kv"] + 4)
            dve.tensor_tensor(KR[:], ps[2][0:ROPE, 0:TOK], COS[0:ROPE], ALU.mult)
            link(dve.tensor_tensor(KT[:], ps[3][0:ROPE, 0:TOK], SIN[0:ROPE], ALU.mult))
            dve.tensor_tensor(KR[:], KR[:], KT[:], ALU.add).then_inc(kr_ready, 1)
            scaled(XN, X, G_MIX1, DC).then_inc(xn_ready, 1)
            dve.wait_ge(act_step, 2)
            dve.wait_ge(xn_ready, 4)
            dve.wait_ge(kr_ready, 1)
            dve.memset(stat[:, 0, 5:6], 0.0).then_inc(kv_free, 1)
            ones_for(3)
            inv_rms(3, LAT)
            scaled(CT, CR, G_CKV, LC).then_inc(ct_ready, 1)
            dve.memset(stat[:, 0, 6:7], 0.0).then_inc(xn_ready, 1)
            ones_for(4)
            inv_rms(4, QLORA)
            scaled(CQN, CQ, G_Q, QC).then_inc(xn_ready, 1)
            for t in range(4, 8):
                s = t % 4
                dve.wait_ge(proj_done, PLAIN["w_uq"] + t + 1)
                dst, tab = (QRC, COS) if t < 6 else (QRS, SIN)
                g = 2 * (t % 2)
                dve.tensor_tensor(dst[:, g, :], ps[s][:, 0:TOK], tab[:], ALU.mult)
                dve.tensor_tensor(dst[:, g + 1, :], ps[4 + s][:, 0:TOK], tab[:], ALU.mult).then_inc(proj_evac, 1)
            dve.wait_ge(proj_evac, EVAC["w_uq"] + 8)
            dve.tensor_tensor(QRC[:], QRC[:], QRS[:], ALU.add).then_inc(qr_ready, 1)

            dve.wait_ge(ol_ready, 1)
            for m in range(32):
                qb = m // HEADS
                kk = P * (qb + 1)
                st = stat[:, m % 2, :]
                pp = PP[m % 2]
                dve.wait_ge(sc_done, m + 1)
                if m >= 2:
                    dve.wait_ge(pt_done, m - 1)
                if qb:
                    dve.tensor_copy(pp[:, 0:P], ps[m % 2][:, 0:P])
                link(dve.tensor_tensor(pp[:, kk - P:kk], ps[m % 2][:, kk - P:kk], causal[:], ALU.add))
                link(dve.tensor_reduce(st[:, 0:1], pp[:, 0:kk], AX_X, ALU.max))
                dve.tensor_scalar(st[:, 1:2], st[:, 0:1], -SCALE, None, ALU.mult).then_inc(nm_ready, 1)
                dve.wait_ge(p_exp, m + 1)
                link(dve.reciprocal(st[:, 3:4], st[:, 2:3]))
                dve.tensor_scalar(pp[:, 0:kk], pp[:, 0:kk], st[:, 3:4], None, ALU.mult).then_inc(p_ready, 1)
            for b in range(DB):
                bk = 3 * (b % 2)
                st = stat[0:64, b % 2, :]
                p = PS[b % 2]
                dve.wait_ge(sc_done, 32 + b + 1)
                if b >= 2:
                    dve.wait_ge(pt_done, 32 + b - 1)
                else:
                    dve.wait_ge(p_ready, 32)
                link(dve.tensor_tensor(p[:, PAST:], ps[bk + 2][0:64, 0:NSAMP], smask[:, b, :], ALU.add))
                dve.tensor_reduce(st[:, 5:6], ps[bk][0:64, :], AX_X, ALU.max)
                dve.tensor_reduce(st[:, 6:7], ps[bk + 1][0:64, :], AX_X, ALU.max)
                link(dve.tensor_reduce(st[:, 7:8], p[:, PAST:], AX_X, ALU.max))
                link(dve.tensor_reduce(st[:, 0:1], st[:, 5:8], AX_X, ALU.max))
                dve.tensor_scalar(st[:, 1:2], st[:, 0:1], -SCALE, None, ALU.mult).then_inc(nm_ready, 1)
                dve.wait_ge(p_exp, 32 + b + 1)
                link(dve.tensor_reduce(st[:, 5:6], st[:, 2:5], AX_X, ALU.add))
                link(dve.reciprocal(st[:, 6:7], st[:, 5:6]))
                dve.tensor_scalar(p[:], p[:], st[:, 6:7], None, ALU.mult).then_inc(p_ready, 1)
            add_to_x("w_o")
            link(dve.memset(RT[:, 0:1], 0.0))
            dve.memset(RV[:, 0:1], 0.0).then_inc(x_ready, 1)
            experts(1)
            ones_for(6)
            inv_rms(6, D)
            scaled(X, X, G_FIN, DC).then_inc(y_fin, 1)

        @block.gpsimd
        def _(pool):
            link = Steps(pool, pool_step)
            pool.wait_ge(lru_in, 16 * 4)
            pool.memset(XB[:, :, 0:HIST], 0.0)
            for c in range(DC):
                pool.tensor_copy(XB[:, c, HIST + SEQ:XBW].rearrange("p (b t) -> p b t", b=DB)[:, :, 0:HIST],
                                 hist[:, c])
                pool.memset(LA[:, c, SEQ:SCW].rearrange("p (b t) -> p b t", b=DB)[:, :, 0:1], 0.0)
                ins = pool.tensor_copy(LB[:, c, SEQ:SCW].rearrange("p (b t) -> p b t", b=DB)[:, :, 0:1],
                                       h0[:, c, :].unsqueeze(2))
            ins.then_inc(hist_ready, 1)
            for l in range(2):
                if l == 1:
                    pool.wait_ge(proj_evac, EVAC["q_lat"] + 32)
                    pool.wait_ge(qr_in, 16 * 4)
                    for c in range(LC):
                        pool.tensor_copy(QLS[:, c].rearrange("p b (h t) -> p h b t", t=DS),
                                         QL[:, c, :, SEQ:TOK].rearrange("p h (b t) -> p h b t", t=DS))
                    pool.tensor_copy(QRP[:].rearrange("p b (h t) -> p h b t", t=DS),
                                     QR[:, :, SEQ:TOK].rearrange("p h (b t) -> p h b t", t=DS)).then_inc(qs_ready, 1)
                with pool.Fori(0, P // SLOTS) as i:
                    for k in range(2 * SLOTS):
                        half = slice((k % 2) * HALF, (k % 2 + 1) * HALF)
                        pool.wait_ge(hi_ready, i * (2 * SLOTS) + 512 * l + k + 1)
                        pool.tensor_tensor(lo[k % 4][:], raw[k // 2][:, half], hi[k % 4][:].bitcast(F32), ALU.subtract)\
                            .then_inc(lo_ready, 1)
                pool.wait_ge(gt_ready, l + 1)

                def difference(i, u):
                    if not (isinstance(i, int) and 72 * l + u - 1 <= 0):
                        pool.wait_ge(g_done, i * 4 + 72 * l + u - 1)
                    pool.tensor_tensor(ohi[u % 2][:], iota[:].unsqueeze(1).broadcast_to([P, 4, P]),
                                       IT[:, bass.ds(i * 16 + 4 * u, 4)].unsqueeze(2).broadcast_to([P, 4, P]),
                                       ALU.subtract).then_inc(dif_ready, 1)

                for u in range(4):
                    difference(0, u)
                with pool.Fori(1, TOK // 16) as i:
                    for u in range(4):
                        difference(i, u)


MLA_LOADS = 7
V_OUT = [[(c, 0, 0, TOK, True)] for c in range(7)] + \
        [[(6, TOK, 0, 512 - TOK, False), (7, 0, 512 - TOK, TOK, True)]]


def shape_constants():
    f = np.float32
    half = ROPE // 2
    inv = np.power(f(10000.0), -np.arange(half, dtype=f) / f(half)).astype(f)
    pos = np.concatenate([np.arange(SEQ), np.tile(PAST + np.arange(DS), DB)]).astype(f)
    ang = inv[:, None] * pos[None, :]
    cos = np.tile(np.cos(ang), (P // half, 1)).astype(f)
    sin = np.tile(np.concatenate([-np.sin(ang), np.sin(ang)]), (P // ROPE, 1)).astype(f)
    q, k = np.arange(P)[:, None], np.arange(P)[None, :]
    causal = np.where(k <= q, 0.0, NEG).astype(f)
    t = np.tile(np.arange(DS), HEADS)[:, None, None]
    b = np.arange(DB)[None, :, None]
    kb, kt = (np.arange(NSAMP) // DS)[None, None, :], (np.arange(NSAMP) % DS)[None, None, :]
    smask = np.where((kb == b) & (kt <= t), 0.0, NEG).astype(f)
    return {"cos": cos, "sin": sin, "causal": causal, "smask": smask, "ident": np.eye(P, dtype=f),
            "blk": (q // TOPK == k // TOPK).astype(f), "iota": np.tile(np.arange(P, dtype=f), (P, 1))}


def kernel(**inputs):
    import concourse.bacc as _bacc
    from concourse.bass_utils import run_bass_kernel_spmd as _run

    x = {k: np.asarray(v) for k, v in inputs.items()}
    f = np.float32

    def cols(v):
        return v.reshape(-1, P).T

    def tiles(w):
        k, m = w.shape
        return w.reshape(k // P, P, m // P, P).transpose(2, 1, 0, 3).reshape(m // P, P, k)

    def features(a3):
        return a3.reshape(a3.shape[0], -1, P).transpose(2, 1, 0)

    stream = np.zeros((NTILES, P, TILE), f)

    def put(phase, t):
        stream[FIRST[phase]:FIRST[phase] + len(t), :, :t.shape[2]] = t

    t = tiles(x["lru_w_in"][0])
    put("w_gate", t[:DC])
    put("w_x", t[DC:])
    put("w_out", tiles(x["lru_w_out"][0]))
    for l in range(2):
        put(f"wq{l}", tiles(x["peer_w_q"][l]))
        u = x["peer_u"][l].reshape(P, P, DC, P)
        for j in range(P):
            stream[FIRST[f"u{l}"] + j] = u[:, j].transpose(2, 1, 0).reshape(P, TILE)
        put(f"v{l}", x["peer_v"][l].reshape(P, P, D).transpose(1, 0, 2))
    swap = np.concatenate([np.arange(ROPE // 2, ROPE), np.arange(ROPE // 2)])
    put("kv", tiles(x["w_dkv"]))
    for s, w in ((2, x["w_kr"]), (3, x["w_kr"][:, swap])):
        stream[FIRST["kv"] + s, :, :DC * ROPE] = w.reshape(DC, P, ROPE).transpose(1, 0, 2).reshape(P, -1)
    put("w_dq", tiles(x["mla_w_dq"][0]))
    uq = x["mla_w_uq"][0].reshape(QLORA, HEADS, NOPE + ROPE)
    parts = [tiles(np.ascontiguousarray(w).reshape(QLORA, -1)) for w in
             (uq[:, :, :NOPE], uq[:, :, NOPE:], uq[:, :, NOPE:][:, :, swap])]
    t = np.concatenate(parts)
    put("w_uq", t.reshape(8, 2, P, QLORA).transpose(0, 2, 1, 3).reshape(8, P, 2 * QLORA))
    put("w_o", tiles(x["mla_w_o"][0]))

    xs = x["x_sample"].reshape(NSAMP, D)
    arrays = {
        "stream": stream,
        "x": features(np.concatenate([x["x_prompt"][0], xs])),
        "gains": np.concatenate([cols(x["ln_mix"][0]), cols(x["ln_ffn"][0]), cols(x["ln_mix"][1]),
                                 cols(x["ln_ffn"][1]), cols(x["ln_final"]), cols(x["kv_norm"]),
                                 cols(x["ckv_norm"]), cols(x["mla_q_norm"][0])], axis=1),
        "lru": np.concatenate([cols(x["lru_conv_w"][0].reshape(-1)), cols(x["lru_conv_b"][0]),
                               cols(x["lru_gate_a_b"][0]), cols(x["lru_gate_x_b"][0]), cols(x["lru_lambda"][0])], axis=1),
        "hist": x["state_conv"][:, 0].reshape(DB, HIST, DC, P).transpose(3, 2, 0, 1),
        "h0": x["state_h"][:, 0].reshape(DB, DC, P).transpose(2, 1, 0),
        "wg": np.concatenate([x["lru_gate_a_w"][0], x["lru_gate_x_w"][0]]).transpose(1, 0, 2),
        "sk": x["peer_subkeys"].reshape(2, 2 * PH, KEYS, P).transpose(0, 3, 1, 2),
        "wuk": x["w_uk"].reshape(LAT, HEADS // 2, 2 * NOPE).transpose(2, 1, 0),
        "wuv": x["w_uv"].reshape(LC, P, HEADS * VH).transpose(1, 0, 2),
        "pool": np.concatenate([
            x["cache_ckv"], x["cache_ckv"].reshape(NPOOL, PAGE, LC, P).transpose(0, 3, 2, 1).reshape(NPOOL, P, LC * PAGE),
            np.pad(x["cache_krope"].transpose(0, 2, 1), ((0, 0), (0, P - ROPE), (0, 0)))], axis=2),
        "pages": x["page_table"].reshape(1, -1).astype(np.int32),
        **shape_constants(),
    }
    arrays = {k: np.ascontiguousarray(v) for k, v in arrays.items()}
    outs = {"y": (P, DC, TOK), "h": (P, DC, 1 + DB), "conv": (P, DC, (1 + DB) * HIST),
            "ckv": (P, LC, TOK), "kr": (ROPE, TOK)}

    nc = _bacc.Bacc("TRN2", target_bir_lowering=False, num_devices=1)
    a = {k: nc.dram_tensor(f"in_{k}", v.shape, mybir.dt.from_np(v.dtype), kind="ExternalInput").ap()
         for k, v in arrays.items()}
    o = {k: nc.dram_tensor(f"out_{k}", s, F32, kind="ExternalOutput").ap() for k, s in outs.items()}
    build(nc, a, o)
    r = _run(nc, [{f"in_{k}": v for k, v in arrays.items()}], core_ids=[0]).results[0]

    def tokens(t):
        return t.transpose(2, 1, 0).reshape(t.shape[2], -1)

    y, ckv, kr = tokens(r["out_y"]), tokens(r["out_ckv"]), r["out_kr"].T
    h = r["out_h"].transpose(2, 1, 0).reshape(1 + DB, D)
    conv = r["out_conv"].reshape(P, DC, 1 + DB, HIST).transpose(2, 3, 1, 0).reshape(1 + DB, HIST, D)
    c = np.ascontiguousarray
    return (c(y[None, :SEQ]), c(y[SEQ:].reshape(DB, DS, D)), c(h[None, :1]), c(conv[None, :1]),
            c(ckv[None, :SEQ]), c(kr[None, :SEQ]), c(h[1:, None]), c(conv[1:, None]),
            c(ckv[SEQ:].reshape(DB, DS, LAT)), c(kr[SEQ:].reshape(DB, DS, ROPE)))
```

```python
from contextlib import ExitStack

import numpy as np

import concourse.bass as bass
from concourse import mybir

F32 = mybir.dt.float32
F32R = mybir.dt.float32r
U32 = mybir.dt.uint32
I32 = mybir.dt.int32
ALU = mybir.AluOpType
ACT = mybir.ActivationFunctionType
AX_X = mybir.AxisListType.X

P = 128
D = 1024
DC = D // P
SEQ, DB, DS = 256, 8, 4
NSAMP = DB * DS
TOK = SEQ + NSAMP
PAST, PAGE = 1024, 128
NPAGES = PAST // PAGE
NPOOL = 80
CONV = 4
HIST = CONV - 1
HEADS, NOPE, ROPE, VH = 16, 64, 32, 64
LAT, QLORA = 256, 512
LC, QC = LAT // P, QLORA // P
SCALE = float(NOPE + ROPE) ** -0.5
PH, KEYS, TOPK = 8, 128, 16
EPS = 1e-6
NEG = -1e30
LOWEST = -3.0e38
BLOCKS = [(0, 128), (128, 128), (256, NSAMP)]

NG = TOK // 16

SLOTS = 4
TILE = 1024
HALF = TILE // 2
PHASES = [("w_x", 8), ("w_gate", 8), ("w_out", 8), ("wq0", 16), ("u0", 128), ("v0", 128),
          ("kv", 4), ("w_dq", 4), ("w_uq", 8), ("w_o", 8), ("wq1", 16), ("u1", 128), ("v1", 128)]
FIRST = {}
NTILES = 0
for _name, _n in PHASES:
    FIRST[_name] = NTILES
    NTILES += _n
COUNT = dict(PHASES)

XBW = HIST + SEQ + DB * (HIST + DS)
SCW = SEQ + DB * (1 + DS)

G_MIX0, G_FFN0, G_MIX1, G_FFN1, G_FIN, G_KV, G_CKV, G_Q = 0, 8, 16, 24, 32, 40, 48, 50
NGAIN = 54
C_W, C_B, C_GA, C_GX, C_LAM = 0, 32, 40, 48, 56
NLRU = 64


class Steps:

    def __init__(self, eng, sem):
        self.eng, self.sem, self.n = eng, sem, 0

    def __call__(self, ins):
        self.n += 1
        ins.then_inc(self.sem, 1)
        self.eng.wait_ge(self.sem, self.n)


def build(nc, a, o):
    with ExitStack() as ctx:
        BASE = (nc.sbuf_base + 63) // 64 * 64
        HBW = P * TOK
        R0, RAW, HL = HBW, HBW + 4608, HBW + 4608 + SLOTS * TILE
        KON = HL + 4 * TILE

        def at(name, word, shape, dt=F32):
            return nc.alloc_sbuf_tensor_at(name, shape, dt, offset=BASE + 4 * word)

        def sem(name):
            return ctx.enter_context(nc.semaphore(name))

        raw = [at(f"raw{s}", RAW + s * TILE, [P, TILE]) for s in range(SLOTS)]
        hi = [at(f"hi{s}", HL + s * TILE, [P, HALF], F32R) for s in range(4)]
        lo = [at(f"lo{s}", HL + s * TILE + HALF, [P, HALF], F32R) for s in range(4)]
        X = at("X", KON, [P, DC, TOK])
        E = at("E", KON + 2304, [P, 3, P])
        CM = at("CM", KON + 2688, [P, 3, P])
        ident = at("ident", KON + 3072, [P, P])
        blk = at("blk", KON + 3200, [P, P])
        iota = at("iota", KON + 3328, [P, P])
        gains = at("gains", KON + 3456, [P, NGAIN])
        assert BASE + 4 * (KON + 3456 + NGAIN) <= nc.sbuf_usable_end

        SQ = at("SQ", HL, [P, DC, TOK])
        ones = at("ones", HL + 2304, [P, P])
        RT = at("RT", HL + 2432, [P, TOK])
        RV = at("RV", HL + 2720, [P, TOK])
        XN = at("XN", 25600, [P, DC, TOK])

        XB = at("XB", 0, [P, DC, XBW])
        XC = at("XC", 2560, [P, DC, TOK])
        GATE = at("GATE", 4864, [P, DC, TOK])
        RG = at("RG", 7168, [P, DC, TOK])
        IG = at("IG", 9536, [P, DC, TOK])
        LA = at("LA", 11840, [P, DC, SCW])
        LB = at("LB", 14208, [P, DC, SCW])
        LH = at("LH", 16576, [P, DC, SCW])
        Y = at("Y", 18944, [P, DC, TOK])
        T1 = at("T1", 21248, [P, DC, TOK])
        T2 = at("T2", 16576, [P, DC, TOK])
        wg = at("wg", 23552, [P, 2 * DC, P])
        hist = at("hist", 27904, [P, DC, DB, HIST])
        h0 = at("h0", 28096, [P, DC, DB])
        lru = at("lru", 28160, [P, NLRU])
        SP = at("SP", 28224, [P, 10, DC])
        HS = at("HS", 28352, [P, DC, 1 + DB])
        CV = at("CV", 28480, [P, DC, (1 + DB) * HIST])

        HB = at("HB", 0, [P, P, TOK])
        XH = at("XH", R0, [P, DC, TOK], F32R)
        XL = at("XL", R0 + 2304, [P, DC, TOK], F32R)
        XP = at("XP", 15840, [P, DC, TOK])
        QT = at("QT", 18144, [P, 2 * PH, TOK])
        SK = at("SK", 22752, [P, 2 * PH, KEYS])
        FREE_Q = 15840 // TOK
        S = at("S", 24800, [P, 3, 2 * PH, KEYS])
        FREE_S = 24800 // TOK
        W0 = 24800 + 6144
        V16 = at("V16", W0, [P, 2 * PH, TOPK])
        I16 = at("I16", W0 + 256, [P, 2 * PH, TOPK], U32)
        IF = at("IF", W0 + 512, [P, 2 * PH, TOPK])
        CAND = at("CAND", W0 + 768, [P, PH, TOPK, TOPK])
        CS = at("CS", W0 + 2816, [P, PH, TOPK])
        CP = at("CP", W0 + 2944, [P, PH, TOPK], U32)
        CA = at("CA", W0 + 3072, [P, 2, PH * TOPK], U32)
        CF = at("CF", W0 + 3328, [P, 2, PH * TOPK])
        EE = at("EE", W0 + 3584, [P, 2, PH * TOPK])
        IT = at("IT", R0, [P, TOK])
        JT = at("JT", R0 + 288, [P, TOK])
        GT = at("GT", R0 + 576, [P, TOK])
        EU = at("EU", R0 + 864, [P, TOK], U32)
        IU = at("IU", R0 + 1152, [P, TOK], U32)
        JU = at("JU", R0 + 1440, [P, TOK], U32)
        EX = at("EX", R0 + 1728, [P, TOK])
        ohi = [at(f"ohi{b}", HL + 512 * b, [P, 4, P]) for b in range(4)]
        ohj = [at(f"ohj{b}", HL + 2048 + 512 * b, [P, 4, P]) for b in range(2)]
        GS = at("GS", HL + 3072, [P, 4, P])
        WH = [at(f"WH{b}", R0 + 288 * b, [P, TOK], F32R) for b in range(2)]
        WL = [at(f"WL{b}", R0 + 576 + 288 * b, [P, TOK], F32R) for b in range(2)]

        QL = at("QL", 0, [P, LC, HEADS, TOK])
        QR = at("QR", 9216, [ROPE, HEADS, TOK])
        CT = at("CT", 13824, [P, LC, TOK])
        KR = at("KR", 14400, [ROPE, TOK])
        KT = at("KT", 14688, [ROPE, TOK])
        CN = at("CN", 14976, [P, 3, LAT])
        QN = at("QN", 15744, [P, HEADS // 2, TOK])
        QRC = at("QRC", 18048, [P, 4, TOK])
        QRS = at("QRS", 19200, [P, 4, TOK])
        CQ = at("CQ", 20352, [P, QC, TOK])
        CQN = at("CQN", 21504, [P, QC, TOK])
        wuk = at("wuk", 22656, [P, HEADS // 2, LAT])
        OL = at("OL", 15744, [P, LC, HEADS, TOK])
        stat = at("stat", 24960, [P, 2, 8])
        smask = at("smask", 25024, [HEADS * DS, DB, NSAMP])
        CR = at("CR", 30000, [P, LC, TOK])
        QLS = at("QLS", 25600, [P, LC, DB, HEADS * DS])
        QRP = at("QRP", 26624, [ROPE, DB, HEADS * DS])
        AO = at("AO", 25600, [P, DC, TOK])
        wuv = at("wuv", 27904, [P, LC, HEADS * VH])
        PP = [at(f"PP{b}", 29952 + 256 * b, [P, SEQ]) for b in range(2)]
        PT = [at(f"PT{b}", 30464 + 256 * b, [P, 2, P]) for b in range(2)]
        PTS = at("PTS", 29952, [P, NPAGES + 1, HEADS * DS])
        PS = [at(f"PS{b}", HL + 1024 + 1088 * b, [HEADS * DS, PAST + NSAMP]) for b in range(2)]
        OS = at("OS", HL, [HEADS * DS, LAT])
        PKW = LAT + PAGE
        plat = [at(f"plat{b}", 30976 + b * NPAGES * LAT, [P, NPAGES, LAT]) for b in range(2)]
        pkeys = [at(f"pkeys{b}", 30976 + NPAGES * (2 * LAT + b * PKW), [P, NPAGES, PKW]) for b in range(2)]
        COS = at("COS", KON + 2304, [P, TOK])
        SIN = at("SIN", KON + 2592, [P, TOK])
        causal = at("causal", KON + 2880, [P, P])
        pages = at("pages", 25280, [1, DB * NPAGES], I32)

        ps = [ctx.enter_context(nc.psum_tensor(f"ps{b}", [P, 512], F32)) for b in range(8)]

        raw_full = [sem(f"raw_full{s}") for s in range(SLOTS)]
        x_in, const_in, lru_in, sk_in, mla_in, out_dma = map(sem, (
            "x_in", "const_in", "lru_in", "sk_in", "mla_in", "out_dma"))
        keys_in = [sem("keys_in0"), sem("keys_in1")]
        lat_in = [sem("lat_in0"), sem("lat_in1")]
        os_ready = sem("os_ready")
        proj_done, proj_evac = sem("proj_done"), sem("proj_evac")
        sq_ready, ones_ready, ss_done, ms_ready, sqrt_ready, xn_ready, x_ready = map(sem, (
            "sq_ready", "ones_ready", "ss_done", "ms_ready", "sqrt_ready", "xn_ready", "x_ready"))
        act_step, dve_step, pool_step = sem("act_step"), sem("dve_step"), sem("pool_step")
        sp_act, sp_dve = sem("sp_act"), sem("sp_dve")
        hist_ready, xc_ready, z_ready, at_ready, m2_ready, m_ready, y_ready, st_ready = map(sem, (
            "hist_ready", "xc_ready", "z_ready", "at_ready", "m2_ready", "m_ready", "y_ready", "st_ready"))
        s_done, s_evac, xh_ready, xl_ready = map(sem, ("s_done", "s_evac", "xh_ready", "xl_ready"))
        hi_ready, lo_ready, mm_done, h_evac = map(sem, ("hi_ready", "lo_ready", "mm_done", "h_evac"))
        topk_done, tr_done, ex_ready, bs_done, ij_ready, gt_ready = map(sem, (
            "topk_done", "tr_done", "ex_ready", "bs_done", "ij_ready", "gt_ready"))
        g_copied, g_pool = sem("g_copied"), sem("g_pool")
        dif_ready, dif_sq, ohi_ready, ohj_ready, g_done, g_used = map(sem, (
            "dif_ready", "dif_sq", "ohi_ready", "ohj_ready", "g_done", "g_used"))
        kr_ready, ct_ready, cnt_done, cn_ready, qr_ready, qr_in = map(sem, (
            "kr_ready", "ct_ready", "cnt_done", "cn_ready", "qr_ready", "qr_in"))
        sc_done, nm_ready, p_exp, p_ready, pt_done, pt_ready, pv_done, ol_ready = map(sem, (
            "sc_done", "nm_ready", "p_exp", "p_ready", "pt_done", "pt_ready", "pv_done", "ol_ready"))
        gate_ready = sem("gate_ready")
        y_fin, qs_ready, kv_free = sem("y_fin"), sem("qs_ready"), sem("kv_free")

        PLAIN, EVAC = {}, {}
        n = 0
        for name, k in [("w_x", 8), ("gates", 16), ("w_gate", 8), ("w_out", 8), ("wq0", 16), ("kv", 4), ("w_dq", 4),
                        ("w_uq", 8), ("q_lat", 32), ("v_up", 8), ("w_o", 8), ("wq1", 16)]:
            PLAIN[name] = n
            EVAC[name] = n if n <= PLAIN["kv" if "kv" in PLAIN else name] else n - 4
            n += k

        def last_use(phase, k):
            if phase[0] in "uv":
                return lo_ready, 512 * int(phase[1]) + (0 if phase[0] == "u" else 256) + 2 * k + 2
            return proj_done, PLAIN[phase] + k + 1

        block = ctx.enter_context(nc.Block())

        @block.sync
        def _(sp):
            sp.dma_start(X[:], a["x"]).then_inc(x_in, 16)

            def load(t, s):
                src = a["stream"][t] if isinstance(t, int) else \
                    a["stream"][bass.ds(t, 1)].rearrange("a p f -> (a p) f")
                sp.dma_start(raw[s][:], src).then_inc(raw_full[s], 16)

            before = None
            for phase, count in PHASES:
                t0 = FIRST[phase]
                if phase == "w_o":
                    sp.wait_ge(mla_in, 16 * MLA_LOADS)
                    sp.wait_ge(ol_ready, 1)

                    def load_pages(numbers, dst, cols, loaded):
                        for j, pg in enumerate(numbers):
                            sp.dma_start(dst[:, j, :], a["pool"][bass.ds(pg, 1), :, cols].rearrange("a p f -> (a p) f"))\
                                .then_inc(loaded, 16)

                    for b in range(DB):
                        numbers = [sp.value_load(pages[0:1, n:n + 1], min_val=0, max_val=NPOOL - 1)
                                   for n in range(b * NPAGES, (b + 1) * NPAGES)]
                        if b >= 2:
                            sp.wait_ge(sc_done, 32 + b - 1)
                        load_pages(numbers, pkeys[b % 2], slice(LAT, LAT + PKW), keys_in[b % 2])
                        if b >= 2:
                            sp.wait_ge(pv_done, 32 + b - 1)
                        load_pages(numbers, plat[b % 2], slice(0, LAT), lat_in[b % 2])
                for s in range(SLOTS):
                    if before:
                        sp.wait_ge(*last_use(before, COUNT[before] - SLOTS + s))
                    load(t0 + s, s)
                if count > SLOTS:
                    with sp.Fori(1, count // SLOTS) as i:
                        for s in range(SLOTS):
                            used, value = last_use(phase, s - SLOTS)
                            rate = 2 if phase[0] in "uv" else 1
                            sp.wait_ge(used, i * (SLOTS * rate) + value)
                            load(i * SLOTS + t0 + s, s)
                before = phase
            sp.wait_ge(y_fin, 1)
            sp.dma_start(o["y"], X[:]).then_inc(out_dma, 16)
            sp.wait_ge(out_dma, 16 * 5)

        @block.tensor
        def _(pe):
            def full(phase, i, s):
                pe.wait_ge(raw_full[s], i * 16 + 16 * (FIRST[phase] // SLOTS + 1))

            def norm(k, chunks):
                pe.wait_ge(ones_ready, k + 1)
                for c in range(chunks):
                    pe.wait_ge(sq_ready, N_BEFORE[k] + c + 1)
                    mm = pe.matmul(ps[7][:, 0:TOK], ones[:], SQ[:, c, :], start=c == 0, stop=c == chunks - 1)
                mm.then_inc(ss_done, 1)

            def project(phase, xin, chunks=DC, come=None):
                def tile(i, s):
                    full(phase, i, s)
                    p = EVAC[phase] + s
                    if not isinstance(i, int) or i * SLOTS + p - 3 > 0:
                        pe.wait_ge(proj_evac, i * SLOTS + p - 3)
                    for c in range(chunks):
                        if come is not None and isinstance(i, int) and s == 0:
                            pe.wait_ge(xn_ready, come + c + 1)
                        mm = pe.matmul(ps[s][:, 0:TOK], raw[s][:, c * P:(c + 1) * P], xin[:, c, :],
                                       start=c == 0, stop=c == chunks - 1)
                    mm.then_inc(proj_done, 1)

                for s in range(SLOTS):
                    tile(0, s)
                if COUNT[phase] > SLOTS:
                    with pe.Fori(1, COUNT[phase] // SLOTS) as i:
                        for s in range(SLOTS):
                            tile(i, s)

            def experts(l):
                kn = (1, 5)[l]
                norm(kn, DC)
                project(f"wq{l}", XP, come=(XN_FFN0, XN_FFN1)[l])
                pe.wait_ge(proj_evac, EVAC[f"wq{l}"] + 16)
                pe.wait_ge(sk_in, 16 * (l + 1))
                for nb, (n0, rows) in enumerate(BLOCKS):
                    for g in range(4):
                        k = 12 * l + 4 * nb + g
                        if k >= 4:
                            pe.wait_ge(s_evac, k - 3)
                        for q in range(4):
                            hp = 4 * g + q
                            mm = pe.matmul(ps[4 + g][0:rows, q * KEYS:(q + 1) * KEYS], QT[:, hp, n0:n0 + rows],
                                           SK[:, hp, :], start=True, stop=True)
                        mm.then_inc(s_done, 1)
                pe.wait_ge(xl_ready, l + 1)

                def h_tile(i, s):
                    if not isinstance(i, int) or 128 * l + s - 3 > 0:
                        pe.wait_ge(h_evac, i * SLOTS + 128 * l + s - 3)
                    for half in range(2):
                        k = 2 * s + half
                        pe.wait_ge(lo_ready, i * (2 * SLOTS) + 512 * l + k + 1)
                        for c in range(4 * half, 4 * half + 4):
                            w = slice((c % 4) * P, (c % 4 + 1) * P)
                            h, r = hi[k % 4][:, w], lo[k % 4][:, w]
                            pe.matmul(ps[s][:, 0:TOK], h, XH[:, c, :], start=c == 0, stop=False)
                            pe.matmul(ps[s][:, 0:TOK], h, XL[:, c, :], start=False, stop=False)
                            mm = pe.matmul(ps[s][:, 0:TOK], r, XH[:, c, :], start=False, stop=c == DC - 1)
                        mm.then_inc(mm_done, 1)

                for s in range(SLOTS):
                    h_tile(0, s)
                with pe.Fori(1, P // SLOTS) as i:
                    for s in range(SLOTS):
                        h_tile(i, s)
                pe.wait_ge(topk_done, 3 * (l + 1))
                for bank, src in ((4, E), (5, CM)):
                    for nb, (n0, rows) in enumerate(BLOCKS):
                        mm = pe.transpose(ps[bank][:, n0:n0 + rows], src[0:rows, nb, :], ident[0:rows, 0:rows])
                    mm.then_inc(tr_done, 1)
                pe.wait_ge(ex_ready, l + 1)
                pe.matmul(ps[6][:, 0:TOK], blk[:], EX[:], start=True, stop=True).then_inc(bs_done, 1)
                pe.wait_ge(gt_ready, l + 1)

                def g_batch(i, u):
                    pe.wait_ge(ohi_ready, i * 4 + 4 * NG * l + u + 1)
                    pe.wait_ge(ohj_ready, i * 4 + 4 * NG * l + u + 1)
                    if u == 3:
                        if not isinstance(i, int) or l:
                            pe.wait_ge(g_copied, i + NG * l)
                    elif not isinstance(i, int) or l:
                        pe.wait_ge(g_used, i * 3 + 3 * NG * l + u - 2)
                    for t in range(4):
                        mm = pe.matmul(ps[u][:, t * P:(t + 1) * P], ohi[u][:, t, :], ohj[u % 2][:, t, :],
                                       start=True, stop=True)
                    mm.then_inc(g_done, 1)

                for u in range(4):
                    g_batch(0, u)
                with pe.Fori(1, NG) as i:
                    for u in range(4):
                        g_batch(i, u)

                def v_tile(i, s, first, last):
                    for half in range(2):
                        k = 2 * s + half
                        pe.wait_ge(lo_ready, i * (2 * SLOTS) + 512 * l + 256 + k + 1)
                        for c in range(4 * half, 4 * half + 4):
                            w = slice((c % 4) * P, (c % 4 + 1) * P)
                            for n, (x, y) in enumerate(((hi, WH), (hi, WL), (lo, WH))):
                                mm = pe.matmul(ps[c][:, 0:TOK], x[k % 4][:, w], y[s % 2][:],
                                               start=first and n == 0, stop=last and n == 2, skip_group_check=True)
                        mm.then_inc(mm_done, 1)

                for s in range(SLOTS):
                    v_tile(0, s, s == 0, False)
                with pe.Fori(1, P // SLOTS - 1) as i:
                    for s in range(SLOTS):
                        v_tile(i, s, False, False)
                for s in range(SLOTS):
                    v_tile(P // SLOTS - 1, s, False, s == SLOTS - 1)

            pe.wait_ge(const_in, 16 * 4)
            norm(0, DC)
            project("w_x", XN, come=XN_MIX0)
            pe.wait_ge(lru_in, 16 * 4)
            for k in range(16):
                p = PLAIN["gates"] + k
                pe.wait_ge(proj_evac, p - 3)
                pe.wait_ge(xc_ready, min(k, DC - 1) + 1)
                pe.matmul(ps[p % 4][:, 0:TOK], wg[:, k, :], XC[:, k % DC, :], start=True, stop=True)\
                    .then_inc(proj_done, 1)
            project("w_gate", XN)
            pe.wait_ge(y_ready, 1)
            project("w_out", Y)
            experts(0)

            norm(2, DC)
            for s in range(4):
                full("kv", 0, s)
                m = P if s < LC else ROPE
                for c in range(DC):
                    pe.wait_ge(xn_ready, XN_KV + c + 1)
                    mm = pe.matmul(ps[s][0:m, 0:TOK], raw[s][:, c * m:(c + 1) * m], XN[:, c, :],
                                   start=c == 0, stop=c == DC - 1)
                mm.then_inc(proj_done, 1)
            norm(3, LC)
            pe.wait_ge(kv_free, 1)
            project("w_dq", XN, come=XN_MIX1)
            pe.wait_ge(ct_ready, 1)
            for nb, (n0, rows) in enumerate(BLOCKS):
                for c in range(LC):
                    mm = pe.transpose(ps[4 + nb][0:rows, c * P:(c + 1) * P], CT[:, c, n0:n0 + rows], ident[:])
            mm.then_inc(cnt_done, 1)
            norm(4, QC)
            pe.wait_ge(xn_ready, XN_Q + QC)
            pe.wait_ge(cn_ready, 1)
            for t in range(8):
                i, s = divmod(t, SLOTS)
                full("w_uq", i, s)
                pe.wait_ge(proj_evac, EVAC["w_uq"] + (t - 3 if t < 4 else 4))
                for half in range(2):
                    for c in range(QC):
                        mm = pe.matmul(ps[s + 4 * half][:, 0:TOK], raw[s][:, (half * QC + c) * P:(half * QC + c + 1) * P],
                                       CQN[:, c, :], start=c == 0, stop=c == QC - 1)
                mm.then_inc(proj_done, 1)
            pe.wait_ge(mla_in, 16 * MLA_LOADS)
            for h in range(HEADS):
                for c in range(LC):
                    p = PLAIN["q_lat"] + LC * h + c
                    k = EVAC["q_lat"] + LC * h + c
                    pe.wait_ge(proj_evac, k if k == EVAC["q_lat"] else k - 3)
                    r = slice(NOPE * (h % 2), NOPE * (h % 2) + NOPE)
                    pe.matmul(ps[p % 4][:, 0:TOK], wuk[r, h // 2, c * P:(c + 1) * P], QN[r, h // 2, :],
                              start=True, stop=True).then_inc(proj_done, 1)
            pe.wait_ge(proj_evac, EVAC["q_lat"] + 32)
            pe.wait_ge(qr_in, 16 * 4)

            def p_scores(m):
                qb, h = divmod(m, HEADS)
                q = slice(qb * P, qb * P + P)
                kk = P * (qb + 1)
                out = ps[m % 2][:, 0:kk]
                if m >= 2:
                    pe.wait_ge(nm_ready, m - 1)
                for c in range(LC):
                    pe.matmul(out, QL[:, c, h, q], CT[:, c, 0:kk], start=c == 0, stop=False)
                pe.matmul(out, QR[:, h, q], KR[:, 0:kk], start=False, stop=True).then_inc(sc_done, 1)

            def p_turn(m):
                qb = m // HEADS
                pe.wait_ge(p_ready, m + 1)
                if m >= 2:
                    pe.wait_ge(pt_ready, m - 1)
                for kb in range(qb + 1):
                    mm = pe.transpose(ps[2 + m % 2][:, kb * P:(kb + 1) * P], PP[m % 2][:, kb * P:(kb + 1) * P], ident[:])
                mm.then_inc(pt_done, 1)

            def p_values(m):
                qb = m // HEADS
                pe.wait_ge(pt_ready, m + 1)
                if m >= 2:
                    pe.wait_ge(ol_ready, m)
                for c in range(LC):
                    for kb in range(qb + 1):
                        mm = pe.matmul(ps[4 + m % 2][:, c * P:(c + 1) * P], CN[:, kb, c * P:(c + 1) * P],
                                       PT[m % 2][:, kb, :], start=kb == 0, stop=kb == qb)
                mm.then_inc(pv_done, 1)

            for m in range(32 + 2):
                if m < 32:
                    p_scores(m)
                if 1 <= m <= 32:
                    p_turn(m - 1)
                if m >= 2:
                    p_values(m - 2)

            pe.wait_ge(qs_ready, 1)

            def s_scores(b):
                bk = 3 * (b % 2)
                pe.wait_ge(keys_in[b % 2], 16 * NPAGES * (b // 2 + 1))
                if b >= 2:
                    pe.wait_ge(p_exp, 32 + b - 1)
                else:
                    pe.wait_ge(ol_ready, 33)
                q = [QLS[:, c, b, :] for c in range(LC)] + [QRP[:, b, :]]
                for half in range(2):
                    pg = slice(4 * half, 4 * half + 4)
                    keys = [pkeys[b % 2][:, pg, c * PAGE:(c + 1) * PAGE] for c in range(LC)]
                    keys.append(pkeys[b % 2][0:ROPE, pg, LAT:])
                    for k in range(3):
                        pe.matmul(ps[bk + half][0:64, :], q[k], keys[k], start=k == 0, stop=k == 2)
                keys = [CT[:, c, SEQ:TOK] for c in range(LC)] + [KR[:, SEQ:TOK]]
                for k in range(3):
                    mm = pe.matmul(ps[bk + 2][0:64, 0:NSAMP], q[k], keys[k], start=k == 0, stop=k == 2)
                mm.then_inc(sc_done, 1)

            def s_turn(b):
                if b >= 1:
                    pe.wait_ge(os_ready, b)
                    for c in range(LC):
                        mm = pe.transpose(ps[7][:, LAT + 64 * c:LAT + 64 * c + 64], OS[:, c * P:(c + 1) * P],
                                          ident[0:64, 0:64])
                if b < DB:
                    pe.wait_ge(p_ready, 32 + b + 1)
                    for j in range(NPAGES):
                        pe.transpose(ps[6][:, 64 * j:64 * j + 64], PS[b % 2][:, j * P:(j + 1) * P], ident[0:64, 0:64])
                    mm = pe.transpose(ps[7][0:NSAMP, 448:512], PS[b % 2][:, PAST:PAST + NSAMP], ident[0:64, 0:64])
                mm.then_inc(pt_done, 1)

            def s_values(b):
                pe.wait_ge(lat_in[b % 2], 16 * NPAGES * (b // 2 + 1))
                pe.wait_ge(pt_ready, 32 + b + 1)
                out = ps[7][0:64, 0:LAT]
                for j in range(NPAGES):
                    pe.matmul(out, PTS[:, j, :], plat[b % 2][:, j, :], start=j == 0, stop=False)
                pe.matmul(out, PTS[0:NSAMP, NPAGES, :], CN[0:NSAMP, 2, :], start=False, stop=True).then_inc(pv_done, 1)

            s_scores(0)
            for b in range(DB + 1):
                if b + 1 < DB:
                    s_scores(b + 1)
                s_turn(b)
                if b < DB:
                    s_values(b)
            pe.wait_ge(ol_ready, 32 + 2)
            for k in range(HEADS // 2):
                p = PLAIN["v_up"] + k
                pe.wait_ge(proj_evac, EVAC["v_up"] + k - 3)
                for h in (2 * k, 2 * k + 1):
                    r = VH * (h % 2)
                    for c in range(LC):
                        mm = pe.matmul(ps[p % 4][r:r + VH, 0:TOK], wuv[:, c, h * VH:(h + 1) * VH], OL[:, c, h, :],
                                       start=c == 0, stop=c == LC - 1)
                mm.then_inc(proj_done, 1)
            pe.wait_ge(proj_evac, EVAC["w_o"])
            project("w_o", AO)
            experts(1)
            norm(6, DC)

        @block.scalar
        def _(act):
            link = Steps(act, act_step)

            def square(k, src, came, meanwhile=None, first=0):
                for c in range(N_CHUNKS[k]):
                    came(c)
                    act.activation(SQ[:, c, :], src[:, (c + first) % N_CHUNKS[k], :], ACT.Square)\
                        .then_inc(sq_ready, 1)
                if meanwhile:
                    meanwhile()
                act.wait_ge(ms_ready, k + 1)
                act.activation(RV[:], RV[:], ACT.Sqrt).then_inc(sqrt_ready, 1)

            def evacuate(phase, write):
                def tile(i, s):
                    act.wait_ge(proj_done, i * SLOTS + PLAIN[phase] + s + 1)
                    write(i * SLOTS + s, s).then_inc(proj_evac, 1)
                with act.Fori(0, COUNT[phase] // SLOTS) as i:
                    for s in range(SLOTS):
                        tile(i, s)

            def at_chunk(t, k):
                return t[:, bass.ds(k, 1), :].rearrange("p a n -> p (a n)")

            def experts(l):
                kn = (1, 5)[l]
                added = EVAC[("w_out", "w_o")[l]]
                square(kn, X, lambda c: act.wait_ge(proj_evac, added + c + 1),
                       lambda: act.dma_start(SK[:], a["sk"][l]).then_inc(sk_in, 16))
                for c in range(DC):
                    act.wait_ge(xn_ready, (XN_FFN0, XN_FFN1)[l] + c + 1)
                    act.activation(XH[:, c, :], XP[:, c, :], ACT.Copy).then_inc(xh_ready, 1)
                evacuate(f"wq{l}", lambda k, s: act.activation(at_chunk(QT, k), ps[s][:, 0:TOK], ACT.Copy))
                for nb, (n0, rows) in enumerate(BLOCKS):
                    for g in range(4):
                        act.wait_ge(s_done, 12 * l + 4 * nb + g + 1)
                        act.activation(S[0:rows, nb, 4 * g:4 * g + 4, :],
                                       ps[4 + g][0:rows, :].rearrange("p (q k) -> p q k", q=4), ACT.Copy)\
                            .then_inc(s_evac, 1)

                def split(i, s, phase, base):
                    act.wait_ge(raw_full[s], i * 16 + 16 * (FIRST[phase] // SLOTS + 1))
                    for half in range(2):
                        k = 2 * s + half
                        if not (isinstance(i, int) and base + 2 * SLOTS * i + k - 3 <= 0):
                            act.wait_ge(mm_done, i * (2 * SLOTS) + base + k - 3)
                        act.activation(hi[k % 4][:], raw[s][:, half * HALF:(half + 1) * HALF], ACT.Copy)\
                            .then_inc(hi_ready, 1)

                def gelu(i, s):
                    act.activation(at_chunk(HB, i * SLOTS + s), ps[s % SLOTS][:, 0:TOK], ACT.Gelu_apprx_tanh)\
                        .then_inc(h_evac, 1)

                def h_tile(i, s):
                    split(i, s, f"u{l}", 512 * l)
                    if not (isinstance(i, int) and SLOTS * i + s < 2):
                        gelu(i, s - 2)

                for s in range(SLOTS):
                    h_tile(0, s)
                for r0, r1 in ((1, FREE_Q // 4 + 1), (FREE_Q // 4 + 1, FREE_S // 4 + 1), (FREE_S // 4 + 1, 32)):
                    if r0 == FREE_Q // 4 + 1:
                        act.wait_ge(s_done, 12 * (l + 1))
                        act.wait_ge(xl_ready, l + 1)
                    if r0 == FREE_S // 4 + 1:
                        act.wait_ge(topk_done, 3 * (l + 1))
                    with act.Fori(r0, r1) as i:
                        for s in range(SLOTS):
                            h_tile(i, s)
                for s in (2, 3):
                    act.wait_ge(mm_done, 512 * l + 2 * (124 + s + 1))
                    gelu(31, s)
                act.wait_ge(tr_done, 2 * (l + 1))
                act.activation(EX[:], ps[5][:, 0:TOK], ACT.Exp).then_inc(ex_ready, 1)
                def g_square(i, u):
                    act.wait_ge(dif_ready, i * 4 + 4 * NG * l + u + 1)
                    act.activation(ohi[u][:], ohi[u][:], ACT.Square).then_inc(dif_sq, 1)

                def g_onehot(i, u):
                    if isinstance(i, int) and i == NG - 1:
                        if u < 3:
                            g_square(i, u + 1)
                    else:
                        g_square(*((i, u + 1) if u < 3 else (i + 1, 0)))
                    act.wait_ge(dif_sq, i * 4 + 4 * NG * l + u + 1)
                    act.activation(ohi[u][:], ohi[u][:], ACT.Relu, scale=-1.0, bias=1.0).then_inc(ohi_ready, 1)

                def g_copy(i):
                    act.wait_ge(g_done, i * 4 + 4 * NG * l + 4)
                    if not (isinstance(i, int) and i + l == 0):
                        act.wait_ge(g_pool, i + NG * l)
                    act.activation(GS[:], ps[3][:].rearrange("p (n j) -> p n j", n=4), ACT.Copy).then_inc(g_copied, 1)

                g_square(0, 0)
                for u in range(4):
                    g_onehot(0, u)

                def g_group(i):
                    g_onehot(i, 0)
                    g_onehot(i, 1)
                    g_copy(i - 1)
                    g_onehot(i, 2)
                    g_onehot(i, 3)

                with act.Fori(1, NG - 1) as i:
                    g_group(i)
                g_group(NG - 1)
                g_copy(NG - 1)
                act.wait_ge(g_used, 3 * NG * (l + 1))
                act.wait_ge(g_pool, NG * (l + 1))

                def v_tile(i, s):
                    if not (isinstance(i, int)):
                        act.wait_ge(mm_done, i * (2 * SLOTS) + 512 * l + 256 + 2 * s - 2)
                    act.activation(WH[s % 2][:], at_chunk(HB, i * SLOTS + s), ACT.Copy)
                    split(i, s, f"v{l}", 512 * l + 256)

                with act.Fori(0, P // SLOTS) as i:
                    for s in range(SLOTS):
                        v_tile(i, s)

            for t, name in ((gains, "gains"), (ident, "ident"), (blk, "blk"), (iota, "iota")):
                act.dma_start(t[:], a[name]).then_inc(const_in, 16)
            for t, name in ((lru, "lru"), (hist, "hist"), (h0, "h0"), (wg, "wg")):
                act.dma_start(t[:], a[name]).then_inc(lru_in, 16)
            square(0, X, lambda c: act.wait_ge(x_in, 16))
            act.wait_ge(lru_in, 16 * 4)
            link(act.activation(SP[:, 0, :], lru[:, C_LAM:C_LAM + DC], ACT.Abs))
            act.activation(SP[:, 1, :], SP[:, 0, :], ACT.Exp, scale=-1.0).then_inc(sp_act, 1)
            act.wait_ge(sp_dve, 1)
            act.activation(SP[:, 3, :], SP[:, 2, :], ACT.Ln).then_inc(sp_act, 1)
            act.wait_ge(hist_ready, 1)
            for c in range(DC):
                s = c % SLOTS
                act.wait_ge(proj_done, c + 1)
                act.activation(XB[:, c, HIST:HIST + SEQ], ps[s][:, 0:SEQ], ACT.Copy)
                act.activation(XB[:, c, HIST + SEQ:XBW].rearrange("p (b t) -> p b t", b=DB)[:, :, HIST:],
                               ps[s][:, SEQ:TOK].rearrange("p (b t) -> p b t", b=DB), ACT.Copy)\
                    .then_inc(proj_evac, 1)
            for k in range(16):
                p = PLAIN["gates"] + k
                act.wait_ge(proj_done, p + 1)
                dst, bias = (RG, C_GA) if k < DC else (IG, C_GX)
                c = k % DC
                act.activation(dst[:, c, :], ps[p % 4][:, 0:TOK], ACT.Sigmoid, bias=lru[:, bias + c:bias + c + 1])\
                    .then_inc(proj_evac, 1)

            def gate_inputs(*chunks):
                for c in chunks:
                    act.wait_ge(proj_done, PLAIN["w_gate"] + c + 1)
                    act.activation(GATE[:, c, :], ps[c % SLOTS][:, 0:TOK], ACT.Copy).then_inc(proj_evac, 1)

            act.wait_ge(z_ready, 1)
            act.activation(LA[:, :, 0:SEQ], RG[:, :, 0:SEQ], ACT.Exp)
            act.activation(LA[:, :, SEQ:SCW].rearrange("p c (b t) -> p c b t", b=DB)[:, :, :, 1:],
                           RG[:, :, SEQ:TOK].rearrange("p c (b t) -> p c b t", b=DB), ACT.Exp)
            link(act.activation(T1[:], RG[:], ACT.Tanh, scale=-1.0))
            gate_inputs(0, 1)
            link(act.activation(T2[:], T1[:], ACT.Ln, bias=1.0))
            act.activation(T2[:], T2[:], ACT.Exp, scale=-1.0).then_inc(at_ready, 1)
            gate_inputs(2, 3, 4)
            act.wait_ge(m2_ready, 1)
            act.activation(T1[:], T1[:], ACT.Sqrt, scale=2.0).then_inc(m_ready, 1)
            gate_inputs(5, 6, 7)
            act.wait_ge(proj_evac, PLAIN["w_gate"] + DC)
            act.activation(GATE[:], GATE[:], ACT.Gelu_apprx_tanh).then_inc(gate_ready, 1)
            act.wait_ge(st_ready, 1)
            act.dma_start(o["h"], HS[:]).then_inc(out_dma, 16)
            act.dma_start(o["conv"], CV[:]).then_inc(out_dma, 16)
            act.wait_ge(out_dma, 32)
            experts(0)

            def load_mla():
                for t, name in ((COS, "cos"), (SIN, "sin"), (causal, "causal"), (smask, "smask"), (wuk, "wuk"),
                                (wuv, "wuv"), (pages, "pages")):
                    act.dma_start(t[:], a[name]).then_inc(mla_in, 16)

            square(2, X, lambda c: act.wait_ge(x_ready, c + 1), load_mla, first=DC - 1)
            for s in range(LC):
                act.wait_ge(proj_done, PLAIN["kv"] + s + 1)
                ins = act.activation(CR[:, s, :], ps[s][:, 0:TOK], ACT.Copy)
                if s == LC - 1:
                    link(ins)
            act.wait_ge(xn_ready, XN_MIX1 + DC)
            square(3, CR, lambda c: None)
            evacuate("w_dq", lambda k, s: act.activation(at_chunk(CQ, k), ps[s][:, 0:TOK], ACT.Copy))
            act.wait_ge(cnt_done, 1)
            for nb, (n0, rows) in enumerate(BLOCKS):
                ins = act.activation(CN[0:rows, nb, :], ps[4 + nb][0:rows, 0:LAT], ACT.Copy)
            ins.then_inc(cn_ready, 1)
            square(4, CQ, lambda c: act.wait_ge(proj_evac, EVAC["w_dq"] + 4))
            act.wait_ge(ct_ready, 1)
            act.wait_ge(kr_ready, 1)
            act.dma_start(o["ckv"], CT[:]).then_inc(out_dma, 16)
            act.dma_start(o["kr"], KR[:]).then_inc(out_dma, 16)
            for t in range(4):
                act.wait_ge(proj_done, PLAIN["w_uq"] + t + 1)
                act.activation(QN[:, 2 * t, :], ps[t][:, 0:TOK], ACT.Copy)
                act.activation(QN[:, 2 * t + 1, :], ps[4 + t][:, 0:TOK], ACT.Copy).then_inc(proj_evac, 1)
            act.wait_ge(qr_ready, 1)
            for q in range(4):
                act.dma_start(QR[:].rearrange("r (g q) n -> r g q n", q=4)[:, :, q, :],
                              QRC[ROPE * q:ROPE * (q + 1), :, :]).then_inc(qr_in, 16)
            for h in range(HEADS):
                for c in range(LC):
                    p = PLAIN["q_lat"] + LC * h + c
                    act.wait_ge(proj_done, p + 1)
                    act.activation(QL[:, c, h, :], ps[p % 4][:, 0:TOK], ACT.Copy).then_inc(proj_evac, 1)
            act.wait_ge(qr_in, 16 * 4)
            act.wait_ge(proj_done, PLAIN["q_lat"] + 32)
            act.activation(stat[:, 0, 7:8], ident[:, 0:1], ACT.Copy).then_inc(ol_ready, 1)

            def p_exp_item(m):
                kk = P * (m // HEADS + 1)
                act.wait_ge(nm_ready, m + 1)
                act.activation(PP[m % 2][:, 0:kk], PP[m % 2][:, 0:kk], ACT.Exp, bias=stat[:, m % 2, 1:2],
                               scale=SCALE, accum_out=stat[:, m % 2, 2:3]).then_inc(p_exp, 1)

            def p_turn(m):
                qb = m // HEADS
                act.wait_ge(pt_done, m + 1)
                if m >= 2:
                    act.wait_ge(pv_done, m - 1)
                act.activation(PT[m % 2][:, 0:qb + 1, :], ps[2 + m % 2][:, 0:P * (qb + 1)].rearrange(
                    "p (k q) -> p k q", q=P), ACT.Copy).then_inc(pt_ready, 1)

            def p_out(m):
                qb, h = divmod(m, HEADS)
                act.wait_ge(pv_done, m + 1)
                act.activation(OL[:, :, h, qb * P:(qb + 1) * P],
                               ps[4 + m % 2][:, 0:LC * P].rearrange("p (c q) -> p c q", c=LC), ACT.Copy)\
                    .then_inc(ol_ready, 1)

            for m in range(32 + 2):
                if m < 32:
                    p_exp_item(m)
                if 1 <= m <= 32:
                    p_turn(m - 1)
                if m >= 2:
                    p_out(m - 2)

            def s_exp(b):
                bk = 3 * (b % 2)
                act.wait_ge(nm_ready, 32 + b + 1)
                st = stat[0:64, b % 2, :]
                for k in range(2):
                    act.activation(PS[b % 2][:, 512 * k:512 * k + 512], ps[bk + k][0:64, :], ACT.Exp,
                                   bias=st[:, 1:2], scale=SCALE, accum_out=st[:, 2 + k:3 + k])
                act.activation(PS[b % 2][:, PAST:], PS[b % 2][:, PAST:], ACT.Exp, bias=st[:, 1:2], scale=SCALE,
                               accum_out=st[:, 4:5]).then_inc(p_exp, 1)

            def s_turn(b):
                act.wait_ge(pt_done, 32 + b + 1)
                if b >= 1:
                    n0 = SEQ + DS * (b - 1)
                    ins = act.activation(OL[:, :, :, n0:n0 + DS], ps[7][:, LAT:LAT + P].rearrange(
                        "p (c h t) -> p c h t", c=LC, t=DS), ACT.Copy)
                if b < DB:
                    act.activation(PTS[:, 0:NPAGES, :], ps[6][:].rearrange("p (j q) -> p j q", q=64), ACT.Copy)
                    act.activation(PTS[0:NSAMP, NPAGES, :], ps[7][0:NSAMP, 448:512], ACT.Copy).then_inc(pt_ready, 1)
                else:
                    ins.then_inc(ol_ready, 1)

            def s_out(b):
                act.wait_ge(pv_done, 32 + b + 1)
                act.activation(OS[:], ps[7][0:64, 0:LAT], ACT.Copy).then_inc(os_ready, 1)

            s_exp(0)
            for b in range(DB + 1):
                s_turn(b)
                if b + 1 < DB:
                    s_exp(b + 1)
                if b < DB:
                    s_out(b)
            for k in range(HEADS // 2):
                p = PLAIN["v_up"] + k
                act.wait_ge(proj_done, p + 1)
                act.activation(AO[:, k, :], ps[p % 4][:, 0:TOK], ACT.Copy).then_inc(proj_evac, 1)
            experts(1)
            square(6, X, lambda c: act.wait_ge(x_ready, DC + c + 1), first=DC - 1)

        @block.vector
        def _(dve):
            link = Steps(dve, dve_step)

            def ones_for(k):
                dve.memset(ones[:], 1.0).then_inc(ones_ready, 1)

            def inv_rms(k, width):
                dve.wait_ge(ss_done, k + 1)
                dve.tensor_scalar(RV[:], ps[7][:, 0:TOK], 1.0 / width, EPS, ALU.mult, ALU.add).then_inc(ms_ready, 1)
                dve.wait_ge(sqrt_ready, k + 1)
                link(dve.reciprocal(RT[:], RV[:]))

            def scaled(dst, src, gain, chunks, ready=None):
                for c in range(chunks):
                    ins = dve.scalar_tensor_tensor(dst[:, c, :], src[:, c, :], gains[:, gain + c:gain + c + 1], RT[:],
                                                   ALU.mult, ALU.mult)
                    if ready:
                        ins.then_inc(ready, 1)
                return ins

            def add_to_x(phase):
                with dve.Fori(0, COUNT[phase] // SLOTS) as i:
                    for s in range(SLOTS):
                        dve.wait_ge(proj_done, i * SLOTS + PLAIN[phase] + s + 1)
                        xc = X[:, bass.ds(i * SLOTS + s, 1), :].rearrange("p a n -> p (a n)")
                        dve.tensor_tensor(xc, xc, ps[s][:, 0:TOK], ALU.add).then_inc(proj_evac, 1)
                dve.wait_ge(proj_evac, EVAC[phase] + COUNT[phase])

            def per_head(fn, count):
                for k in range(count):
                    ins = fn(k)
                link(ins)

            def topk(nb, rows):
                r = slice(0, rows)
                s = [S[r, nb, hp, :] for hp in range(2 * PH)]
                per_head(lambda k: dve.max(V16[r, k, 0:8], s[k]), 16)
                per_head(lambda k: dve.max_index(I16[r, k, 0:8], V16[r, k, 0:8], s[k]), 16)
                per_head(lambda k: dve.match_replace(s[k], V16[r, k, 0:8], s[k], LOWEST), 16)
                per_head(lambda k: dve.max(V16[r, k, 8:16], s[k]), 16)
                per_head(lambda k: dve.max_index(I16[r, k, 8:16], V16[r, k, 8:16], s[k]), 16)
                v = V16[r].rearrange("p (h t) k -> p h t k", t=2)
                c4 = CAND[r]
                link(dve.tensor_tensor(
                    c4, v[:, :, 0, :].unsqueeze(3).broadcast_to([rows, PH, TOPK, TOPK]),
                    v[:, :, 1, :].unsqueeze(2).broadcast_to([rows, PH, TOPK, TOPK]), ALU.add))
                c = [CAND[r, h].rearrange("p a b -> p (a b)") for h in range(PH)]
                per_head(lambda k: dve.max(CS[r, k, 0:8], c[k]), 8)
                per_head(lambda k: dve.max_index(CP[r, k, 0:8], CS[r, k, 0:8], c[k]), 8)
                per_head(lambda k: dve.match_replace(c[k], CS[r, k, 0:8], c[k], LOWEST), 8)
                per_head(lambda k: dve.max(CS[r, k, 8:16], c[k]), 8)
                per_head(lambda k: dve.max_index(CP[r, k, 8:16], CS[r, k, 8:16], c[k]), 8)
                cp = CP[r].rearrange("p h k -> p (h k)")
                dve.tensor_scalar(CA[r, 0, :], cp, 4, None, ALU.logical_shift_right)
                dve.tensor_scalar(CA[r, 1, :], cp, 15, None, ALU.bitwise_and)
                i2 = I16[r].rearrange("p (h t) k -> p h t k", t=2)
                f2 = IF[r].rearrange("p (h t) k -> p h t k", t=2)
                dve.tensor_scalar(f2[:, :, 0, :], i2[:, :, 0, :], float(KEYS), None, ALU.mult)
                dve.tensor_copy(f2[:, :, 1, :], i2[:, :, 1, :])
                link(dve.tensor_tensor(CM[r, nb].rearrange("p (h k) -> p h k", k=TOPK), CS[r],
                                       CS[r, :, 0:1].broadcast_to([rows, PH, TOPK]), ALU.subtract))
                link(dve.tensor_copy(CF[r], CA[r]))
                for t in range(2):
                    eq = CAND[r].rearrange("p h k a -> p (h k) a")
                    link(dve.tensor_tensor(eq, CF[r, t, :].unsqueeze(2).broadcast_to([rows, PH * TOPK, TOPK]),
                                           iota[r, 0:TOPK].unsqueeze(1).broadcast_to([rows, PH * TOPK, TOPK]),
                                           ALU.is_equal))
                    link(dve.tensor_tensor(c4, c4, f2[:, :, t, :].unsqueeze(2).broadcast_to([rows, PH, TOPK, TOPK]),
                                           ALU.mult))
                    link(dve.tensor_reduce(EE[r, t, :], eq, AX_X, ALU.add))
                dve.tensor_tensor(E[r, nb], EE[r, 0, :], EE[r, 1, :], ALU.add).then_inc(topk_done, 1)

            def experts(l):
                kn = (1, 5)[l]
                inv_rms(kn, D)
                scaled(XP, X, (G_FFN0, G_FFN1)[l], DC, xn_ready)
                dve.wait_ge(xn_ready, (XN_FFN0, XN_FFN1)[l] + DC)
                dve.wait_ge(xh_ready, DC * (l + 1))
                dve.tensor_tensor(XL[:], XP[:], XH[:].bitcast(F32), ALU.subtract).then_inc(xl_ready, 1)
                for nb, (_, rows) in enumerate(BLOCKS):
                    dve.wait_ge(s_evac, 12 * l + 4 * nb + 4)
                    if 3 * l + nb:
                        dve.wait_ge(topk_done, 3 * l + nb)
                    topk(nb, rows)
                dve.wait_ge(tr_done, 2 * (l + 1))
                link(dve.tensor_copy(EU[:], ps[4][:, 0:TOK]))
                dve.tensor_scalar(IU[:], EU[:], 7, None, ALU.logical_shift_right)
                link(dve.tensor_scalar(JU[:], EU[:], KEYS - 1, None, ALU.bitwise_and))
                dve.tensor_copy(IT[:], IU[:])
                link(dve.tensor_copy(JT[:], JU[:]))
                dve.wait_ge(bs_done, l + 1)
                link(dve.reciprocal(GT[:], ps[6][:, 0:TOK]))
                dve.tensor_tensor(GT[:], GT[:], EX[:], ALU.mult).then_inc(gt_ready, 1)
                dve.wait_ge(gt_ready, l + 1)
                dve.wait_ge(h_evac, 128 * (l + 1))
                hb = HB[:].rearrange("p j n -> p n j")

                def g_onehot(i, u):
                    if not (isinstance(i, int) and 4 * (i + NG * l) + u - 1 <= 0):
                        dve.wait_ge(g_done, i * 4 + 4 * NG * l + u - 1)
                    for t in range(4):
                        n = i * 16 + 4 * u + t
                        ins = dve.tensor_scalar(ohj[u % 2][:, t, :], iota[:], JT[:, bass.ds(n, 1)],
                                                GT[:, bass.ds(n, 1)], ALU.is_equal, ALU.mult)
                    ins.then_inc(ohj_ready, 1)

                def g_apply(i, u):
                    dve.wait_ge(g_done, i * 4 + 4 * NG * l + u + 1)
                    w = hb[:, bass.ds(i * 16 + 4 * u, 4), :]
                    dve.tensor_tensor(w, w, ps[u % 4][:].rearrange("p (n j) -> p n j", n=4), ALU.mult)\
                        .then_inc(g_used, 1)

                g_onehot(0, 0)
                with dve.Fori(0, NG - 1) as i:
                    for u in range(4):
                        if u < 3:
                            g_onehot(i, u + 1)
                            g_apply(i, u)
                        else:
                            g_onehot(i + 1, 0)
                for u in range(3):
                    g_onehot(NG - 1, u + 1)
                    g_apply(NG - 1, u)
                dve.wait_ge(g_used, 3 * NG * (l + 1))
                dve.wait_ge(g_pool, NG * (l + 1))
                with dve.Fori(0, P // SLOTS) as i:
                    for s in range(SLOTS):
                        for half in range(2):
                            k = 2 * s + half
                            dve.wait_ge(hi_ready, i * (2 * SLOTS) + 512 * l + 256 + k + 1)
                            if half == 0:
                                hbr = HB[:, bass.ds(i * SLOTS + s, 1), :].rearrange("p a n -> p (a n)")
                                dve.tensor_tensor(WL[s % 2][:], hbr, WH[s % 2][:].bitcast(F32), ALU.subtract)
                            dve.tensor_tensor(lo[k % 4][:], raw[s][:, half * HALF:(half + 1) * HALF],
                                              hi[k % 4][:].bitcast(F32), ALU.subtract).then_inc(lo_ready, 1)
                dve.wait_ge(mm_done, 512 * (l + 1))
                ones_for((2, 6)[l])
                for k in range(DC):
                    c = (k + DC - 1) % DC
                    dve.tensor_tensor(X[:, c, :], X[:, c, :], ps[c][:, 0:TOK], ALU.add).then_inc(x_ready, 1)
                dve.wait_ge(x_ready, DC * (l + 1))

            ones_for(0)
            dve.wait_ge(const_in, 16 * 4)
            dve.wait_ge(x_in, 16)
            inv_rms(0, D)
            scaled(XN, X, G_MIX0, DC, xn_ready)
            dve.wait_ge(lru_in, 16 * 4)
            dve.wait_ge(sp_act, 1)
            dve.tensor_scalar(SP[:, 2, :], SP[:, 1, :], 1.0, None, ALU.add).then_inc(sp_dve, 1)
            dve.wait_ge(sp_dve, 1)
            link(dve.tensor_scalar(SP[:, 4, :], SP[:, 2, :], -1.0, None, ALU.add))
            dve.tensor_scalar(SP[:, 5, :], SP[:, 4, :], 1e-30, None, ALU.max)
            link(dve.scalar_tensor_tensor(SP[:, 7, :], SP[:, 4, :], 0.0, SP[:, 1, :], ALU.is_equal, ALU.mult))
            link(dve.reciprocal(SP[:, 6, :], SP[:, 5, :]))
            dve.wait_ge(sp_act, 2)
            link(dve.tensor_tensor(SP[:, 6, :], SP[:, 6, :], SP[:, 3, :], ALU.mult))
            link(dve.tensor_tensor(SP[:, 6, :], SP[:, 6, :], SP[:, 1, :], ALU.mult))
            link(dve.tensor_tensor(SP[:, 6, :], SP[:, 6, :], SP[:, 7, :], ALU.add))
            link(dve.tensor_scalar(SP[:, 8, :], lru[:, C_LAM:C_LAM + DC], -1.0, 0.0, ALU.mult, ALU.max))
            link(dve.tensor_tensor(SP[:, 8, :], SP[:, 8, :], SP[:, 6, :], ALU.add))
            link(dve.tensor_scalar(SP[:, 9, :], SP[:, 8, :], -8.0, None, ALU.mult))
            def taps(k, c):
                return ((XC[:, c, 0:SEQ], XB[:, c, k:k + SEQ]),
                        (XC[:, c, SEQ:TOK].rearrange("p (b t) -> p b t", b=DB),
                         XB[:, c, HIST + SEQ:XBW].rearrange("p (b t) -> p b t", b=DB)[:, :, k:k + DS]))

            for c in range(DC):
                dve.wait_ge(proj_evac, c + 1)
                for k in range(CONV):
                    w = lru[:, C_W + k * DC + c:C_W + k * DC + c + 1]
                    for dst, src in taps(k, c):
                        if k == 0:
                            ins = dve.tensor_scalar(dst, src, w, lru[:, C_B + c:C_B + c + 1], ALU.mult, ALU.add)
                        else:
                            ins = dve.scalar_tensor_tensor(dst, src, w, dst, ALU.mult, ALU.add)
                    if k < CONV - 1:
                        link(ins)
                ins.then_inc(xc_ready, 1)
            dve.wait_ge(proj_evac, PLAIN["gates"] + DC)
            for c in range(DC):
                ins = dve.tensor_scalar(RG[:, c, :], RG[:, c, :], SP[:, 9, c:c + 1], None, ALU.mult)
            ins.then_inc(z_ready, 1)
            dve.wait_ge(proj_evac, PLAIN["gates"] + 2 * DC)
            dve.wait_ge(xc_ready, DC)
            link(dve.tensor_tensor(IG[:], IG[:], XC[:], ALU.mult))
            dve.wait_ge(at_ready, 1)
            dve.tensor_tensor(T1[:], T1[:], T2[:], ALU.mult).then_inc(m2_ready, 1)
            dve.wait_ge(m_ready, 1)

            def sample_cols(t, off):
                return t[:, :, SEQ:SCW].rearrange("p c (b t) -> p c b t", b=DB)[:, :, :, off:]

            def samples(t):
                return t[:, :, SEQ:TOK].rearrange("p c (b t) -> p c b t", b=DB)

            dve.wait_ge(hist_ready, 1)
            dve.tensor_tensor(LB[:, :, 0:SEQ], T1[:, :, 0:SEQ], IG[:, :, 0:SEQ], ALU.mult)
            link(dve.tensor_tensor(sample_cols(LB, 1), samples(T1), samples(IG), ALU.mult))
            for c in range(DC):
                ins = dve.tensor_tensor_scan(LH[:, c, :], LA[:, c, :], LB[:, c, :], 0.0, ALU.mult, ALU.add)
            link(ins)
            dve.wait_ge(gate_ready, 1)
            dve.tensor_tensor(Y[:, :, 0:SEQ], LH[:, :, 0:SEQ], GATE[:, :, 0:SEQ], ALU.mult)
            dve.tensor_tensor(samples(Y), sample_cols(LH, 1), samples(GATE), ALU.mult).then_inc(y_ready, 1)
            dve.tensor_copy(HS[:, :, 0:1], LH[:, :, SEQ - 1:SEQ])
            dve.tensor_copy(CV[:, :, 0:HIST], XB[:, :, SEQ:SEQ + HIST])
            for c in range(DC):
                dve.tensor_copy(HS[:, c, 1:].unsqueeze(2), sample_cols(LH, DS)[:, c])
                ins = dve.tensor_copy(CV[:, c, HIST:].rearrange("p (b t) -> p b t", b=DB),
                                      XB[:, c, HIST + SEQ:XBW].rearrange("p (b t) -> p b t", b=DB)[:, :, DS:])
            ins.then_inc(st_ready, 1)
            ones_for(1)
            add_to_x("w_out")
            experts(0)

            inv_rms(2, D)
            scaled(XN, X, G_KV, DC, xn_ready)
            dve.wait_ge(mla_in, 16 * MLA_LOADS)
            dve.wait_ge(proj_done, PLAIN["kv"] + 4)
            dve.tensor_tensor(KR[:], ps[2][0:ROPE, 0:TOK], COS[0:ROPE], ALU.mult)
            link(dve.tensor_tensor(KT[:], ps[3][0:ROPE, 0:TOK], SIN[0:ROPE], ALU.mult))
            dve.tensor_tensor(KR[:], KR[:], KT[:], ALU.add).then_inc(kr_ready, 1)
            scaled(XN, X, G_MIX1, DC, xn_ready)
            dve.wait_ge(act_step, 2)
            dve.wait_ge(xn_ready, XN_MIX1 + DC)
            dve.wait_ge(kr_ready, 1)
            dve.memset(stat[:, 0, 5:6], 0.0).then_inc(kv_free, 1)
            ones_for(3)
            inv_rms(3, LAT)
            scaled(CT, CR, G_CKV, LC).then_inc(ct_ready, 1)
            ones_for(4)
            inv_rms(4, QLORA)
            scaled(CQN, CQ, G_Q, QC, xn_ready)
            for t in range(4, 8):
                s = t % 4
                dve.wait_ge(proj_done, PLAIN["w_uq"] + t + 1)
                dst, tab = (QRC, COS) if t < 6 else (QRS, SIN)
                g = 2 * (t % 2)
                dve.tensor_tensor(dst[:, g, :], ps[s][:, 0:TOK], tab[:], ALU.mult)
                dve.tensor_tensor(dst[:, g + 1, :], ps[4 + s][:, 0:TOK], tab[:], ALU.mult).then_inc(proj_evac, 1)
            dve.wait_ge(proj_evac, EVAC["w_uq"] + 8)
            dve.tensor_tensor(QRC[:], QRC[:], QRS[:], ALU.add).then_inc(qr_ready, 1)

            dve.wait_ge(ol_ready, 1)
            for m in range(32):
                qb = m // HEADS
                kk = P * (qb + 1)
                st = stat[:, m % 2, :]
                pp = PP[m % 2]
                dve.wait_ge(sc_done, m + 1)
                if m >= 2:
                    dve.wait_ge(pt_done, m - 1)
                if qb:
                    dve.tensor_copy(pp[:, 0:P], ps[m % 2][:, 0:P])
                link(dve.tensor_tensor(pp[:, kk - P:kk], ps[m % 2][:, kk - P:kk], causal[:], ALU.add))
                link(dve.tensor_reduce(st[:, 0:1], pp[:, 0:kk], AX_X, ALU.max))
                dve.tensor_scalar(st[:, 1:2], st[:, 0:1], -SCALE, None, ALU.mult).then_inc(nm_ready, 1)
                dve.wait_ge(p_exp, m + 1)
                link(dve.reciprocal(st[:, 3:4], st[:, 2:3]))
                dve.tensor_scalar(pp[:, 0:kk], pp[:, 0:kk], st[:, 3:4], None, ALU.mult).then_inc(p_ready, 1)
            for b in range(DB):
                bk = 3 * (b % 2)
                st = stat[0:64, b % 2, :]
                p = PS[b % 2]
                dve.wait_ge(sc_done, 32 + b + 1)
                if b >= 2:
                    dve.wait_ge(pt_done, 32 + b - 1)
                else:
                    dve.wait_ge(p_ready, 32)
                link(dve.tensor_tensor(p[:, PAST:], ps[bk + 2][0:64, 0:NSAMP], smask[:, b, :], ALU.add))
                dve.tensor_reduce(st[:, 5:6], ps[bk][0:64, :], AX_X, ALU.max)
                dve.tensor_reduce(st[:, 6:7], ps[bk + 1][0:64, :], AX_X, ALU.max)
                link(dve.tensor_reduce(st[:, 7:8], p[:, PAST:], AX_X, ALU.max))
                link(dve.tensor_reduce(st[:, 0:1], st[:, 5:8], AX_X, ALU.max))
                dve.tensor_scalar(st[:, 1:2], st[:, 0:1], -SCALE, None, ALU.mult).then_inc(nm_ready, 1)
                dve.wait_ge(p_exp, 32 + b + 1)
                link(dve.tensor_reduce(st[:, 5:6], st[:, 2:5], AX_X, ALU.add))
                link(dve.reciprocal(st[:, 6:7], st[:, 5:6]))
                dve.tensor_scalar(p[:], p[:], st[:, 6:7], None, ALU.mult).then_inc(p_ready, 1)
            dve.wait_ge(pt_done, 32 + DB + 1)
            ones_for(5)
            add_to_x("w_o")
            experts(1)
            inv_rms(6, D)
            scaled(X, X, G_FIN, DC).then_inc(y_fin, 1)

        @block.gpsimd
        def _(pool):
            link = Steps(pool, pool_step)
            pool.wait_ge(lru_in, 16 * 4)
            pool.memset(XB[:, :, 0:HIST], 0.0)
            for c in range(DC):
                pool.tensor_copy(XB[:, c, HIST + SEQ:XBW].rearrange("p (b t) -> p b t", b=DB)[:, :, 0:HIST],
                                 hist[:, c])
                pool.memset(LA[:, c, SEQ:SCW].rearrange("p (b t) -> p b t", b=DB)[:, :, 0:1], 0.0)
                ins = pool.tensor_copy(LB[:, c, SEQ:SCW].rearrange("p (b t) -> p b t", b=DB)[:, :, 0:1],
                                       h0[:, c, :].unsqueeze(2))
            ins.then_inc(hist_ready, 1)
            for l in range(2):
                if l == 1:
                    pool.wait_ge(proj_evac, EVAC["q_lat"] + 32)
                    pool.wait_ge(qr_in, 16 * 4)
                    for c in range(LC):
                        pool.tensor_copy(QLS[:, c].rearrange("p b (h t) -> p h b t", t=DS),
                                         QL[:, c, :, SEQ:TOK].rearrange("p h (b t) -> p h b t", t=DS))
                    pool.tensor_copy(QRP[:].rearrange("p b (h t) -> p h b t", t=DS),
                                     QR[:, :, SEQ:TOK].rearrange("p h (b t) -> p h b t", t=DS)).then_inc(qs_ready, 1)
                with pool.Fori(0, P // SLOTS) as i:
                    for k in range(2 * SLOTS):
                        half = slice((k % 2) * HALF, (k % 2 + 1) * HALF)
                        pool.wait_ge(hi_ready, i * (2 * SLOTS) + 512 * l + k + 1)
                        pool.tensor_tensor(lo[k % 4][:], raw[k // 2][:, half], hi[k % 4][:].bitcast(F32), ALU.subtract)\
                            .then_inc(lo_ready, 1)
                pool.wait_ge(gt_ready, l + 1)

                def difference(i, u):
                    if not (isinstance(i, int) and 4 * (i + NG * l) + u - 3 <= 0):
                        pool.wait_ge(g_done, i * 4 + 4 * NG * l + u - 3)
                    pool.tensor_tensor(ohi[u][:], iota[:].unsqueeze(1).broadcast_to([P, 4, P]),
                                       IT[:, bass.ds(i * 16 + 4 * u, 4)].unsqueeze(2).broadcast_to([P, 4, P]),
                                       ALU.subtract).then_inc(dif_ready, 1)

                hb = HB[:].rearrange("p j n -> p n j")

                def apply(i):
                    pool.wait_ge(g_copied, i + NG * l + 1)
                    w = hb[:, bass.ds(i * 16 + 12, 4), :]
                    pool.tensor_tensor(w, w, GS[:], ALU.mult).then_inc(g_pool, 1)

                pool.wait_ge(h_evac, 128 * (l + 1))
                for u in range(4):
                    difference(0, u)
                with pool.Fori(1, NG) as i:
                    for u in range(4):
                        difference(i, u)
                    apply(i - 1)
                apply(NG - 1)


MLA_LOADS = 7
N_CHUNKS = [8, 8, 8, LC, QC, 8, 8]
N_BEFORE = [sum(N_CHUNKS[:k]) for k in range(7)]
XN_MIX0, XN_FFN0, XN_KV, XN_MIX1, XN_Q, XN_FFN1 = 0, 8, 16, 24, 32, 36


def shape_constants():
    f = np.float32
    half = ROPE // 2
    inv = np.power(f(10000.0), -np.arange(half, dtype=f) / f(half)).astype(f)
    pos = np.concatenate([np.arange(SEQ), np.tile(PAST + np.arange(DS), DB)]).astype(f)
    ang = inv[:, None] * pos[None, :]
    cos = np.tile(np.cos(ang), (P // half, 1)).astype(f)
    sin = np.tile(np.concatenate([-np.sin(ang), np.sin(ang)]), (P // ROPE, 1)).astype(f)
    q, k = np.arange(P)[:, None], np.arange(P)[None, :]
    causal = np.where(k <= q, 0.0, NEG).astype(f)
    t = np.tile(np.arange(DS), HEADS)[:, None, None]
    b = np.arange(DB)[None, :, None]
    kb, kt = (np.arange(NSAMP) // DS)[None, None, :], (np.arange(NSAMP) % DS)[None, None, :]
    smask = np.where((kb == b) & (kt <= t), 0.0, NEG).astype(f)
    return {"cos": cos, "sin": sin, "causal": causal, "smask": smask, "ident": np.eye(P, dtype=f),
            "blk": (q // TOPK == k // TOPK).astype(f), "iota": np.tile(np.arange(P, dtype=f), (P, 1))}


def kernel(**inputs):
    import concourse.bacc as _bacc
    from concourse.bass_utils import run_bass_kernel_spmd as _run

    x = {k: np.asarray(v) for k, v in inputs.items()}
    f = np.float32

    def cols(v):
        return v.reshape(-1, P).T

    def tiles(w):
        k, m = w.shape
        return w.reshape(k // P, P, m // P, P).transpose(2, 1, 0, 3).reshape(m // P, P, k)

    def features(a3):
        return a3.reshape(a3.shape[0], -1, P).transpose(2, 1, 0)

    stream = np.zeros((NTILES, P, TILE), f)

    def put(phase, t):
        stream[FIRST[phase]:FIRST[phase] + len(t), :, :t.shape[2]] = t

    t = tiles(x["lru_w_in"][0])
    put("w_gate", t[:DC])
    put("w_x", t[DC:])
    put("w_out", tiles(x["lru_w_out"][0]))
    for l in range(2):
        put(f"wq{l}", tiles(x["peer_w_q"][l]))
        u = x["peer_u"][l].reshape(P, P, DC, P)
        for j in range(P):
            stream[FIRST[f"u{l}"] + j] = u[:, j].transpose(2, 1, 0).reshape(P, TILE)
        put(f"v{l}", x["peer_v"][l].reshape(P, P, D).transpose(1, 0, 2))
    swap = np.concatenate([np.arange(ROPE // 2, ROPE), np.arange(ROPE // 2)])
    put("kv", tiles(x["w_dkv"]))
    for s, w in ((2, x["w_kr"]), (3, x["w_kr"][:, swap])):
        stream[FIRST["kv"] + s, :, :DC * ROPE] = w.reshape(DC, P, ROPE).transpose(1, 0, 2).reshape(P, -1)
    put("w_dq", tiles(x["mla_w_dq"][0]))
    uq = x["mla_w_uq"][0].reshape(QLORA, HEADS, NOPE + ROPE)
    parts = [tiles(np.ascontiguousarray(w).reshape(QLORA, -1)) for w in
             (uq[:, :, :NOPE], uq[:, :, NOPE:], uq[:, :, NOPE:][:, :, swap])]
    t = np.concatenate(parts)
    put("w_uq", t.reshape(8, 2, P, QLORA).transpose(0, 2, 1, 3).reshape(8, P, 2 * QLORA))
    put("w_o", tiles(x["mla_w_o"][0]))

    xs = x["x_sample"].reshape(NSAMP, D)
    arrays = {
        "stream": stream,
        "x": features(np.concatenate([x["x_prompt"][0], xs])),
        "gains": np.concatenate([cols(x["ln_mix"][0]), cols(x["ln_ffn"][0]), cols(x["ln_mix"][1]),
                                 cols(x["ln_ffn"][1]), cols(x["ln_final"]), cols(x["kv_norm"]),
                                 cols(x["ckv_norm"]), cols(x["mla_q_norm"][0])], axis=1),
        "lru": np.concatenate([cols(x["lru_conv_w"][0].reshape(-1)), cols(x["lru_conv_b"][0]),
                               cols(x["lru_gate_a_b"][0]), cols(x["lru_gate_x_b"][0]), cols(x["lru_lambda"][0])], axis=1),
        "hist": x["state_conv"][:, 0].reshape(DB, HIST, DC, P).transpose(3, 2, 0, 1),
        "h0": x["state_h"][:, 0].reshape(DB, DC, P).transpose(2, 1, 0),
        "wg": np.concatenate([x["lru_gate_a_w"][0], x["lru_gate_x_w"][0]]).transpose(1, 0, 2),
        "sk": x["peer_subkeys"].reshape(2, 2 * PH, KEYS, P).transpose(0, 3, 1, 2),
        "wuk": x["w_uk"].reshape(LAT, HEADS // 2, 2 * NOPE).transpose(2, 1, 0),
        "wuv": x["w_uv"].reshape(LC, P, HEADS * VH).transpose(1, 0, 2),
        "pool": np.concatenate([
            x["cache_ckv"], x["cache_ckv"].reshape(NPOOL, PAGE, LC, P).transpose(0, 3, 2, 1).reshape(NPOOL, P, LC * PAGE),
            np.pad(x["cache_krope"].transpose(0, 2, 1), ((0, 0), (0, P - ROPE), (0, 0)))], axis=2),
        "pages": x["page_table"].reshape(1, -1).astype(np.int32),
        **shape_constants(),
    }
    arrays = {k: np.ascontiguousarray(v) for k, v in arrays.items()}
    outs = {"y": (P, DC, TOK), "h": (P, DC, 1 + DB), "conv": (P, DC, (1 + DB) * HIST),
            "ckv": (P, LC, TOK), "kr": (ROPE, TOK)}

    nc = _bacc.Bacc("TRN2", target_bir_lowering=False, num_devices=1)
    a = {k: nc.dram_tensor(f"in_{k}", v.shape, mybir.dt.from_np(v.dtype), kind="ExternalInput").ap()
         for k, v in arrays.items()}
    o = {k: nc.dram_tensor(f"out_{k}", s, F32, kind="ExternalOutput").ap() for k, s in outs.items()}
    build(nc, a, o)
    r = _run(nc, [{f"in_{k}": v for k, v in arrays.items()}], core_ids=[0]).results[0]

    def tokens(t):
        return t.transpose(2, 1, 0).reshape(t.shape[2], -1)

    y, ckv, kr = tokens(r["out_y"]), tokens(r["out_ckv"]), r["out_kr"].T
    h = r["out_h"].transpose(2, 1, 0).reshape(1 + DB, D)
    conv = r["out_conv"].reshape(P, DC, 1 + DB, HIST).transpose(2, 3, 1, 0).reshape(1 + DB, HIST, D)
    c = np.ascontiguousarray
    return (c(y[None, :SEQ]), c(y[SEQ:].reshape(DB, DS, D)), c(h[None, :1]), c(conv[None, :1]),
            c(ckv[None, :SEQ]), c(kr[None, :SEQ]), c(h[1:, None]), c(conv[1:, None]),
            c(ckv[SEQ:].reshape(DB, DS, LAT)), c(kr[SEQ:].reshape(DB, DS, ROPE)))
```

```python
from contextlib import ExitStack

import numpy as np

import concourse.bass as bass
from concourse import mybir

F32 = mybir.dt.float32
F32R = mybir.dt.float32r
U32 = mybir.dt.uint32
I32 = mybir.dt.int32
ALU = mybir.AluOpType
ACT = mybir.ActivationFunctionType
AX_X = mybir.AxisListType.X

P = 128
D = 1024
DC = D // P
SEQ, DB, DS = 256, 8, 4
NSAMP = DB * DS
TOK = SEQ + NSAMP
PAST, PAGE = 1024, 128
NPAGES = PAST // PAGE
NPOOL = 80
CONV = 4
HIST = CONV - 1
HEADS, NOPE, ROPE, VH = 16, 64, 32, 64
LAT, QLORA = 256, 512
LC, QC = LAT // P, QLORA // P
SCALE = float(NOPE + ROPE) ** -0.5
PH, KEYS, TOPK = 8, 128, 16
EPS = 1e-6
NEG = -1e30
LOWEST = -3.0e38
BLOCKS = [(0, 128), (128, 128), (256, NSAMP)]

NG = TOK // 16

SLOTS = 4
TILE = 1024
HALF = TILE // 2
PHASES = [("w_x", 8), ("w_gate", 8), ("w_out", 8), ("wq0", 16), ("u0", 128), ("v0", 128),
          ("kv", 4), ("w_dq", 4), ("w_uq", 8), ("w_o", 8), ("wq1", 16), ("u1", 128), ("v1", 128)]
FIRST = {}
NTILES = 0
for _name, _n in PHASES:
    FIRST[_name] = NTILES
    NTILES += _n
COUNT = dict(PHASES)
SPLIT = {}
_n = 0
for _name, _k in PHASES:
    if _name[:-1] in ("wq", "u", "v"):
        SPLIT[_name] = _n
        _n += 2 * _k
QROWS = 16 + P

XBW = HIST + SEQ + DB * (HIST + DS)
SCW = SEQ + DB * (1 + DS)

G_MIX0, G_FFN0, G_MIX1, G_FFN1, G_FIN, G_KV, G_CKV, G_Q = 0, 8, 16, 24, 32, 40, 48, 50
NGAIN = 54
C_W, C_B, C_GA, C_GX, C_LAM = 0, 32, 40, 48, 56
NLRU = 64


class Steps:

    def __init__(self, eng, sem):
        self.eng, self.sem, self.n = eng, sem, 0

    def __call__(self, ins):
        self.n += 1
        ins.then_inc(self.sem, 1)
        self.eng.wait_ge(self.sem, self.n)


def build(nc, a, o):
    with ExitStack() as ctx:
        BASE = (nc.sbuf_base + 63) // 64 * 64
        HBW = P * TOK
        R0, RAW, HL = HBW, HBW + 4608, HBW + 4608 + SLOTS * TILE
        KON = HL + 4 * TILE

        def at(name, word, shape, dt=F32):
            return nc.alloc_sbuf_tensor_at(name, shape, dt, offset=BASE + 4 * word)

        def sem(name):
            return ctx.enter_context(nc.semaphore(name))

        raw = [at(f"raw{s}", RAW + s * TILE, [P, TILE]) for s in range(SLOTS)]
        hi = [at(f"hi{s}", HL + s * TILE, [P, HALF], F32R) for s in range(4)]
        lo = [at(f"lo{s}", HL + s * TILE + HALF, [P, HALF], F32R) for s in range(4)]
        X = at("X", KON, [P, DC, TOK])
        E = at("E", KON + 2304, [P, 3, P])
        CM = at("CM", KON + 2688, [P, 3, P])
        blk = at("blk", KON + 3072, [P, P])
        ident = at("ident", KON + 3200, [P, P])
        iota = at("iota", KON + 3328, [P, P])
        gains = at("gains", KON + 3456, [P, NGAIN])
        assert BASE + 4 * (KON + 3456 + NGAIN) <= nc.sbuf_usable_end

        SQ = at("SQ", HL, [P, DC, TOK])
        ones = at("ones", HL + 2304, [P, P])
        RT = at("RT", HL + 2432, [P, TOK])
        RV = at("RV", HL + 2720, [P, TOK])
        XN = at("XN", 25600, [P, DC, TOK])

        XB = at("XB", 0, [P, DC, XBW])
        XC = at("XC", 2560, [P, DC, TOK])
        GATE = at("GATE", 4864, [P, DC, TOK])
        RG = at("RG", 7168, [P, DC, TOK])
        IG = at("IG", 9536, [P, DC, TOK])
        LA = at("LA", 11840, [P, DC, SCW])
        LB = at("LB", 14208, [P, DC, SCW])
        LH = at("LH", 16576, [P, DC, SCW])
        Y = at("Y", 18944, [P, DC, TOK])
        T1 = at("T1", 21248, [P, DC, TOK])
        T2 = at("T2", 16576, [P, DC, TOK])
        wg = at("wg", 23552, [P, 2 * DC, P])
        hist = at("hist", 27904, [P, DC, DB, HIST])
        h0 = at("h0", 28096, [P, DC, DB])
        lru = at("lru", 28160, [P, NLRU])
        SP = at("SP", 28224, [P, 10, DC])
        HS = at("HS", 28352, [P, DC, 1 + DB])
        CV = at("CV", 28480, [P, DC, (1 + DB) * HIST])

        HB = at("HB", 0, [P, P, TOK])
        XH = at("XH", R0, [P, DC, TOK], F32R)
        XL = at("XL", R0 + 2304, [P, DC, TOK], F32R)
        XP = at("XP", 15840, [P, DC, TOK])
        QT = at("QT", 18144, [P, 2 * PH, TOK])
        SK = at("SK", 22752, [P, 2 * PH, KEYS])
        FREE_Q = 15840 // TOK
        S = at("S", 24800, [P, 3, 2 * PH, KEYS])
        FREE_S = 24800 // TOK
        W0 = 24800 + 6144
        V16 = at("V16", W0, [P, 2 * PH, TOPK])
        I16 = at("I16", W0 + 256, [P, 2 * PH, TOPK], U32)
        IF = at("IF", W0 + 512, [P, 2 * PH, TOPK])
        CAND = at("CAND", W0 + 768, [P, PH, TOPK, TOPK])
        CS = at("CS", W0 + 2816, [P, PH, TOPK])
        CP = at("CP", W0 + 2944, [P, PH, TOPK], U32)
        CA = at("CA", W0 + 3072, [P, 2, PH * TOPK], U32)
        CF = at("CF", W0 + 3328, [P, 2, PH * TOPK])
        EE = at("EE", W0 + 3584, [P, 2, PH * TOPK])
        IT = at("IT", KON + 2304, [P, TOK])
        JT = at("JT", KON + 2592, [P, TOK])
        GT = at("GT", KON + 2880, [P, TOK])
        FREE_T = P - 4
        EU = at("EU", FREE_T * TOK, [P, TOK], U32)
        IU = at("IU", (FREE_T + 1) * TOK, [P, TOK], U32)
        JU = at("JU", (FREE_T + 2) * TOK, [P, TOK], U32)
        EX = at("EX", (FREE_T + 3) * TOK, [P, TOK])
        ohi = [at(f"ohi{b}", HL + 512 * b, [P, 4, P]) for b in range(4)]
        ohj = [at(f"ohj{b}", R0 + 512 * b, [P, 4, P]) for b in range(4)]
        GS = at("GS", HL + 3072, [P, 4, P])
        WH = [at(f"WH{b}", R0 + 288 * b, [P, TOK], F32R) for b in range(2)]
        WL = [at(f"WL{b}", R0 + 576 + 288 * b, [P, TOK], F32R) for b in range(2)]

        QL = at("QL", 0, [P, LC, HEADS, TOK])
        QR = at("QR", 9216, [ROPE, HEADS, TOK])
        CT = at("CT", 13824, [P, LC, TOK])
        KR = at("KR", 14400, [ROPE, TOK])
        KT = at("KT", 14688, [ROPE, TOK])
        CN = at("CN", 14976, [P, 3, LAT])
        QN = at("QN", 15744, [P, HEADS // 2, TOK])
        QRC = at("QRC", 18048, [P, 4, TOK])
        QRS = at("QRS", 19200, [P, 4, TOK])
        CQ = at("CQ", 20352, [P, QC, TOK])
        CQN = at("CQN", 21504, [P, QC, TOK])
        wuk = at("wuk", 22656, [P, HEADS // 2, LAT])
        OL = at("OL", 15744, [P, LC, HEADS, TOK])
        stat = at("stat", 24960, [P, 3, 8])
        smask = at("smask", 25024, [HEADS * DS, DB, NSAMP])
        CR = at("CR", 30000, [P, LC, TOK])
        QLS = at("QLS", 25600, [P, LC, DB, HEADS * DS])
        QRP = at("QRP", 26624, [ROPE, DB, HEADS * DS])
        AO = at("AO", 25600, [P, DC, TOK])
        wuv = at("wuv", 27904, [P, LC, HEADS * VH])
        PP = [at(f"PP{b}", w, [P, SEQ]) for b, w in enumerate((29952, 29952 + 256, HL + 256))]
        PT = [at(f"PT{b}", 30464 + 256 * b, [P, 2, P]) for b in range(2)]
        PTS = at("PTS", 29952, [P, NPAGES + 1, HEADS * DS])
        PS = [at(f"PS{b}", HL + 1024 + 1088 * b, [HEADS * DS, PAST + NSAMP]) for b in range(2)]
        OS = at("OS", HL, [HEADS * DS, LAT])
        PKW = LAT + PAGE
        plat = [at(f"plat{b}", 30976 + b * NPAGES * LAT, [P, NPAGES, LAT]) for b in range(2)]
        pkeys = [at(f"pkeys{b}", 30976 + NPAGES * (2 * LAT + b * PKW), [P, NPAGES, PKW]) for b in range(2)]
        COS = at("COS", KON + 2304, [P, TOK])
        SIN = at("SIN", KON + 2592, [P, TOK])
        causal = at("causal", KON + 2880, [P, P])
        pages = at("pages", 25280, [1, DB * NPAGES], I32)

        ps = [ctx.enter_context(nc.psum_tensor(f"ps{b}", [P, 512], F32)) for b in range(8)]

        raw_full = [sem(f"raw_full{s}") for s in range(SLOTS)]
        x_in, const_in, lru_in, sk_in, mla_in, out_dma = map(sem, (
            "x_in", "const_in", "lru_in", "sk_in", "mla_in", "out_dma"))
        keys_in = [sem("keys_in0"), sem("keys_in1")]
        lat_in = [sem("lat_in0"), sem("lat_in1")]
        os_ready = sem("os_ready")
        proj_done, proj_evac = sem("proj_done"), sem("proj_evac")
        sq_ready, ones_ready, ss_done, ms_ready, sqrt_ready, xn_ready, x_ready = map(sem, (
            "sq_ready", "ones_ready", "ss_done", "ms_ready", "sqrt_ready", "xn_ready", "x_ready"))
        act_step, dve_step, pool_step = sem("act_step"), sem("dve_step"), sem("pool_step")
        sp_act, sp_dve = sem("sp_act"), sem("sp_dve")
        hist_ready, xc_ready, z_ready, at_ready, m2_ready, m_ready, y_ready, st_ready = map(sem, (
            "hist_ready", "xc_ready", "z_ready", "at_ready", "m2_ready", "m_ready", "y_ready", "st_ready"))
        s_done, s_evac, xh_ready, xl_ready = map(sem, ("s_done", "s_evac", "xh_ready", "xl_ready"))
        hi_ready, lo_ready, mm_done, h_evac = map(sem, ("hi_ready", "lo_ready", "mm_done", "h_evac"))
        topk_done, tr_done, ex_ready, bs_done, gt_ready = map(sem, (
            "topk_done", "tr_done", "ex_ready", "bs_done", "gt_ready"))
        g_copied, g_pool = sem("g_copied"), sem("g_pool")
        dif_ready, dif_sq, ohi_ready, ohj_ready, g_done, g_used = map(sem, (
            "dif_ready", "dif_sq", "ohi_ready", "ohj_ready", "g_done", "g_used"))
        kr_ready, ct_ready, cnt_done, cn_ready, qr_ready, qr_in = map(sem, (
            "kr_ready", "ct_ready", "cnt_done", "cn_ready", "qr_ready", "qr_in"))
        sc_done, nm_ready, p_exp, p_ready, pt_done, pt_ready, pv_done, ol_ready = map(sem, (
            "sc_done", "nm_ready", "p_exp", "p_ready", "pt_done", "pt_ready", "pv_done", "ol_ready"))
        gate_ready = sem("gate_ready")
        y_fin, qs_ready, kv_free = sem("y_fin"), sem("qs_ready"), sem("kv_free")

        PLAIN, EVAC = {}, {}
        n = 0
        for name, k in [("w_x", 8), ("gates", 16), ("w_gate", 8), ("w_out", 8), ("kv", 4), ("w_dq", 4),
                        ("w_uq", 8), ("q_lat", 32), ("v_up", 8), ("w_o", 8)]:
            PLAIN[name] = n
            EVAC[name] = n - COUNT["kv"] if "kv" in PLAIN and name != "kv" else n
            n += k

        def last_use(phase, k):
            if phase in SPLIT:
                return lo_ready, SPLIT[phase] + 2 * k + 2
            return proj_done, PLAIN[phase] + k + 1

        block = ctx.enter_context(nc.Block())

        @block.sync
        def _(sp):
            sp.dma_start(X[:], a["x"]).then_inc(x_in, 16)

            def load(t, s):
                src = a["stream"][t] if isinstance(t, int) else \
                    a["stream"][bass.ds(t, 1)].rearrange("a p f -> (a p) f")
                sp.dma_start(raw[s][:], src).then_inc(raw_full[s], 16)

            before = None
            for phase, count in PHASES:
                t0 = FIRST[phase]
                if phase == "w_o":
                    sp.wait_ge(mla_in, 16 * MLA_LOADS)
                    sp.wait_ge(ol_ready, 1)

                    def load_pages(numbers, dst, cols, loaded):
                        for j, pg in enumerate(numbers):
                            sp.dma_start(dst[:, j, :], a["pool"][bass.ds(pg, 1), :, cols].rearrange("a p f -> (a p) f"))\
                                .then_inc(loaded, 16)

                    def page_numbers(b):
                        return [sp.value_load(pages[0:1, n:n + 1], min_val=0, max_val=NPOOL - 1)
                                for n in range(b * NPAGES, (b + 1) * NPAGES)]

                    coming = page_numbers(0)
                    for b in range(DB):
                        numbers = coming
                        if b >= 2:
                            sp.wait_ge(sc_done, 32 + b - 1)
                        load_pages(numbers, pkeys[b % 2], slice(LAT, LAT + PKW), keys_in[b % 2])
                        if b + 1 < DB:
                            coming = page_numbers(b + 1)
                        if b >= 2:
                            sp.wait_ge(pv_done, 32 + b - 1)
                        load_pages(numbers, plat[b % 2], slice(0, LAT), lat_in[b % 2])
                for s in range(SLOTS):
                    if before:
                        sp.wait_ge(*last_use(before, COUNT[before] - SLOTS + s))
                    load(t0 + s, s)
                if count > SLOTS:
                    with sp.Fori(1, count // SLOTS) as i:
                        for s in range(SLOTS):
                            used, value = last_use(phase, s - SLOTS)
                            rate = 2 if phase in SPLIT else 1
                            sp.wait_ge(used, i * (SLOTS * rate) + value)
                            load(i * SLOTS + t0 + s, s)
                before = phase
            sp.wait_ge(y_fin, 1)
            sp.dma_start(o["y"], X[:]).then_inc(out_dma, 16)
            sp.wait_ge(out_dma, 16 * 5)

        @block.tensor
        def _(pe):
            def full(phase, i, s):
                pe.wait_ge(raw_full[s], i * 16 + 16 * (FIRST[phase] // SLOTS + 1))

            def norm_chunk(k, c):
                if c == 0:
                    pe.wait_ge(ones_ready, k + 1)
                pe.wait_ge(sq_ready, N_BEFORE[k] + c + 1)
                last = c == N_CHUNKS[k] - 1
                mm = pe.matmul(ps[7][:, 0:TOK], ones[:], SQ[:, c, :], start=c == 0, stop=last)
                if last:
                    mm.then_inc(ss_done, 1)

            def norm(k):
                for c in range(N_CHUNKS[k]):
                    norm_chunk(k, c)

            def add_and_norm(phase, xin, come, k):
                project(phase, xin, come=come, follow=lambda t: norm_chunk(k, t - 2) if t >= 2 else None)
                norm_chunk(k, DC - 2)
                norm_chunk(k, DC - 1)

            def project(phase, xin, chunks=DC, come=None, follow=None):
                def tile(i, s):
                    full(phase, i, s)
                    p = EVAC[phase] + s
                    if not isinstance(i, int) or i * SLOTS + p - 3 > 0:
                        pe.wait_ge(proj_evac, i * SLOTS + p - 3)
                    for c in range(chunks):
                        if come is not None and isinstance(i, int) and s == 0:
                            pe.wait_ge(come[0], come[1] + c + 1)
                        mm = pe.matmul(ps[s][:, 0:TOK], raw[s][:, c * P:(c + 1) * P], xin[:, c, :],
                                       start=c == 0, stop=c == chunks - 1)
                    mm.then_inc(proj_done, 1)
                    if follow:
                        follow(i * SLOTS + s)

                for s in range(SLOTS):
                    tile(0, s)
                if COUNT[phase] > SLOTS:
                    with pe.Fori(1, COUNT[phase] // SLOTS) as i:
                        for s in range(SLOTS):
                            tile(i, s)

            def experts(l):
                def three_passes(i, s, phase, row):
                    if not isinstance(i, int) or row + s - 3 > 0:
                        pe.wait_ge(h_evac, i * SLOTS + row + s - 3)
                    for half in range(2):
                        k = 2 * s + half
                        pe.wait_ge(lo_ready, i * (2 * SLOTS) + SPLIT[phase] + k + 1)
                        for c in range(4 * half, 4 * half + 4):
                            if phase[0] == "w" and isinstance(i, int) and s == 0:
                                pe.wait_ge(xl_ready, DC * l + c + 1)
                            w = slice((c % 4) * P, (c % 4 + 1) * P)
                            h, r = hi[k % 4][:, w], lo[k % 4][:, w]
                            pe.matmul(ps[s][:, 0:TOK], h, XH[:, c, :], start=c == 0, stop=False)
                            pe.matmul(ps[s][:, 0:TOK], h, XL[:, c, :], start=False, stop=False)
                            mm = pe.matmul(ps[s][:, 0:TOK], r, XH[:, c, :], start=False, stop=c == DC - 1)
                        mm.then_inc(mm_done, 1)

                wq = f"wq{l}"
                for s in range(SLOTS):
                    three_passes(0, s, wq, QROWS * l)
                with pe.Fori(1, COUNT[wq] // SLOTS) as i:
                    for s in range(SLOTS):
                        three_passes(i, s, wq, QROWS * l)
                pe.wait_ge(h_evac, QROWS * l + 16)
                pe.wait_ge(sk_in, 16 * (l + 1))
                for nb, (n0, rows) in enumerate(BLOCKS):
                    for g in range(4):
                        k = 12 * l + 4 * nb + g
                        if k >= 4:
                            pe.wait_ge(s_evac, k - 3)
                        for q in range(4):
                            hp = 4 * g + q
                            mm = pe.matmul(ps[4 + g][0:rows, q * KEYS:(q + 1) * KEYS], QT[:, hp, n0:n0 + rows],
                                           SK[:, hp, :], start=True, stop=True)
                        mm.then_inc(s_done, 1)
                u = f"u{l}"

                def u_tiles(i0, i1):
                    with pe.Fori(i0, i1) as i:
                        for s in range(SLOTS):
                            three_passes(i, s, u, QROWS * l + 16)

                for s in range(SLOTS):
                    three_passes(0, s, u, QROWS * l + 16)
                u_tiles(1, AT_TURN)
                pe.wait_ge(topk_done, 3 * (l + 1))
                for bank, src in ((4, E), (5, CM)):
                    for nb, (n0, rows) in enumerate(BLOCKS):
                        mm = pe.transpose(ps[bank][:, n0:n0 + rows], src[0:rows, nb, :], ident[0:rows, 0:rows])
                    mm.then_inc(tr_done, 1)
                u_tiles(AT_TURN, AT_TURN + 3)
                pe.wait_ge(ex_ready, l + 1)
                if l:
                    pe.wait_ge(mla_in, 16 * MLA_LOADS)
                pe.matmul(ps[6][:, 0:TOK], blk[:], EX[:], start=True, stop=True).then_inc(bs_done, 1)
                u_tiles(AT_TURN + 3, P // SLOTS)
                pe.wait_ge(gt_ready, l + 1)

                def g_batch(i, u):
                    pe.wait_ge(ohi_ready, i * 4 + 4 * NG * l + u + 1)
                    pe.wait_ge(ohj_ready, i * 4 + 4 * NG * l + u + 1)
                    if u == 3:
                        if not isinstance(i, int) or l:
                            pe.wait_ge(g_copied, i + NG * l)
                    elif not isinstance(i, int) or l:
                        pe.wait_ge(g_used, i * 3 + 3 * NG * l + u - 2)
                    for t in range(4):
                        mm = pe.matmul(ps[u][:, t * P:(t + 1) * P], ohi[u][:, t, :], ohj[u][:, t, :],
                                       start=True, stop=True)
                    mm.then_inc(g_done, 1)

                for u in range(4):
                    g_batch(0, u)
                with pe.Fori(1, NG) as i:
                    for u in range(4):
                        g_batch(i, u)

                def v_tile(i, s, first, last):
                    for half in range(2):
                        k = 2 * s + half
                        pe.wait_ge(lo_ready, i * (2 * SLOTS) + SPLIT[f"v{l}"] + k + 1)
                        for c in range(4 * half, 4 * half + 4):
                            w = slice((c % 4) * P, (c % 4 + 1) * P)
                            for n, (x, y) in enumerate(((hi, WH), (hi, WL), (lo, WH))):
                                mm = pe.matmul(ps[c][:, 0:TOK], x[k % 4][:, w], y[s % 2][:],
                                               start=first and n == 0, stop=last and n == 2, skip_group_check=True)
                        mm.then_inc(mm_done, 1)

                for s in range(SLOTS):
                    v_tile(0, s, s == 0, False)
                with pe.Fori(1, P // SLOTS - 1) as i:
                    for s in range(SLOTS):
                        v_tile(i, s, False, False)
                for s in range(SLOTS):
                    v_tile(P // SLOTS - 1, s, False, s == SLOTS - 1)

            pe.wait_ge(const_in, 16 * 4)
            norm(0)
            project("w_x", XN, come=(xn_ready, XN_MIX0))
            pe.wait_ge(lru_in, 16 * 4)
            for k in range(16):
                p = PLAIN["gates"] + k
                pe.wait_ge(proj_evac, p - 3)
                pe.wait_ge(xc_ready, min(k, DC - 1) + 1)
                pe.matmul(ps[p % 4][:, 0:TOK], wg[:, k, :], XC[:, k % DC, :], start=True, stop=True)\
                    .then_inc(proj_done, 1)
            project("w_gate", XN)
            add_and_norm("w_out", Y, (y_ready, 0), 1)
            experts(0)

            norm(2)
            for s in range(4):
                full("kv", 0, s)
                m = P if s < LC else ROPE
                for c in range(DC):
                    pe.wait_ge(xn_ready, XN_KV + c + 1)
                    mm = pe.matmul(ps[s][0:m, 0:TOK], raw[s][:, c * m:(c + 1) * m], XN[:, c, :],
                                   start=c == 0, stop=c == DC - 1)
                mm.then_inc(proj_done, 1)
            norm(3)
            pe.wait_ge(kv_free, 1)
            project("w_dq", XN, come=(xn_ready, XN_MIX1))
            pe.wait_ge(ct_ready, 1)
            for nb, (n0, rows) in enumerate(BLOCKS):
                for c in range(LC):
                    mm = pe.transpose(ps[4 + nb][0:rows, c * P:(c + 1) * P], CT[:, c, n0:n0 + rows], ident[:])
            mm.then_inc(cnt_done, 1)
            norm(4)
            pe.wait_ge(xn_ready, XN_Q + QC)
            pe.wait_ge(cn_ready, 1)
            for t in range(8):
                i, s = divmod(t, SLOTS)
                full("w_uq", i, s)
                pe.wait_ge(proj_evac, EVAC["w_uq"] + (t - 3 if t < 4 else 4))
                for half in range(2):
                    for c in range(QC):
                        mm = pe.matmul(ps[s + 4 * half][:, 0:TOK], raw[s][:, (half * QC + c) * P:(half * QC + c + 1) * P],
                                       CQN[:, c, :], start=c == 0, stop=c == QC - 1)
                mm.then_inc(proj_done, 1)
            pe.wait_ge(mla_in, 16 * MLA_LOADS)
            for h in range(HEADS):
                for c in range(LC):
                    p = PLAIN["q_lat"] + LC * h + c
                    k = EVAC["q_lat"] + LC * h + c
                    pe.wait_ge(proj_evac, k if k == EVAC["q_lat"] else k - 3)
                    r = slice(NOPE * (h % 2), NOPE * (h % 2) + NOPE)
                    pe.matmul(ps[p % 4][:, 0:TOK], wuk[r, h // 2, c * P:(c + 1) * P], QN[r, h // 2, :],
                              start=True, stop=True).then_inc(proj_done, 1)
            pe.wait_ge(proj_evac, EVAC["q_lat"] + 32)
            pe.wait_ge(qr_in, 16 * 4)

            def p_scores(m):
                qb, h = divmod(m, HEADS)
                q = slice(qb * P, qb * P + P)
                kk = P * (qb + 1)
                out = ps[SC_BANK[m % 3]][:, 0:kk]
                if m >= 3:
                    pe.wait_ge(nm_ready, m - 2)
                for c in range(LC):
                    pe.matmul(out, QL[:, c, h, q], CT[:, c, 0:kk], start=c == 0, stop=False)
                pe.matmul(out, QR[:, h, q], KR[:, 0:kk], start=False, stop=True).then_inc(sc_done, 1)

            def p_turn(m):
                qb = m // HEADS
                pe.wait_ge(p_ready, m + 1)
                if m >= 2:
                    pe.wait_ge(pt_ready, m - 1)
                for kb in range(qb + 1):
                    mm = pe.transpose(ps[2 + m % 2][:, kb * P:(kb + 1) * P], PP[m % 3][:, kb * P:(kb + 1) * P], ident[:])
                mm.then_inc(pt_done, 1)

            def p_values(m):
                qb = m // HEADS
                pe.wait_ge(pt_ready, m + 1)
                if m >= 2:
                    pe.wait_ge(ol_ready, m)
                for c in range(LC):
                    for kb in range(qb + 1):
                        mm = pe.matmul(ps[4 + m % 2][:, c * P:(c + 1) * P], CN[:, kb, c * P:(c + 1) * P],
                                       PT[m % 2][:, kb, :], start=kb == 0, stop=kb == qb)
                mm.then_inc(pv_done, 1)

            for m in range(32 + 3):
                if m < 32:
                    p_scores(m)
                if 2 <= m < 32 + 2:
                    p_turn(m - 2)
                if m >= 3:
                    p_values(m - 3)

            pe.wait_ge(qs_ready, 1)

            def s_scores(b):
                bk = 3 * (b % 2)
                pe.wait_ge(keys_in[b % 2], 16 * NPAGES * (b // 2 + 1))
                if b >= 2:
                    pe.wait_ge(p_exp, 32 + b - 1)
                else:
                    pe.wait_ge(ol_ready, 33)
                q = [QLS[:, c, b, :] for c in range(LC)] + [QRP[:, b, :]]
                for half in range(2):
                    pg = slice(4 * half, 4 * half + 4)
                    keys = [pkeys[b % 2][:, pg, c * PAGE:(c + 1) * PAGE] for c in range(LC)]
                    keys.append(pkeys[b % 2][0:ROPE, pg, LAT:])
                    for k in range(3):
                        pe.matmul(ps[bk + half][0:64, :], q[k], keys[k], start=k == 0, stop=k == 2)
                keys = [CT[:, c, SEQ:TOK] for c in range(LC)] + [KR[:, SEQ:TOK]]
                for k in range(3):
                    mm = pe.matmul(ps[bk + 2][0:64, 0:NSAMP], q[k], keys[k], start=k == 0, stop=k == 2)
                mm.then_inc(sc_done, 1)

            def s_turn(b):
                if b >= 1:
                    pe.wait_ge(os_ready, b)
                    for c in range(LC):
                        mm = pe.transpose(ps[7][:, LAT + 64 * c:LAT + 64 * c + 64], OS[:, c * P:(c + 1) * P],
                                          ident[0:64, 0:64])
                if b < DB:
                    pe.wait_ge(p_ready, 32 + b + 1)
                    for j in range(NPAGES):
                        pe.transpose(ps[6][:, 64 * j:64 * j + 64], PS[b % 2][:, j * P:(j + 1) * P], ident[0:64, 0:64])
                    mm = pe.transpose(ps[7][0:NSAMP, 448:512], PS[b % 2][:, PAST:PAST + NSAMP], ident[0:64, 0:64])
                mm.then_inc(pt_done, 1)

            def s_values(b):
                pe.wait_ge(lat_in[b % 2], 16 * NPAGES * (b // 2 + 1))
                pe.wait_ge(pt_ready, 32 + b + 1)
                out = ps[7][0:64, 0:LAT]
                for j in range(NPAGES):
                    pe.matmul(out, PTS[:, j, :], plat[b % 2][:, j, :], start=j == 0, stop=False)
                pe.matmul(out, PTS[0:NSAMP, NPAGES, :], CN[0:NSAMP, 2, :], start=False, stop=True).then_inc(pv_done, 1)

            s_scores(0)
            for b in range(DB + 1):
                if b + 1 < DB:
                    s_scores(b + 1)
                s_turn(b)
                if b < DB:
                    s_values(b)
            pe.wait_ge(ol_ready, 32 + 2)
            for k in range(HEADS // 2):
                p = PLAIN["v_up"] + k
                pe.wait_ge(proj_evac, EVAC["v_up"] + k - 3)
                for h in (2 * k, 2 * k + 1):
                    r = VH * (h % 2)
                    for c in range(LC):
                        mm = pe.matmul(ps[p % 4][r:r + VH, 0:TOK], wuv[:, c, h * VH:(h + 1) * VH], OL[:, c, h, :],
                                       start=c == 0, stop=c == LC - 1)
                mm.then_inc(proj_done, 1)
            pe.wait_ge(proj_evac, EVAC["w_o"])
            add_and_norm("w_o", AO, None, 5)
            experts(1)
            norm(6)

        @block.scalar
        def _(act):
            link = Steps(act, act_step)

            def square(k, src, came, meanwhile=None, first=0):
                for c in range(N_CHUNKS[k]):
                    came(c)
                    act.activation(SQ[:, c, :], src[:, (c + first) % N_CHUNKS[k], :], ACT.Square)\
                        .then_inc(sq_ready, 1)
                if meanwhile:
                    meanwhile()
                act.wait_ge(ms_ready, k + 1)
                act.activation(RV[:], RV[:], ACT.Sqrt).then_inc(sqrt_ready, 1)

            def evacuate(phase, write):
                def tile(i, s):
                    act.wait_ge(proj_done, i * SLOTS + PLAIN[phase] + s + 1)
                    write(i * SLOTS + s, s).then_inc(proj_evac, 1)
                with act.Fori(0, COUNT[phase] // SLOTS) as i:
                    for s in range(SLOTS):
                        tile(i, s)

            def at_chunk(t, k):
                return t[:, bass.ds(k, 1), :].rearrange("p a n -> p (a n)")

            def experts(l):
                kn = (1, 5)[l]
                added = EVAC[("w_out", "w_o")[l]]
                square(kn, X, lambda c: act.wait_ge(proj_evac, added + c + 1),
                       lambda: act.dma_start(SK[:], a["sk"][l]).then_inc(sk_in, 16))

                def split(i, s, phase):
                    act.wait_ge(raw_full[s], i * 16 + 16 * (FIRST[phase] // SLOTS + 1))
                    for half in range(2):
                        k = 2 * s + half
                        if not (isinstance(i, int) and SPLIT[phase] + 2 * SLOTS * i + k - 3 <= 0):
                            act.wait_ge(mm_done, i * (2 * SLOTS) + SPLIT[phase] + k - 3)
                        act.activation(hi[k % 4][:], raw[s][:, half * HALF:(half + 1) * HALF], ACT.Copy)\
                            .then_inc(hi_ready, 1)

                wq = f"wq{l}"
                split(0, 0, wq)
                for c in range(DC):
                    act.wait_ge(xn_ready, (XN_FFN0, XN_FFN1)[l] + c + 1)
                    act.activation(XH[:, c, :], XP[:, c, :], ACT.Copy).then_inc(xh_ready, 1)

                def query(i, s):
                    act.activation(at_chunk(QT, i * SLOTS + s), ps[s % SLOTS][:, 0:TOK], ACT.Copy).then_inc(h_evac, 1)

                for s in range(1, SLOTS):
                    split(0, s, wq)
                    if s >= 2:
                        query(0, s - 2)
                with act.Fori(1, COUNT[wq] // SLOTS) as i:
                    for s in range(SLOTS):
                        split(i, s, wq)
                        query(i, s - 2)
                for s in (2, 3):
                    act.wait_ge(mm_done, SPLIT[wq] + 2 * (12 + s + 1))
                    query(3, s)

                def gelu(i, s):
                    act.activation(at_chunk(HB, i * SLOTS + s), ps[s % SLOTS][:, 0:TOK], ACT.Gelu_apprx_tanh)\
                        .then_inc(h_evac, 1)

                def h_tile(i, s):
                    split(i, s, f"u{l}")
                    if not (isinstance(i, int) and SLOTS * i + s < 2):
                        gelu(i, s - 2)

                h_tile(0, 0)
                h_tile(0, 1)
                for nb, (n0, rows) in enumerate(BLOCKS):
                    for g in range(4):
                        act.wait_ge(s_done, 12 * l + 4 * nb + g + 1)
                        act.activation(S[0:rows, nb, 4 * g:4 * g + 4, :],
                                       ps[4 + g][0:rows, :].rearrange("p (q k) -> p q k", q=4), ACT.Copy)\
                            .then_inc(s_evac, 1)
                h_tile(0, 2)
                h_tile(0, 3)
                for r0, r1 in ((1, FREE_Q // 4 + 1), (FREE_Q // 4 + 1, FREE_S // 4 + 1),
                               (FREE_S // 4 + 1, AT_TURN + 1), (AT_TURN + 2, FREE_T // 4), (FREE_T // 4, 32)):
                    if r0 == FREE_Q // 4 + 1:
                        act.wait_ge(s_done, 12 * (l + 1))
                        act.wait_ge(xl_ready, DC * (l + 1))
                    if r0 == FREE_S // 4 + 1:
                        act.wait_ge(topk_done, 3 * (l + 1))
                    if r0 == AT_TURN + 2:
                        act.wait_ge(tr_done, 2 * (l + 1))
                        act.activation(EX[:], ps[5][:, 0:TOK], ACT.Exp).then_inc(ex_ready, 1)
                        for s in range(SLOTS):
                            h_tile(AT_TURN + 1, s)
                    if r0 == FREE_T // 4:
                        act.wait_ge(gt_ready, l + 1)
                    with act.Fori(r0, r1) as i:
                        for s in range(SLOTS):
                            h_tile(i, s)
                for s in (2, 3):
                    act.wait_ge(mm_done, SPLIT[f"u{l}"] + 2 * (124 + s + 1))
                    gelu(31, s)
                def g_square(i, u):
                    act.wait_ge(dif_ready, i * 4 + 4 * NG * l + u + 1)
                    act.activation(ohi[u][:], ohi[u][:], ACT.Square).then_inc(dif_sq, 1)

                def g_onehot(i, u):
                    if isinstance(i, int) and i == NG - 1:
                        if u < 3:
                            g_square(i, u + 1)
                    else:
                        g_square(*((i, u + 1) if u < 3 else (i + 1, 0)))
                    act.wait_ge(dif_sq, i * 4 + 4 * NG * l + u + 1)
                    act.activation(ohi[u][:], ohi[u][:], ACT.Relu, scale=-1.0, bias=1.0).then_inc(ohi_ready, 1)

                def g_copy(i):
                    act.wait_ge(g_done, i * 4 + 4 * NG * l + 4)
                    if not (isinstance(i, int) and i + l == 0):
                        act.wait_ge(g_pool, i + NG * l)
                    act.activation(GS[:], ps[3][:].rearrange("p (n j) -> p n j", n=4), ACT.Copy).then_inc(g_copied, 1)

                g_square(0, 0)
                for u in range(4):
                    g_onehot(0, u)

                def g_group(i):
                    g_onehot(i, 0)
                    g_onehot(i, 1)
                    g_copy(i - 1)
                    g_onehot(i, 2)
                    g_onehot(i, 3)

                with act.Fori(1, NG - 1) as i:
                    g_group(i)
                g_group(NG - 1)
                g_copy(NG - 1)
                act.wait_ge(g_used, 3 * NG * (l + 1))
                act.wait_ge(g_pool, NG * (l + 1))

                def v_tile(i, s):
                    if not (isinstance(i, int)):
                        act.wait_ge(mm_done, i * (2 * SLOTS) + SPLIT[f"v{l}"] + 2 * s - 2)
                    act.activation(WH[s % 2][:], at_chunk(HB, i * SLOTS + s), ACT.Copy)
                    split(i, s, f"v{l}")

                with act.Fori(0, P // SLOTS) as i:
                    for s in range(SLOTS):
                        v_tile(i, s)

            for t, name in ((gains, "gains"), (ident, "ident"), (blk, "blk"), (iota, "iota")):
                act.dma_start(t[:], a[name]).then_inc(const_in, 16)
            for t, name in ((lru, "lru"), (hist, "hist"), (h0, "h0"), (wg, "wg")):
                act.dma_start(t[:], a[name]).then_inc(lru_in, 16)
            square(0, X, lambda c: act.wait_ge(x_in, 16))
            act.wait_ge(lru_in, 16 * 4)
            link(act.activation(SP[:, 0, :], lru[:, C_LAM:C_LAM + DC], ACT.Abs))
            act.activation(SP[:, 1, :], SP[:, 0, :], ACT.Exp, scale=-1.0).then_inc(sp_act, 1)
            act.wait_ge(sp_dve, 1)
            act.activation(SP[:, 3, :], SP[:, 2, :], ACT.Ln).then_inc(sp_act, 1)
            act.wait_ge(hist_ready, 1)
            for c in range(DC):
                s = c % SLOTS
                act.wait_ge(proj_done, c + 1)
                act.activation(XB[:, c, HIST:HIST + SEQ], ps[s][:, 0:SEQ], ACT.Copy)
                act.activation(XB[:, c, HIST + SEQ:XBW].rearrange("p (b t) -> p b t", b=DB)[:, :, HIST:],
                               ps[s][:, SEQ:TOK].rearrange("p (b t) -> p b t", b=DB), ACT.Copy)\
                    .then_inc(proj_evac, 1)
            for k in range(16):
                p = PLAIN["gates"] + k
                act.wait_ge(proj_done, p + 1)
                dst, bias = (RG, C_GA) if k < DC else (IG, C_GX)
                c = k % DC
                act.activation(dst[:, c, :], ps[p % 4][:, 0:TOK], ACT.Sigmoid, bias=lru[:, bias + c:bias + c + 1])\
                    .then_inc(proj_evac, 1)

            def gate_inputs(*chunks):
                for c in chunks:
                    act.wait_ge(proj_done, PLAIN["w_gate"] + c + 1)
                    act.activation(GATE[:, c, :], ps[c % SLOTS][:, 0:TOK], ACT.Copy).then_inc(proj_evac, 1)

            act.wait_ge(z_ready, 1)
            act.activation(LA[:, :, 0:SEQ], RG[:, :, 0:SEQ], ACT.Exp)
            act.activation(LA[:, :, SEQ:SCW].rearrange("p c (b t) -> p c b t", b=DB)[:, :, :, 1:],
                           RG[:, :, SEQ:TOK].rearrange("p c (b t) -> p c b t", b=DB), ACT.Exp)
            link(act.activation(T1[:], RG[:], ACT.Tanh, scale=-1.0))
            gate_inputs(0, 1)
            link(act.activation(T2[:], T1[:], ACT.Ln, bias=1.0))
            act.activation(T2[:], T2[:], ACT.Exp, scale=-1.0).then_inc(at_ready, 1)
            gate_inputs(2, 3, 4)
            act.wait_ge(m2_ready, 1)
            act.activation(T1[:], T1[:], ACT.Sqrt, scale=2.0).then_inc(m_ready, 1)
            gate_inputs(5, 6, 7)
            act.wait_ge(proj_evac, PLAIN["w_gate"] + DC)
            for c in range(DC):
                act.activation(GATE[:, c, :], GATE[:, c, :], ACT.Gelu_apprx_tanh).then_inc(gate_ready, 1)
            act.wait_ge(st_ready, 1)
            act.dma_start(o["h"], HS[:]).then_inc(out_dma, 16)
            act.dma_start(o["conv"], CV[:]).then_inc(out_dma, 16)
            act.wait_ge(out_dma, 32)
            experts(0)

            def load_mla():
                for t, name in ((COS, "cos"), (SIN, "sin"), (causal, "causal"), (smask, "smask"), (wuk, "wuk"),
                                (wuv, "wuv"), (pages, "pages"), (blk, "blk")):
                    act.dma_start(t[:], a[name]).then_inc(mla_in, 16)

            square(2, X, lambda c: act.wait_ge(x_ready, c + 1), load_mla, first=DC - 1)
            for s in range(LC):
                act.wait_ge(proj_done, PLAIN["kv"] + s + 1)
                ins = act.activation(CR[:, s, :], ps[s][:, 0:TOK], ACT.Copy)
                if s == LC - 1:
                    link(ins)
            act.wait_ge(xn_ready, XN_MIX1 + DC)
            square(3, CR, lambda c: None)
            evacuate("w_dq", lambda k, s: act.activation(at_chunk(CQ, k), ps[s][:, 0:TOK], ACT.Copy))
            act.wait_ge(cnt_done, 1)
            for nb, (n0, rows) in enumerate(BLOCKS):
                ins = act.activation(CN[0:rows, nb, :], ps[4 + nb][0:rows, 0:LAT], ACT.Copy)
            ins.then_inc(cn_ready, 1)
            square(4, CQ, lambda c: act.wait_ge(proj_evac, EVAC["w_dq"] + 4))
            act.wait_ge(ct_ready, 1)
            act.wait_ge(kr_ready, 1)
            act.dma_start(o["ckv"], CT[:]).then_inc(out_dma, 16)
            act.dma_start(o["kr"], KR[:]).then_inc(out_dma, 16)
            for t in range(4):
                act.wait_ge(proj_done, PLAIN["w_uq"] + t + 1)
                act.activation(QN[:, 2 * t, :], ps[t][:, 0:TOK], ACT.Copy)
                act.activation(QN[:, 2 * t + 1, :], ps[4 + t][:, 0:TOK], ACT.Copy).then_inc(proj_evac, 1)
            act.wait_ge(qr_ready, 1)
            for q in range(4):
                act.dma_start(QR[:].rearrange("r (g q) n -> r g q n", q=4)[:, :, q, :],
                              QRC[ROPE * q:ROPE * (q + 1), :, :]).then_inc(qr_in, 16)
            for h in range(HEADS):
                for c in range(LC):
                    p = PLAIN["q_lat"] + LC * h + c
                    act.wait_ge(proj_done, p + 1)
                    act.activation(QL[:, c, h, :], ps[p % 4][:, 0:TOK], ACT.Copy).then_inc(proj_evac, 1)
            act.wait_ge(qr_in, 16 * 4)
            act.wait_ge(proj_done, PLAIN["q_lat"] + 32)
            act.activation(stat[:, 0, 7:8], ident[:, 0:1], ACT.Copy).then_inc(ol_ready, 1)

            def p_exp_item(m):
                kk = P * (m // HEADS + 1)
                act.wait_ge(nm_ready, m + 1)
                act.activation(PP[m % 3][:, 0:kk], PP[m % 3][:, 0:kk], ACT.Exp, bias=stat[:, m % 3, 1:2],
                               scale=SCALE, accum_out=stat[:, m % 3, 2:3]).then_inc(p_exp, 1)

            def p_turn(m):
                qb = m // HEADS
                act.wait_ge(pt_done, m + 1)
                if m >= 2:
                    act.wait_ge(pv_done, m - 1)
                act.activation(PT[m % 2][:, 0:qb + 1, :], ps[2 + m % 2][:, 0:P * (qb + 1)].rearrange(
                    "p (k q) -> p k q", q=P), ACT.Copy).then_inc(pt_ready, 1)

            def p_out(m):
                qb, h = divmod(m, HEADS)
                act.wait_ge(pv_done, m + 1)
                act.activation(OL[:, :, h, qb * P:(qb + 1) * P],
                               ps[4 + m % 2][:, 0:LC * P].rearrange("p (c q) -> p c q", c=LC), ACT.Copy)\
                    .then_inc(ol_ready, 1)

            for m in range(32 + 3):
                if m < 32:
                    p_exp_item(m)
                if 2 <= m < 32 + 2:
                    p_turn(m - 2)
                if m >= 3:
                    p_out(m - 3)

            def s_exp(b):
                bk = 3 * (b % 2)
                act.wait_ge(nm_ready, 32 + b + 1)
                st = stat[0:64, b % 2, :]
                for k in range(2):
                    act.activation(PS[b % 2][:, 512 * k:512 * k + 512], ps[bk + k][0:64, :], ACT.Exp,
                                   bias=st[:, 1:2], scale=SCALE, accum_out=st[:, 2 + k:3 + k])
                act.activation(PS[b % 2][:, PAST:], PS[b % 2][:, PAST:], ACT.Exp, bias=st[:, 1:2], scale=SCALE,
                               accum_out=st[:, 4:5]).then_inc(p_exp, 1)

            def s_turn(b):
                act.wait_ge(pt_done, 32 + b + 1)
                if b >= 1:
                    n0 = SEQ + DS * (b - 1)
                    ins = act.activation(OL[:, :, :, n0:n0 + DS], ps[7][:, LAT:LAT + P].rearrange(
                        "p (c h t) -> p c h t", c=LC, t=DS), ACT.Copy)
                if b < DB:
                    act.activation(PTS[:, 0:NPAGES, :], ps[6][:].rearrange("p (j q) -> p j q", q=64), ACT.Copy)
                    act.activation(PTS[0:NSAMP, NPAGES, :], ps[7][0:NSAMP, 448:512], ACT.Copy).then_inc(pt_ready, 1)
                else:
                    ins.then_inc(ol_ready, 1)

            def s_out(b):
                act.wait_ge(pv_done, 32 + b + 1)
                act.activation(OS[:], ps[7][0:64, 0:LAT], ACT.Copy).then_inc(os_ready, 1)

            s_exp(0)
            for b in range(DB + 1):
                s_turn(b)
                if b + 1 < DB:
                    s_exp(b + 1)
                if b < DB:
                    s_out(b)
            for k in range(HEADS // 2):
                p = PLAIN["v_up"] + k
                act.wait_ge(proj_done, p + 1)
                act.activation(AO[:, k, :], ps[p % 4][:, 0:TOK], ACT.Copy).then_inc(proj_evac, 1)
            experts(1)
            square(6, X, lambda c: act.wait_ge(x_ready, DC + c + 1), first=DC - 1)

        @block.vector
        def _(dve):
            link = Steps(dve, dve_step)

            def ones_for(k):
                dve.memset(ones[:], 1.0).then_inc(ones_ready, 1)

            def inv_rms(k, width):
                dve.wait_ge(ss_done, k + 1)
                dve.tensor_scalar(RV[:], ps[7][:, 0:TOK], 1.0 / width, EPS, ALU.mult, ALU.add).then_inc(ms_ready, 1)
                dve.wait_ge(sqrt_ready, k + 1)
                link(dve.reciprocal(RT[:], RV[:]))

            def scaled(dst, src, gain, chunks, ready=None):
                for c in range(chunks):
                    ins = dve.scalar_tensor_tensor(dst[:, c, :], src[:, c, :], gains[:, gain + c:gain + c + 1], RT[:],
                                                   ALU.mult, ALU.mult)
                    if ready:
                        ins.then_inc(ready, 1)
                return ins

            def add_to_x(phase):
                with dve.Fori(0, COUNT[phase] // SLOTS) as i:
                    for s in range(SLOTS):
                        dve.wait_ge(proj_done, i * SLOTS + PLAIN[phase] + s + 1)
                        xc = X[:, bass.ds(i * SLOTS + s, 1), :].rearrange("p a n -> p (a n)")
                        dve.tensor_tensor(xc, xc, ps[s][:, 0:TOK], ALU.add).then_inc(proj_evac, 1)
                dve.wait_ge(proj_evac, EVAC[phase] + COUNT[phase])

            def per_head(fn, count):
                for k in range(count):
                    ins = fn(k)
                link(ins)

            def topk(nb, rows):
                r = slice(0, rows)
                s = [S[r, nb, hp, :] for hp in range(2 * PH)]
                per_head(lambda k: dve.max(V16[r, k, 0:8], s[k]), 16)
                per_head(lambda k: dve.max_index(I16[r, k, 0:8], V16[r, k, 0:8], s[k]), 16)
                per_head(lambda k: dve.match_replace(s[k], V16[r, k, 0:8], s[k], LOWEST), 16)
                per_head(lambda k: dve.max(V16[r, k, 8:16], s[k]), 16)
                per_head(lambda k: dve.max_index(I16[r, k, 8:16], V16[r, k, 8:16], s[k]), 16)
                v = V16[r].rearrange("p (h t) k -> p h t k", t=2)
                c4 = CAND[r]
                link(dve.tensor_tensor(
                    c4, v[:, :, 0, :].unsqueeze(3).broadcast_to([rows, PH, TOPK, TOPK]),
                    v[:, :, 1, :].unsqueeze(2).broadcast_to([rows, PH, TOPK, TOPK]), ALU.add))
                c = [CAND[r, h].rearrange("p a b -> p (a b)") for h in range(PH)]
                per_head(lambda k: dve.max(CS[r, k, 0:8], c[k]), 8)
                per_head(lambda k: dve.max_index(CP[r, k, 0:8], CS[r, k, 0:8], c[k]), 8)
                per_head(lambda k: dve.match_replace(c[k], CS[r, k, 0:8], c[k], LOWEST), 8)
                per_head(lambda k: dve.max(CS[r, k, 8:16], c[k]), 8)
                per_head(lambda k: dve.max_index(CP[r, k, 8:16], CS[r, k, 8:16], c[k]), 8)
                cp = CP[r].rearrange("p h k -> p (h k)")
                dve.tensor_scalar(CA[r, 0, :], cp, 4, None, ALU.logical_shift_right)
                dve.tensor_scalar(CA[r, 1, :], cp, 15, None, ALU.bitwise_and)
                i2 = I16[r].rearrange("p (h t) k -> p h t k", t=2)
                f2 = IF[r].rearrange("p (h t) k -> p h t k", t=2)
                dve.tensor_scalar(f2[:, :, 0, :], i2[:, :, 0, :], float(KEYS), None, ALU.mult)
                dve.tensor_copy(f2[:, :, 1, :], i2[:, :, 1, :])
                link(dve.tensor_tensor(CM[r, nb].rearrange("p (h k) -> p h k", k=TOPK), CS[r],
                                       CS[r, :, 0:1].broadcast_to([rows, PH, TOPK]), ALU.subtract))
                link(dve.tensor_copy(CF[r], CA[r]))
                for t in range(2):
                    eq = CAND[r].rearrange("p h k a -> p (h k) a")
                    link(dve.tensor_tensor(eq, CF[r, t, :].unsqueeze(2).broadcast_to([rows, PH * TOPK, TOPK]),
                                           iota[r, 0:TOPK].unsqueeze(1).broadcast_to([rows, PH * TOPK, TOPK]),
                                           ALU.is_equal))
                    link(dve.tensor_tensor(c4, c4, f2[:, :, t, :].unsqueeze(2).broadcast_to([rows, PH, TOPK, TOPK]),
                                           ALU.mult))
                    link(dve.tensor_reduce(EE[r, t, :], eq, AX_X, ALU.add))
                dve.tensor_tensor(E[r, nb], EE[r, 0, :], EE[r, 1, :], ALU.add).then_inc(topk_done, 1)

            def experts(l):
                kn = (1, 5)[l]
                inv_rms(kn, D)
                scaled(XP, X, (G_FFN0, G_FFN1)[l], DC, xn_ready)
                dve.wait_ge(xn_ready, (XN_FFN0, XN_FFN1)[l] + DC)
                for c in range(DC):
                    dve.wait_ge(xh_ready, DC * l + c + 1)
                    dve.tensor_tensor(XL[:, c, :], XP[:, c, :], XH[:, c, :].bitcast(F32), ALU.subtract)\
                        .then_inc(xl_ready, 1)
                for nb, (_, rows) in enumerate(BLOCKS):
                    dve.wait_ge(s_evac, 12 * l + 4 * nb + 4)
                    if 3 * l + nb:
                        dve.wait_ge(topk_done, 3 * l + nb)
                    topk(nb, rows)
                dve.wait_ge(tr_done, 2 * (l + 1))
                link(dve.tensor_copy(EU[:], ps[4][:, 0:TOK]))
                dve.tensor_scalar(IU[:], EU[:], 7, None, ALU.logical_shift_right)
                link(dve.tensor_scalar(JU[:], EU[:], KEYS - 1, None, ALU.bitwise_and))
                dve.tensor_copy(IT[:], IU[:])
                link(dve.tensor_copy(JT[:], JU[:]))
                dve.wait_ge(bs_done, l + 1)
                link(dve.reciprocal(GT[:], ps[6][:, 0:TOK]))
                dve.tensor_tensor(GT[:], GT[:], EX[:], ALU.mult).then_inc(gt_ready, 1)
                dve.wait_ge(gt_ready, l + 1)
                dve.wait_ge(h_evac, QROWS * (l + 1))
                hb = HB[:].rearrange("p j n -> p n j")

                def g_onehot(i, u):
                    if not (isinstance(i, int) and 4 * (i + NG * l) + u - 3 <= 0):
                        dve.wait_ge(g_done, i * 4 + 4 * NG * l + u - 3)
                    for t in range(4):
                        n = i * 16 + 4 * u + t
                        ins = dve.tensor_scalar(ohj[u][:, t, :], iota[:], JT[:, bass.ds(n, 1)],
                                                GT[:, bass.ds(n, 1)], ALU.is_equal, ALU.mult)
                    ins.then_inc(ohj_ready, 1)

                def g_apply(i, u):
                    dve.wait_ge(g_done, i * 4 + 4 * NG * l + u + 1)
                    w = hb[:, bass.ds(i * 16 + 4 * u, 4), :]
                    dve.tensor_tensor(w, w, ps[u % 4][:].rearrange("p (n j) -> p n j", n=4), ALU.mult)\
                        .then_inc(g_used, 1)

                def g_group(i):
                    for u in range(4):
                        if u < 2:
                            g_onehot(i, u + 2)
                        elif not (isinstance(i, int) and i == NG - 1):
                            g_onehot(i + 1, u - 2)
                        if u < 3:
                            g_apply(i, u)

                g_onehot(0, 0)
                g_onehot(0, 1)
                g_group(0)
                with dve.Fori(1, NG - 1) as i:
                    g_group(i)
                g_group(NG - 1)
                dve.wait_ge(g_used, 3 * NG * (l + 1))
                dve.wait_ge(g_pool, NG * (l + 1))
                with dve.Fori(0, P // SLOTS) as i:
                    for s in range(SLOTS):
                        for half in range(2):
                            k = 2 * s + half
                            dve.wait_ge(hi_ready, i * (2 * SLOTS) + SPLIT[f"v{l}"] + k + 1)
                            if half == 0:
                                hbr = HB[:, bass.ds(i * SLOTS + s, 1), :].rearrange("p a n -> p (a n)")
                                dve.tensor_tensor(WL[s % 2][:], hbr, WH[s % 2][:].bitcast(F32), ALU.subtract)
                            dve.tensor_tensor(lo[k % 4][:], raw[s][:, half * HALF:(half + 1) * HALF],
                                              hi[k % 4][:].bitcast(F32), ALU.subtract).then_inc(lo_ready, 1)
                dve.wait_ge(mm_done, SPLIT[f"v{l}"] + 2 * COUNT[f"v{l}"])
                ones_for((2, 6)[l])
                for k in range(DC):
                    c = (k + DC - 1) % DC
                    dve.tensor_tensor(X[:, c, :], X[:, c, :], ps[c][:, 0:TOK], ALU.add).then_inc(x_ready, 1)
                dve.wait_ge(x_ready, DC * (l + 1))

            ones_for(0)
            dve.wait_ge(const_in, 16 * 4)
            dve.wait_ge(x_in, 16)
            inv_rms(0, D)
            scaled(XN, X, G_MIX0, DC, xn_ready)
            dve.wait_ge(lru_in, 16 * 4)
            dve.wait_ge(sp_act, 1)
            dve.tensor_scalar(SP[:, 2, :], SP[:, 1, :], 1.0, None, ALU.add).then_inc(sp_dve, 1)
            dve.wait_ge(sp_dve, 1)
            link(dve.tensor_scalar(SP[:, 4, :], SP[:, 2, :], -1.0, None, ALU.add))
            dve.tensor_scalar(SP[:, 5, :], SP[:, 4, :], 1e-30, None, ALU.max)
            link(dve.scalar_tensor_tensor(SP[:, 7, :], SP[:, 4, :], 0.0, SP[:, 1, :], ALU.is_equal, ALU.mult))
            link(dve.reciprocal(SP[:, 6, :], SP[:, 5, :]))
            dve.wait_ge(sp_act, 2)
            link(dve.tensor_tensor(SP[:, 6, :], SP[:, 6, :], SP[:, 3, :], ALU.mult))
            link(dve.tensor_tensor(SP[:, 6, :], SP[:, 6, :], SP[:, 1, :], ALU.mult))
            link(dve.tensor_tensor(SP[:, 6, :], SP[:, 6, :], SP[:, 7, :], ALU.add))
            link(dve.tensor_scalar(SP[:, 8, :], lru[:, C_LAM:C_LAM + DC], -1.0, 0.0, ALU.mult, ALU.max))
            link(dve.tensor_tensor(SP[:, 8, :], SP[:, 8, :], SP[:, 6, :], ALU.add))
            link(dve.tensor_scalar(SP[:, 9, :], SP[:, 8, :], -8.0, None, ALU.mult))
            def taps(k, c):
                return ((XC[:, c, 0:SEQ], XB[:, c, k:k + SEQ]),
                        (XC[:, c, SEQ:TOK].rearrange("p (b t) -> p b t", b=DB),
                         XB[:, c, HIST + SEQ:XBW].rearrange("p (b t) -> p b t", b=DB)[:, :, k:k + DS]))

            for c in range(DC):
                dve.wait_ge(proj_evac, c + 1)
                for k in range(CONV):
                    w = lru[:, C_W + k * DC + c:C_W + k * DC + c + 1]
                    for dst, src in taps(k, c):
                        if k == 0:
                            ins = dve.tensor_scalar(dst, src, w, lru[:, C_B + c:C_B + c + 1], ALU.mult, ALU.add)
                        else:
                            ins = dve.scalar_tensor_tensor(dst, src, w, dst, ALU.mult, ALU.add)
                    if k < CONV - 1:
                        link(ins)
                ins.then_inc(xc_ready, 1)
            dve.wait_ge(proj_evac, PLAIN["gates"] + DC)
            for c in range(DC):
                ins = dve.tensor_scalar(RG[:, c, :], RG[:, c, :], SP[:, 9, c:c + 1], None, ALU.mult)
            ins.then_inc(z_ready, 1)
            dve.wait_ge(proj_evac, PLAIN["gates"] + 2 * DC)
            dve.wait_ge(xc_ready, DC)
            link(dve.tensor_tensor(IG[:], IG[:], XC[:], ALU.mult))
            dve.wait_ge(at_ready, 1)
            dve.tensor_tensor(T1[:], T1[:], T2[:], ALU.mult).then_inc(m2_ready, 1)
            dve.wait_ge(m_ready, 1)

            def sample_cols(t, off):
                return t[:, :, SEQ:SCW].rearrange("p c (b t) -> p c b t", b=DB)[:, :, :, off:]

            def samples(t):
                return t[:, :, SEQ:TOK].rearrange("p c (b t) -> p c b t", b=DB)

            dve.wait_ge(hist_ready, 1)
            dve.tensor_tensor(LB[:, :, 0:SEQ], T1[:, :, 0:SEQ], IG[:, :, 0:SEQ], ALU.mult)
            link(dve.tensor_tensor(sample_cols(LB, 1), samples(T1), samples(IG), ALU.mult))
            for c in range(DC):
                ins = dve.tensor_tensor_scan(LH[:, c, :], LA[:, c, :], LB[:, c, :], 0.0, ALU.mult, ALU.add)
            link(ins)
            for c in range(DC):
                dve.wait_ge(gate_ready, c + 1)
                dve.tensor_tensor(Y[:, c, 0:SEQ], LH[:, c, 0:SEQ], GATE[:, c, 0:SEQ], ALU.mult)
                dve.tensor_tensor(samples(Y)[:, c], sample_cols(LH, 1)[:, c], samples(GATE)[:, c], ALU.mult)\
                    .then_inc(y_ready, 1)
            dve.tensor_copy(HS[:, :, 0:1], LH[:, :, SEQ - 1:SEQ])
            dve.tensor_copy(CV[:, :, 0:HIST], XB[:, :, SEQ:SEQ + HIST])
            for c in range(DC):
                dve.tensor_copy(HS[:, c, 1:].unsqueeze(2), sample_cols(LH, DS)[:, c])
                ins = dve.tensor_copy(CV[:, c, HIST:].rearrange("p (b t) -> p b t", b=DB),
                                      XB[:, c, HIST + SEQ:XBW].rearrange("p (b t) -> p b t", b=DB)[:, :, DS:])
            ins.then_inc(st_ready, 1)
            ones_for(1)
            add_to_x("w_out")
            experts(0)

            inv_rms(2, D)
            scaled(XN, X, G_KV, DC, xn_ready)
            dve.wait_ge(mla_in, 16 * MLA_LOADS)
            dve.wait_ge(proj_done, PLAIN["kv"] + 4)
            dve.tensor_tensor(KR[:], ps[2][0:ROPE, 0:TOK], COS[0:ROPE], ALU.mult)
            link(dve.tensor_tensor(KT[:], ps[3][0:ROPE, 0:TOK], SIN[0:ROPE], ALU.mult))
            dve.tensor_tensor(KR[:], KR[:], KT[:], ALU.add).then_inc(kr_ready, 1)
            scaled(XN, X, G_MIX1, DC, xn_ready)
            dve.wait_ge(act_step, 2)
            dve.wait_ge(xn_ready, XN_MIX1 + DC)
            dve.wait_ge(kr_ready, 1)
            dve.memset(stat[:, 0, 5:6], 0.0).then_inc(kv_free, 1)
            ones_for(3)
            inv_rms(3, LAT)
            scaled(CT, CR, G_CKV, LC).then_inc(ct_ready, 1)
            ones_for(4)
            inv_rms(4, QLORA)
            scaled(CQN, CQ, G_Q, QC, xn_ready)
            for t in range(4, 8):
                s = t % 4
                dve.wait_ge(proj_done, PLAIN["w_uq"] + t + 1)
                dst, tab = (QRC, COS) if t < 6 else (QRS, SIN)
                g = 2 * (t % 2)
                dve.tensor_tensor(dst[:, g, :], ps[s][:, 0:TOK], tab[:], ALU.mult)
                dve.tensor_tensor(dst[:, g + 1, :], ps[4 + s][:, 0:TOK], tab[:], ALU.mult).then_inc(proj_evac, 1)
            dve.wait_ge(proj_evac, EVAC["w_uq"] + 8)
            dve.tensor_tensor(QRC[:], QRC[:], QRS[:], ALU.add).then_inc(qr_ready, 1)

            dve.wait_ge(ol_ready, 1)
            def p_max(m):
                qb = m // HEADS
                kk = P * (qb + 1)
                st, pp, sc = stat[:, m % 3, :], PP[m % 3], ps[SC_BANK[m % 3]]
                dve.wait_ge(sc_done, m + 1)
                if m >= 3:
                    dve.wait_ge(pt_done, m - 2)
                if qb:
                    dve.tensor_copy(pp[:, 0:P], sc[:, 0:P])
                link(dve.tensor_tensor(pp[:, kk - P:kk], sc[:, kk - P:kk], causal[:], ALU.add))
                link(dve.tensor_reduce(st[:, 0:1], pp[:, 0:kk], AX_X, ALU.max))
                dve.tensor_scalar(st[:, 1:2], st[:, 0:1], -SCALE, None, ALU.mult).then_inc(nm_ready, 1)

            def p_norm(m):
                kk = P * (m // HEADS + 1)
                st, pp = stat[:, m % 3, :], PP[m % 3]
                dve.wait_ge(p_exp, m + 1)
                link(dve.reciprocal(st[:, 3:4], st[:, 2:3]))
                dve.tensor_scalar(pp[:, 0:kk], pp[:, 0:kk], st[:, 3:4], None, ALU.mult).then_inc(p_ready, 1)

            for m in range(32 + 1):
                if m < 32:
                    p_max(m)
                if m >= 1:
                    p_norm(m - 1)
            for b in range(DB):
                bk = 3 * (b % 2)
                st = stat[0:64, b % 2, :]
                p = PS[b % 2]
                dve.wait_ge(sc_done, 32 + b + 1)
                if b >= 2:
                    dve.wait_ge(pt_done, 32 + b - 1)
                else:
                    dve.wait_ge(p_ready, 32)
                link(dve.tensor_tensor(p[:, PAST:], ps[bk + 2][0:64, 0:NSAMP], smask[:, b, :], ALU.add))
                dve.tensor_reduce(st[:, 5:6], ps[bk][0:64, :], AX_X, ALU.max)
                dve.tensor_reduce(st[:, 6:7], ps[bk + 1][0:64, :], AX_X, ALU.max)
                link(dve.tensor_reduce(st[:, 7:8], p[:, PAST:], AX_X, ALU.max))
                link(dve.tensor_reduce(st[:, 0:1], st[:, 5:8], AX_X, ALU.max))
                dve.tensor_scalar(st[:, 1:2], st[:, 0:1], -SCALE, None, ALU.mult).then_inc(nm_ready, 1)
                dve.wait_ge(p_exp, 32 + b + 1)
                link(dve.tensor_reduce(st[:, 5:6], st[:, 2:5], AX_X, ALU.add))
                link(dve.reciprocal(st[:, 6:7], st[:, 5:6]))
                dve.tensor_scalar(p[:], p[:], st[:, 6:7], None, ALU.mult).then_inc(p_ready, 1)
            dve.wait_ge(pt_done, 32 + DB + 1)
            ones_for(5)
            add_to_x("w_o")
            experts(1)
            inv_rms(6, D)
            scaled(X, X, G_FIN, DC).then_inc(y_fin, 1)

        @block.gpsimd
        def _(pool):
            link = Steps(pool, pool_step)
            pool.wait_ge(lru_in, 16 * 4)
            pool.memset(XB[:, :, 0:HIST], 0.0)
            for c in range(DC):
                pool.tensor_copy(XB[:, c, HIST + SEQ:XBW].rearrange("p (b t) -> p b t", b=DB)[:, :, 0:HIST],
                                 hist[:, c])
                pool.memset(LA[:, c, SEQ:SCW].rearrange("p (b t) -> p b t", b=DB)[:, :, 0:1], 0.0)
                ins = pool.tensor_copy(LB[:, c, SEQ:SCW].rearrange("p (b t) -> p b t", b=DB)[:, :, 0:1],
                                       h0[:, c, :].unsqueeze(2))
            ins.then_inc(hist_ready, 1)
            for l in range(2):
                if l == 1:
                    pool.wait_ge(proj_evac, EVAC["q_lat"] + 32)
                    pool.wait_ge(qr_in, 16 * 4)
                    for c in range(LC):
                        pool.tensor_copy(QLS[:, c].rearrange("p b (h t) -> p h b t", t=DS),
                                         QL[:, c, :, SEQ:TOK].rearrange("p h (b t) -> p h b t", t=DS))
                    pool.tensor_copy(QRP[:].rearrange("p b (h t) -> p h b t", t=DS),
                                     QR[:, :, SEQ:TOK].rearrange("p h (b t) -> p h b t", t=DS)).then_inc(qs_ready, 1)
                with pool.Fori(0, QROWS // SLOTS) as i:
                    for k in range(2 * SLOTS):
                        half = slice((k % 2) * HALF, (k % 2 + 1) * HALF)
                        pool.wait_ge(hi_ready, i * (2 * SLOTS) + SPLIT[f"wq{l}"] + k + 1)
                        pool.tensor_tensor(lo[k % 4][:], raw[k // 2][:, half], hi[k % 4][:].bitcast(F32), ALU.subtract)\
                            .then_inc(lo_ready, 1)
                pool.wait_ge(gt_ready, l + 1)
                pool.wait_ge(mm_done, SPLIT[f"u{l}"] + 2 * P)

                def difference(i, u):
                    if not (isinstance(i, int) and 4 * (i + NG * l) + u - 3 <= 0):
                        pool.wait_ge(g_done, i * 4 + 4 * NG * l + u - 3)
                    pool.tensor_tensor(ohi[u][:], iota[:].unsqueeze(1).broadcast_to([P, 4, P]),
                                       IT[:, bass.ds(i * 16 + 4 * u, 4)].unsqueeze(2).broadcast_to([P, 4, P]),
                                       ALU.subtract).then_inc(dif_ready, 1)

                hb = HB[:].rearrange("p j n -> p n j")

                def apply(i):
                    pool.wait_ge(g_copied, i + NG * l + 1)
                    w = hb[:, bass.ds(i * 16 + 12, 4), :]
                    pool.tensor_tensor(w, w, GS[:], ALU.mult).then_inc(g_pool, 1)

                pool.wait_ge(h_evac, QROWS * (l + 1))
                for u in range(4):
                    difference(0, u)
                with pool.Fori(1, NG) as i:
                    for u in range(4):
                        difference(i, u)
                    apply(i - 1)
                apply(NG - 1)


SC_BANK = (0, 1, 6)
MLA_LOADS = 8
AT_TURN = 23
N_CHUNKS = [8, 8, 8, LC, QC, 8, 8]
N_BEFORE = [sum(N_CHUNKS[:k]) for k in range(7)]
XN_MIX0, XN_FFN0, XN_KV, XN_MIX1, XN_Q, XN_FFN1 = 0, 8, 16, 24, 32, 36


def shape_constants():
    f = np.float32
    half = ROPE // 2
    inv = np.power(f(10000.0), -np.arange(half, dtype=f) / f(half)).astype(f)
    pos = np.concatenate([np.arange(SEQ), np.tile(PAST + np.arange(DS), DB)]).astype(f)
    ang = inv[:, None] * pos[None, :]
    cos = np.tile(np.cos(ang), (P // half, 1)).astype(f)
    sin = np.tile(np.concatenate([-np.sin(ang), np.sin(ang)]), (P // ROPE, 1)).astype(f)
    q, k = np.arange(P)[:, None], np.arange(P)[None, :]
    causal = np.where(k <= q, 0.0, NEG).astype(f)
    t = np.tile(np.arange(DS), HEADS)[:, None, None]
    b = np.arange(DB)[None, :, None]
    kb, kt = (np.arange(NSAMP) // DS)[None, None, :], (np.arange(NSAMP) % DS)[None, None, :]
    smask = np.where((kb == b) & (kt <= t), 0.0, NEG).astype(f)
    return {"cos": cos, "sin": sin, "causal": causal, "smask": smask, "ident": np.eye(P, dtype=f),
            "blk": (q // TOPK == k // TOPK).astype(f), "iota": np.tile(np.arange(P, dtype=f), (P, 1))}


def kernel(**inputs):
    import concourse.bacc as _bacc
    from concourse.bass_utils import run_bass_kernel_spmd as _run

    x = {k: np.asarray(v) for k, v in inputs.items()}
    f = np.float32

    def cols(v):
        return v.reshape(-1, P).T

    def tiles(w):
        k, m = w.shape
        return w.reshape(k // P, P, m // P, P).transpose(2, 1, 0, 3).reshape(m // P, P, k)

    def features(a3):
        return a3.reshape(a3.shape[0], -1, P).transpose(2, 1, 0)

    stream = np.zeros((NTILES, P, TILE), f)

    def put(phase, t):
        stream[FIRST[phase]:FIRST[phase] + len(t), :, :t.shape[2]] = t

    t = tiles(x["lru_w_in"][0])
    put("w_gate", t[:DC])
    put("w_x", t[DC:])
    put("w_out", tiles(x["lru_w_out"][0]))
    for l in range(2):
        put(f"wq{l}", tiles(x["peer_w_q"][l]))
        u = x["peer_u"][l].reshape(P, P, DC, P)
        for j in range(P):
            stream[FIRST[f"u{l}"] + j] = u[:, j].transpose(2, 1, 0).reshape(P, TILE)
        put(f"v{l}", x["peer_v"][l].reshape(P, P, D).transpose(1, 0, 2))
    swap = np.concatenate([np.arange(ROPE // 2, ROPE), np.arange(ROPE // 2)])
    put("kv", tiles(x["w_dkv"]))
    for s, w in ((2, x["w_kr"]), (3, x["w_kr"][:, swap])):
        stream[FIRST["kv"] + s, :, :DC * ROPE] = w.reshape(DC, P, ROPE).transpose(1, 0, 2).reshape(P, -1)
    put("w_dq", tiles(x["mla_w_dq"][0]))
    uq = x["mla_w_uq"][0].reshape(QLORA, HEADS, NOPE + ROPE)
    parts = [tiles(np.ascontiguousarray(w).reshape(QLORA, -1)) for w in
             (uq[:, :, :NOPE], uq[:, :, NOPE:], uq[:, :, NOPE:][:, :, swap])]
    t = np.concatenate(parts)
    put("w_uq", t.reshape(8, 2, P, QLORA).transpose(0, 2, 1, 3).reshape(8, P, 2 * QLORA))
    put("w_o", tiles(x["mla_w_o"][0]))

    xs = x["x_sample"].reshape(NSAMP, D)
    arrays = {
        "stream": stream,
        "x": features(np.concatenate([x["x_prompt"][0], xs])),
        "gains": np.concatenate([cols(x["ln_mix"][0]), cols(x["ln_ffn"][0]), cols(x["ln_mix"][1]),
                                 cols(x["ln_ffn"][1]), cols(x["ln_final"]), cols(x["kv_norm"]),
                                 cols(x["ckv_norm"]), cols(x["mla_q_norm"][0])], axis=1),
        "lru": np.concatenate([cols(x["lru_conv_w"][0].reshape(-1)), cols(x["lru_conv_b"][0]),
                               cols(x["lru_gate_a_b"][0]), cols(x["lru_gate_x_b"][0]), cols(x["lru_lambda"][0])], axis=1),
        "hist": x["state_conv"][:, 0].reshape(DB, HIST, DC, P).transpose(3, 2, 0, 1),
        "h0": x["state_h"][:, 0].reshape(DB, DC, P).transpose(2, 1, 0),
        "wg": np.concatenate([x["lru_gate_a_w"][0], x["lru_gate_x_w"][0]]).transpose(1, 0, 2),
        "sk": x["peer_subkeys"].reshape(2, 2 * PH, KEYS, P).transpose(0, 3, 1, 2),
        "wuk": x["w_uk"].reshape(LAT, HEADS // 2, 2 * NOPE).transpose(2, 1, 0),
        "wuv": x["w_uv"].reshape(LC, P, HEADS * VH).transpose(1, 0, 2),
        "pool": np.concatenate([
            x["cache_ckv"], x["cache_ckv"].reshape(NPOOL, PAGE, LC, P).transpose(0, 3, 2, 1).reshape(NPOOL, P, LC * PAGE),
            np.pad(x["cache_krope"].transpose(0, 2, 1), ((0, 0), (0, P - ROPE), (0, 0)))], axis=2),
        "pages": x["page_table"].reshape(1, -1).astype(np.int32),
        **shape_constants(),
    }
    arrays = {k: np.ascontiguousarray(v) for k, v in arrays.items()}
    outs = {"y": (P, DC, TOK), "h": (P, DC, 1 + DB), "conv": (P, DC, (1 + DB) * HIST),
            "ckv": (P, LC, TOK), "kr": (ROPE, TOK)}

    nc = _bacc.Bacc("TRN2", target_bir_lowering=False, num_devices=1)
    a = {k: nc.dram_tensor(f"in_{k}", v.shape, mybir.dt.from_np(v.dtype), kind="ExternalInput").ap()
         for k, v in arrays.items()}
    o = {k: nc.dram_tensor(f"out_{k}", s, F32, kind="ExternalOutput").ap() for k, s in outs.items()}
    build(nc, a, o)
    r = _run(nc, [{f"in_{k}": v for k, v in arrays.items()}], core_ids=[0]).results[0]

    def tokens(t):
        return t.transpose(2, 1, 0).reshape(t.shape[2], -1)

    y, ckv, kr = tokens(r["out_y"]), tokens(r["out_ckv"]), r["out_kr"].T
    h = r["out_h"].transpose(2, 1, 0).reshape(1 + DB, D)
    conv = r["out_conv"].reshape(P, DC, 1 + DB, HIST).transpose(2, 3, 1, 0).reshape(1 + DB, HIST, D)
    c = np.ascontiguousarray
    return (c(y[None, :SEQ]), c(y[SEQ:].reshape(DB, DS, D)), c(h[None, :1]), c(conv[None, :1]),
            c(ckv[None, :SEQ]), c(kr[None, :SEQ]), c(h[1:, None]), c(conv[1:, None]),
            c(ckv[SEQ:].reshape(DB, DS, LAT)), c(kr[SEQ:].reshape(DB, DS, ROPE)))
```
